# Optimizing a Trainium2 kernel written in Bass

```python
import math
import jax, jax.numpy as jnp
from jax import lax
import numpy as np
import jax
import jax.numpy as jnp

D_MODEL = 1024
BATCH = 1
SEQ = 512
DEPTH = 2

N_MIXERS = 3
EXPAND = 2
D_INNER = EXPAND * D_MODEL
GLA_HEADS = 4
GLA_DK = D_MODEL // GLA_HEADS
GLA_DV = D_INNER // GLA_HEADS
GLA_RANK = 16
GLA_GATE_NORM = 16.0
GLA_CHUNK = 64
DSA_HEADS = 16
DSA_HEAD_DIM = D_INNER // DSA_HEADS
IDX_HEADS = 8
IDX_DIM = 64
TOPK_MAX = 256
Q_BLOCK = 128
ATTN_SCALE = DSA_HEAD_DIM ** -0.5
INDEX_SCALE = (IDX_HEADS ** -0.5) * (IDX_DIM ** -0.5)
CONV_WIDTH = 31
ROPE_THETA = 500000.0
DSA_ROT_DIM = DSA_HEAD_DIM // 4
IDX_ROT_DIM = IDX_DIM // 4
PLE_DIM = 256
ALPHA = (2 * DEPTH) ** 0.25
BETA = (8 * DEPTH) ** -0.25
NORM_EPS = 1e-5

GLA_IN = 2 * GLA_HEADS * GLA_DK + 2 * D_INNER + GLA_RANK
DSA_IN = 2 * D_INNER + 2 * DSA_HEAD_DIM + IDX_HEADS * IDX_DIM + IDX_DIM + IDX_HEADS
CONV_IN = 3 * D_INNER


def layer_norm(x, g, b):
    xf = x.astype(jnp.float32)
    mu = jnp.mean(xf, axis=-1, keepdims=True)
    var = jnp.mean(jnp.square(xf - mu), axis=-1, keepdims=True)
    return ((xf - mu) * lax.rsqrt(var + NORM_EPS) * g + b).astype(x.dtype)

def rope_tables(positions, rot_dim):
    inv_freq = ROPE_THETA ** (-jnp.arange(0, rot_dim, 2, dtype=jnp.float32) / rot_dim)
    ang = positions.astype(jnp.float32)[..., None] * inv_freq
    return jnp.cos(ang), jnp.sin(ang)

def apply_partial_rope(x, cos, sin):
    half = cos.shape[-1]
    rot = 2 * half
    bshape = cos.shape[:2] + (1,) * (x.ndim - 3) + (half,)
    c = cos.reshape(bshape)
    s = sin.reshape(bshape)
    x1 = x[..., :half].astype(jnp.float32)
    x2 = x[..., half:rot].astype(jnp.float32)
    rotated = jnp.concatenate([x1 * c - x2 * s, x2 * c + x1 * s], axis=-1).astype(x.dtype)
    return jnp.concatenate([rotated, x[..., rot:]], axis=-1)

def gla_mixer(x, w_in, w_a2, b_a, gn_g, w_out):
    B, L, _ = x.shape
    n = L // GLA_CHUNK
    qk = GLA_HEADS * GLA_DK
    h = x @ w_in
    q = h[..., :qk]
    k = h[..., qk:2 * qk]
    v = h[..., 2 * qk:2 * qk + D_INNER]
    z = h[..., 2 * qk + D_INNER:2 * qk + 2 * D_INNER]
    a = h[..., 2 * qk + 2 * D_INNER:]
    g = jax.nn.log_sigmoid((a @ w_a2 + b_a).astype(jnp.float32)) / GLA_GATE_NORM

    def chunk(t, d):
        return t.astype(jnp.float32).reshape(B, n, GLA_CHUNK, GLA_HEADS, d)

    q, k, g, v = chunk(q, GLA_DK), chunk(k, GLA_DK), chunk(g, GLA_DK), chunk(v, GLA_DV)
    G = jnp.cumsum(g, axis=2)
    G_last = G[:, :, -1:]
    q_t = q * (GLA_DK ** -0.5) * jnp.exp(G)
    k_t = k * jnp.exp(-G)
    k_s = k * jnp.exp(G_last - G)
    pos = jnp.arange(GLA_CHUNK)
    tril = pos[:, None] >= pos[None, :]
    A = jnp.where(tril, jnp.einsum('bnihd,bnjhd->bnhij', q_t, k_t), 0.0)
    o_intra = jnp.einsum('bnhij,bnjhv->bnihv', A, v)

    def step(S, inp):
        q_c, k_c, v_c, decay = inp
        o_c = jnp.einsum('bihd,bhdv->bihv', q_c, S)
        S = S * decay[..., None] + jnp.einsum('bjhd,bjhv->bhdv', k_c, v_c)
        return S, o_c

    S0 = jnp.zeros((B, GLA_HEADS, GLA_DK, GLA_DV), jnp.float32)
    xs = (jnp.moveaxis(q_t, 1, 0), jnp.moveaxis(k_s, 1, 0), jnp.moveaxis(v, 1, 0),
          jnp.moveaxis(jnp.exp(G_last[:, :, 0]), 1, 0))
    _, o_inter = lax.scan(step, S0, xs)
    o = o_intra + jnp.moveaxis(o_inter, 0, 1)
    o = o * lax.rsqrt(jnp.mean(o * o, axis=-1, keepdims=True) + NORM_EPS)
    o = o.reshape(B, L, D_INNER) * gn_g
    return (o.astype(x.dtype) * jax.nn.silu(z)) @ w_out

def dsa_mixer(x, cos_h, sin_h, cos_i, sin_i, w_in, w_out):
    B, L, _ = x.shape
    topk = min(TOPK_MAX, L // 4)
    nb = L // Q_BLOCK
    h = x @ w_in
    o1 = D_INNER
    o2 = o1 + DSA_HEAD_DIM
    o3 = o2 + DSA_HEAD_DIM
    o4 = o3 + D_INNER
    o5 = o4 + IDX_HEADS * IDX_DIM
    o6 = o5 + IDX_DIM
    q = apply_partial_rope(h[..., :o1].reshape(B, L, DSA_HEADS, DSA_HEAD_DIM), cos_h, sin_h)
    k = apply_partial_rope(h[..., o1:o2], cos_h, sin_h)
    v = h[..., o2:o3]
    z = h[..., o3:o4]
    qi = apply_partial_rope(h[..., o4:o5].reshape(B, L, IDX_HEADS, IDX_DIM), cos_i, sin_i)
    ki = apply_partial_rope(h[..., o5:o6], cos_i, sin_i)
    wi = h[..., o6:]
    gather = jax.vmap(lambda arr, ids: arr[ids])
    s_pos = jnp.arange(L, dtype=jnp.int32)

    def to_blocks(t):
        return jnp.moveaxis(t.reshape((B, nb, Q_BLOCK) + t.shape[2:]), 1, 0)

    def attend_block(args):
        q_b, qi_b, wi_b, start = args
        t_pos = start + jnp.arange(Q_BLOCK, dtype=jnp.int32)
        rel = jax.nn.relu(jnp.einsum('bthd,bsd->bths', qi_b, ki).astype(jnp.float32))
        score = jnp.einsum('bths,bth->bts', rel, wi_b.astype(jnp.float32)) * INDEX_SCALE
        causal = s_pos[None, :] <= t_pos[:, None]
        score = jnp.where(causal[None], score, -jnp.inf)
        _, idx = lax.top_k(score, topk)
        valid = idx <= t_pos[None, :, None]
        k_sel = gather(k, idx)
        v_sel = gather(v, idx)
        logits = jnp.einsum('bthd,btjd->bthj', q_b, k_sel).astype(jnp.float32) * ATTN_SCALE
        logits = jnp.where(valid[:, :, None, :], logits, -jnp.inf)
        probs = jax.nn.softmax(logits, axis=-1).astype(v.dtype)
        return jnp.einsum('bthj,btjd->bthd', probs, v_sel)

    starts = jnp.arange(nb, dtype=jnp.int32) * Q_BLOCK
    o = lax.map(attend_block, (to_blocks(q), to_blocks(qi), to_blocks(wi), starts))
    o = jnp.moveaxis(o, 0, 1).reshape(B, L, D_INNER)
    return (o * jax.nn.silu(z)) @ w_out

def conformer_conv_mixer(x, w_in, dw_w, dw_b, ln_g, ln_b, w_out):
    h = x @ w_in
    a, gate, z = jnp.split(h, 3, axis=-1)
    u = a * jax.nn.sigmoid(gate)
    u = lax.conv_general_dilated(u, dw_w[:, None, :], window_strides=(1,),
                                 padding=[(CONV_WIDTH - 1, 0)],
                                 dimension_numbers=('NWC', 'WIO', 'NWC'),
                                 feature_group_count=D_INNER) + dw_b
    u = jax.nn.silu(layer_norm(u, ln_g, ln_b))
    return (u * jax.nn.silu(z)) @ w_out

def first_inputs(seed: int = 0) -> dict:
    key = jax.random.key(seed)
    ks = jax.random.split(key, 24)
    n_gla = len(range(0, DEPTH, N_MIXERS))
    n_dsa = len(range(1, DEPTH, N_MIXERS))
    n_conv = len(range(2, DEPTH, N_MIXERS))

    def normal(k, shape, scale):
        return jax.random.normal(k, shape, jnp.float32) * scale

    x = normal(ks[0], (BATCH, SEQ, D_MODEL), 1.0)
    p = normal(ks[1], (DEPTH, BATCH, SEQ, PLE_DIM), 1.0)
    offsets = jax.random.randint(ks[2], (BATCH, 1), 0, 1024, dtype=jnp.int32)
    positions = offsets + jnp.arange(SEQ, dtype=jnp.int32)[None, :]
    return {
        'x': x,
        'p': p,
        'positions': positions,
        'gla_w_in': normal(ks[3], (n_gla, D_MODEL, GLA_IN), D_MODEL ** -0.5),
        'gla_w_a2': normal(ks[4], (n_gla, GLA_RANK, GLA_HEADS * GLA_DK), GLA_RANK ** -0.5),
        'gla_b_a': normal(ks[5], (n_gla, GLA_HEADS * GLA_DK), 0.1),
        'gla_gn_g': 1.0 + normal(ks[6], (n_gla, D_INNER), 0.02),
        'gla_w_out': normal(ks[7], (n_gla, D_INNER, D_MODEL), BETA * D_INNER ** -0.5),
        'dsa_w_in': normal(ks[8], (n_dsa, D_MODEL, DSA_IN), D_MODEL ** -0.5),
        'dsa_w_out': normal(ks[9], (n_dsa, D_INNER, D_MODEL), BETA * D_INNER ** -0.5),
        'conv_w_in': normal(ks[10], (n_conv, D_MODEL, CONV_IN), D_MODEL ** -0.5),
        'conv_dw_w': normal(ks[11], (n_conv, CONV_WIDTH, D_INNER), CONV_WIDTH ** -0.5),
        'conv_dw_b': normal(ks[12], (n_conv, D_INNER), 0.02),
        'conv_ln_g': 1.0 + normal(ks[13], (n_conv, D_INNER), 0.02),
        'conv_ln_b': normal(ks[14], (n_conv, D_INNER), 0.02),
        'conv_w_out': normal(ks[15], (n_conv, D_INNER, D_MODEL), BETA * D_INNER ** -0.5),
        'ln_g': 1.0 + normal(ks[16], (DEPTH, D_MODEL), 0.02),
        'ln_b': normal(ks[17], (DEPTH, D_MODEL), 0.02),
        'ple_w': normal(ks[18], (DEPTH, PLE_DIM, D_MODEL), 0.5 * PLE_DIM ** -0.5),
        'ple_gate_w': normal(ks[19], (DEPTH, D_MODEL, D_MODEL), D_MODEL ** -0.5),
    }

def first_block(x, p, positions, gla_w_in, gla_w_a2, gla_b_a, gla_gn_g, gla_w_out,
              dsa_w_in, dsa_w_out, conv_w_in, conv_dw_w, conv_dw_b, conv_ln_g, conv_ln_b,
              conv_w_out, ln_g, ln_b, ple_w, ple_gate_w):
    cos_h, sin_h = rope_tables(positions, DSA_ROT_DIM)
    cos_i, sin_i = rope_tables(positions, IDX_ROT_DIM)
    for i in range(DEPTH):
        kind = i % N_MIXERS
        j = i // N_MIXERS
        if kind == 0:
            y = gla_mixer(x, gla_w_in[j], gla_w_a2[j], gla_b_a[j], gla_gn_g[j], gla_w_out[j])
        elif kind == 1:
            y = dsa_mixer(x, cos_h, sin_h, cos_i, sin_i, dsa_w_in[j], dsa_w_out[j])
        else:
            y = conformer_conv_mixer(x, conv_w_in[j], conv_dw_w[j], conv_dw_b[j],
                                     conv_ln_g[j], conv_ln_b[j], conv_w_out[j])
        x = layer_norm(ALPHA * x + y, ln_g[i], ln_b[i])
        x = x + (p[i] @ ple_w[i]) * jax.nn.sigmoid(x @ ple_gate_w[i])
    return x


DEPTH_2 = 1

N_GROUPS = 5
HEAD_DIM = 64
GROUP_HEADS = 4
GROUP_W = GROUP_HEADS * HEAD_DIM
MIX_W = N_GROUPS * GROUP_W
N_MEM = 256
CHUNK = 128
CONV_K = 4
RWKV_DECAY_RANK = 16
RWKV_A_RANK = 16
EPS = 1e-6

A_COLS = (GROUP_W, GROUP_W, GROUP_W)
B_COLS = (GROUP_W, GROUP_W, GROUP_W, GROUP_HEADS, GROUP_W)
C_COLS = (2 * GROUP_W, GROUP_W, GROUP_HEADS, GROUP_HEADS, GROUP_W, GROUP_W)
D_COLS = (GROUP_W, RWKV_DECAY_RANK, GROUP_W, GROUP_W, RWKV_A_RANK, GROUP_W)
M_COLS = (GROUP_W, GROUP_W)
GROUP_COLS = (sum(A_COLS), sum(B_COLS), sum(C_COLS), sum(D_COLS), sum(M_COLS))
D_W = sum(D_COLS)
IN_COLS = sum(GROUP_COLS)


def rms_norm(x, g):
    xf = x.astype(jnp.float32)
    y = xf * lax.rsqrt(jnp.mean(xf * xf, axis=-1, keepdims=True) + EPS)
    return (y * g.astype(jnp.float32)).astype(x.dtype)

def split_cols(x, widths):
    return jnp.split(x, np.cumsum(widths)[:-1].tolist(), axis=-1)

def to_heads(t):
    return t.reshape(t.shape[:-1] + (GROUP_HEADS, HEAD_DIM))

def causal_dwconv(x, w, b):
    y = lax.conv_general_dilated(
        x, w[:, None, :].astype(x.dtype), (1,), [(CONV_K - 1, 0)],
        dimension_numbers=("NWC", "WIO", "NWC"), feature_group_count=x.shape[-1])
    return y + b

def token_shift(x, mu):
    prev = jnp.pad(x, ((0, 0), (1, 0), (0, 0)))[:, :-1]
    return x + mu * (prev - x)

def spatial_gating(u, v, norm_g, w_s, b_s):
    bsz, seq, _ = u.shape
    nc = seq // CHUNK
    u = jax.nn.gelu(u)
    v = rms_norm(to_heads(jax.nn.gelu(v)), norm_g.reshape(GROUP_HEADS, HEAD_DIM))
    v = v.reshape(bsz, nc, CHUNK, GROUP_HEADS, HEAD_DIM)
    w = jnp.where(jnp.tril(jnp.ones((CHUNK, CHUNK), bool)), w_s, jnp.zeros_like(w_s))
    mixed = jnp.einsum("gts,bcsgd->bctgd", w, v) + b_s.T[:, :, None]
    return u * mixed.reshape(bsz, seq, GROUP_W)

def forgetting_attention(q, k, v, f_logit, q_g, k_g):
    bsz, seq, _ = q.shape
    nb = seq // CHUNK
    q = rms_norm(to_heads(q), q_g)
    k = rms_norm(to_heads(k), k_g)
    v = to_heads(v)
    big_f = jnp.cumsum(jax.nn.log_sigmoid(f_logit.astype(jnp.float32)), axis=1)
    big_f = big_f.transpose(0, 2, 1)
    q_blocks = q.reshape(bsz, nb, CHUNK, GROUP_HEADS, HEAD_DIM).swapaxes(0, 1)
    f_blocks = big_f.reshape(bsz, GROUP_HEADS, nb, CHUNK).transpose(2, 0, 1, 3)
    k_pos = jnp.arange(seq)
    scale = HEAD_DIM ** -0.5

    def one_block(args):
        qb, fb, start = args
        s = jnp.einsum("bthd,bshd->bhts", qb, k).astype(jnp.float32) * scale
        s = s + fb[..., :, None] - big_f[..., None, :]
        q_pos = start + jnp.arange(CHUNK)
        s = jnp.where(k_pos[None, :] <= q_pos[:, None], s, -jnp.inf)
        p = jax.nn.softmax(s, axis=-1).astype(v.dtype)
        return jnp.einsum("bhts,bshd->bthd", p, v)

    out = lax.map(one_block, (q_blocks, f_blocks, jnp.arange(nb) * CHUNK))
    return out.swapaxes(0, 1).reshape(bsz, seq, GROUP_W)

def mlstm(qk, v, i_logit, f_logit, o_logit, conv_w, conv_b, out_g):
    f32 = jnp.float32
    bsz, seq, _ = v.shape
    nc = seq // CHUNK
    q, k = jnp.split(jax.nn.silu(causal_dwconv(qk, conv_w, conv_b)), 2, axis=-1)
    q = to_heads(q).astype(f32)
    k = to_heads(k).astype(f32) * HEAD_DIM ** -0.5
    vh = to_heads(v).astype(f32)
    log_i = i_logit.astype(f32)
    log_f = jax.nn.log_sigmoid(f_logit.astype(f32))

    def chunks(t):
        return t.reshape((bsz, nc, CHUNK) + t.shape[2:]).swapaxes(0, 1)

    causal = jnp.tril(jnp.ones((CHUNK, CHUNK), bool))

    def step(carry, inp):
        c_state, n_state, m_state = carry
        qc, kc, vc, ic, fc = inp
        b = jnp.cumsum(fc, axis=1).swapaxes(1, 2)
        ic = ic.swapaxes(1, 2)
        g = b[..., -1]
        log_d = jnp.where(causal, b[..., :, None] - b[..., None, :] + ic[..., None, :], -jnp.inf)
        inter = b + m_state[..., None]
        m_t = jnp.maximum(jnp.max(log_d, axis=-1), inter)
        s = jnp.einsum("bthd,bshd->bhts", qc, kc) * jnp.exp(log_d - m_t[..., None])
        w_inter = jnp.exp(inter - m_t)
        num = (jnp.einsum("bhts,bshd->bhtd", s, vc)
               + w_inter[..., None] * jnp.einsum("bthk,bhkd->bhtd", qc, c_state))
        den = jnp.sum(s, axis=-1) + w_inter * jnp.einsum("bthk,bhk->bht", qc, n_state)
        h = num / jnp.maximum(jnp.abs(den), jnp.exp(-m_t))[..., None]
        log_w = g[..., None] - b + ic
        m_new = jnp.maximum(g + m_state, jnp.max(log_w, axis=-1))
        w_new = jnp.exp(log_w - m_new[..., None])
        carry_decay = jnp.exp(g + m_state - m_new)
        c_state = carry_decay[..., None, None] * c_state + jnp.einsum("bhs,bshk,bshd->bhkd", w_new, kc, vc)
        n_state = carry_decay[..., None] * n_state + jnp.einsum("bhs,bshk->bhk", w_new, kc)
        return (c_state, n_state, m_new), h.swapaxes(1, 2)

    init = (jnp.zeros((bsz, GROUP_HEADS, HEAD_DIM, HEAD_DIM), f32),
            jnp.zeros((bsz, GROUP_HEADS, HEAD_DIM), f32),
            jnp.zeros((bsz, GROUP_HEADS), f32))
    _, h = lax.scan(step, init, (chunks(q), chunks(k), chunks(vh), chunks(log_i), chunks(log_f)))
    h = h.swapaxes(0, 1).reshape(bsz, seq, GROUP_HEADS, HEAD_DIM)
    h = jax.nn.sigmoid(to_heads(o_logit).astype(f32)) * h
    return rms_norm(h, out_g.reshape(GROUP_HEADS, HEAD_DIM)).reshape(bsz, seq, GROUP_W)

def rwkv7_time_mix(r, w_lo, k, v, a_lo, w0, w2, a0, a2, k_k, k_a, r_k, ln_g):
    f32 = jnp.float32
    bsz, seq, _ = r.shape
    r, w_lo, k, v, a_lo = (t.astype(f32) for t in (r, w_lo, k, v, a_lo))
    w_log = -jax.nn.softplus(-(w0 + jnp.tanh(w_lo) @ w2)) - 0.5
    decay = jnp.exp(-jnp.exp(w_log))
    a = jax.nn.sigmoid(a0 + a_lo @ a2)
    kk = to_heads(k * k_k)
    kk = kk / jnp.maximum(jnp.linalg.norm(kk, axis=-1, keepdims=True), 1e-12)
    k = k * (1 + (a - 1) * k_a)
    rh, dh, kh, vh, ah = (to_heads(t) for t in (r, decay, k, v, a))

    def step(state, inp):
        r_t, w_t, k_t, v_t, kk_t, a_t = inp
        sa = jnp.einsum("bhvk,bhk->bhv", state, -kk_t)
        state = (state * w_t[:, :, None, :] + sa[..., None] * (kk_t * a_t)[:, :, None, :]
                 + v_t[..., None] * k_t[:, :, None, :])
        return state, jnp.einsum("bhvk,bhk->bhv", state, r_t)

    init = jnp.zeros((bsz, GROUP_HEADS, HEAD_DIM, HEAD_DIM), f32)
    _, y = lax.scan(step, init, tuple(t.swapaxes(0, 1) for t in (rh, dh, kh, vh, kk, ah)))
    y = rms_norm(y.swapaxes(0, 1), ln_g.reshape(GROUP_HEADS, HEAD_DIM))
    y = y + jnp.sum(rh * kh * r_k, axis=-1, keepdims=True) * vh
    return y.reshape(bsz, seq, GROUP_W)

def memory_attention(q, mem_n, w_kv, q_g, k_g):
    bsz, seq, _ = q.shape
    k, v = jnp.split(mem_n @ w_kv, 2, axis=-1)
    q = rms_norm(to_heads(q), q_g)
    k = rms_norm(to_heads(k), k_g)
    v = to_heads(v)
    s = jnp.einsum("bthd,bmhd->bhtm", q, k).astype(jnp.float32) * HEAD_DIM ** -0.5
    p = jax.nn.softmax(s, axis=-1).astype(v.dtype)
    return jnp.einsum("bhtm,bmhd->bthd", p, v).reshape(bsz, seq, GROUP_W)

def hybrid_layer(x, mem, norm_g, w_in, w_out, sgu_norm_g, sgu_w, sgu_b,
                 fox_q_g, fox_k_g, fox_f_b,
                 mlstm_conv_w, mlstm_conv_b, mlstm_i_b, mlstm_f_b, mlstm_out_g,
                 rwkv_mu, rwkv_w0, rwkv_w2, rwkv_a0, rwkv_a2, rwkv_k_k, rwkv_k_a, rwkv_r_k, rwkv_ln_g,
                 mem_norm_g, mem_w_kv, mem_q_g, mem_k_g):
    h = rms_norm(x, norm_g)
    proj = h @ w_in
    pa, pb, pc, pd, pm = split_cols(proj, GROUP_COLS)

    a_u, a_v, a_z = split_cols(pa, A_COLS)
    ya = spatial_gating(a_u, a_v, sgu_norm_g, sgu_w, sgu_b)

    b_q, b_k, b_v, b_f, b_z = split_cols(pb, B_COLS)
    yb = forgetting_attention(b_q, b_k, b_v, b_f + fox_f_b, fox_q_g, fox_k_g)

    c_qk, c_v, c_i, c_f, c_o, c_z = split_cols(pc, C_COLS)
    yc = mlstm(c_qk, c_v, c_i + mlstm_i_b, c_f + mlstm_f_b, c_o, mlstm_conv_w, mlstm_conv_b, mlstm_out_g)

    d_r, d_wlo, d_k, d_v, d_alo, d_z = split_cols(token_shift(pd, rwkv_mu), D_COLS)
    yd = rwkv7_time_mix(d_r, d_wlo, d_k, d_v, d_alo, rwkv_w0, rwkv_w2, rwkv_a0, rwkv_a2,
                        rwkv_k_k, rwkv_k_a, rwkv_r_k, rwkv_ln_g)

    m_q, m_z = split_cols(pm, M_COLS)
    ym = memory_attention(m_q, rms_norm(mem, mem_norm_g), mem_w_kv, mem_q_g, mem_k_g)

    branches = [(ya, a_z), (yb, b_z), (yc, c_z), (yd, d_z), (ym, m_z)]
    mixed = jnp.concatenate([y.astype(x.dtype) * jax.nn.silu(z) for y, z in branches], axis=-1)
    return x + mixed @ w_out

def second_inputs(seed: int = 0) -> dict:
    key = jax.random.key(seed)
    ks = iter(jax.random.split(key, 32))
    f32 = jnp.float32

    def nrm(shape, scale):
        return jax.random.normal(next(ks), shape, f32) * scale

    def uni(shape, lo, hi):
        return jax.random.uniform(next(ks), shape, f32, lo, hi)

    def gain(shape):
        return 1.0 + nrm(shape, 0.1)

    L = DEPTH_2
    return {
        "x": nrm((BATCH, SEQ, D_MODEL), 1.0),
        "mem": nrm((BATCH, N_MEM, D_MODEL), 1.0),
        "norm_g": gain((L, D_MODEL)),
        "w_in": nrm((L, D_MODEL, IN_COLS), D_MODEL ** -0.5),
        "w_out": nrm((L, MIX_W, D_MODEL), MIX_W ** -0.5),
        "sgu_norm_g": gain((L, GROUP_W)),
        "sgu_w": nrm((L, GROUP_HEADS, CHUNK, CHUNK), 0.5 * CHUNK ** -0.5),
        "sgu_b": gain((L, GROUP_HEADS, CHUNK)),
        "fox_q_g": gain((L, HEAD_DIM)),
        "fox_k_g": gain((L, HEAD_DIM)),
        "fox_f_b": uni((L, GROUP_HEADS), 1.0, 5.0),
        "mlstm_conv_w": nrm((L, CONV_K, 2 * GROUP_W), CONV_K ** -0.5),
        "mlstm_conv_b": nrm((L, 2 * GROUP_W), 0.02),
        "mlstm_i_b": nrm((L, GROUP_HEADS), 0.1),
        "mlstm_f_b": uni((L, GROUP_HEADS), 3.0, 6.0),
        "mlstm_out_g": gain((L, GROUP_W)),
        "rwkv_mu": uni((L, D_W), 0.0, 1.0),
        "rwkv_w0": uni((L, GROUP_W), -4.0, 0.0),
        "rwkv_w2": nrm((L, RWKV_DECAY_RANK, GROUP_W), 0.5 * RWKV_DECAY_RANK ** -0.5),
        "rwkv_a0": nrm((L, GROUP_W), 0.1),
        "rwkv_a2": nrm((L, RWKV_A_RANK, GROUP_W), 0.5 * RWKV_A_RANK ** -0.5),
        "rwkv_k_k": 0.85 + nrm((L, GROUP_W), 0.05),
        "rwkv_k_a": gain((L, GROUP_W)),
        "rwkv_r_k": nrm((L, GROUP_HEADS, HEAD_DIM), 0.1),
        "rwkv_ln_g": gain((L, GROUP_W)),
        "mem_norm_g": gain((L, D_MODEL)),
        "mem_w_kv": nrm((L, D_MODEL, 2 * GROUP_W), D_MODEL ** -0.5),
        "mem_q_g": gain((L, HEAD_DIM)),
        "mem_k_g": gain((L, HEAD_DIM)),
    }

def second_block(x, mem, norm_g, w_in, w_out, sgu_norm_g, sgu_w, sgu_b,
              fox_q_g, fox_k_g, fox_f_b,
              mlstm_conv_w, mlstm_conv_b, mlstm_i_b, mlstm_f_b, mlstm_out_g,
              rwkv_mu, rwkv_w0, rwkv_w2, rwkv_a0, rwkv_a2, rwkv_k_k, rwkv_k_a, rwkv_r_k, rwkv_ln_g,
              mem_norm_g, mem_w_kv, mem_q_g, mem_k_g):
    stacked = (norm_g, w_in, w_out, sgu_norm_g, sgu_w, sgu_b,
               fox_q_g, fox_k_g, fox_f_b,
               mlstm_conv_w, mlstm_conv_b, mlstm_i_b, mlstm_f_b, mlstm_out_g,
               rwkv_mu, rwkv_w0, rwkv_w2, rwkv_a0, rwkv_a2, rwkv_k_k, rwkv_k_a, rwkv_r_k, rwkv_ln_g,
               mem_norm_g, mem_w_kv, mem_q_g, mem_k_g)
    for layer in range(DEPTH_2):
        x = hybrid_layer(x, mem, *[p[layer] for p in stacked])
    return x


def setup_inputs(seed=0):
    out = dict(first_inputs(seed))
    for name, value in second_inputs(seed + 1).items():
        if name != "x":
            out[name + "_2"] = value
    return out


def reference(
    x, p, positions, gla_w_in, gla_w_a2, gla_b_a, gla_gn_g, gla_w_out, dsa_w_in, dsa_w_out,
    conv_w_in, conv_dw_w, conv_dw_b, conv_ln_g, conv_ln_b, conv_w_out, ln_g, ln_b, ple_w,
    ple_gate_w, mem_2, norm_g_2, w_in_2, w_out_2, sgu_norm_g_2, sgu_w_2, sgu_b_2, fox_q_g_2,
    fox_k_g_2, fox_f_b_2, mlstm_conv_w_2, mlstm_conv_b_2, mlstm_i_b_2, mlstm_f_b_2,
    mlstm_out_g_2, rwkv_mu_2, rwkv_w0_2, rwkv_w2_2, rwkv_a0_2, rwkv_a2_2, rwkv_k_k_2,
    rwkv_k_a_2, rwkv_r_k_2, rwkv_ln_g_2, mem_norm_g_2, mem_w_kv_2, mem_q_g_2, mem_k_g_2,
):
    x = first_block(
        x, p, positions, gla_w_in, gla_w_a2, gla_b_a, gla_gn_g, gla_w_out, dsa_w_in, dsa_w_out,
        conv_w_in, conv_dw_w, conv_dw_b, conv_ln_g, conv_ln_b, conv_w_out, ln_g, ln_b, ple_w,
        ple_gate_w,
    )
    return second_block(
        x, mem_2, norm_g_2, w_in_2, w_out_2, sgu_norm_g_2, sgu_w_2, sgu_b_2, fox_q_g_2,
        fox_k_g_2, fox_f_b_2, mlstm_conv_w_2, mlstm_conv_b_2, mlstm_i_b_2, mlstm_f_b_2,
        mlstm_out_g_2, rwkv_mu_2, rwkv_w0_2, rwkv_w2_2, rwkv_a0_2, rwkv_a2_2, rwkv_k_k_2,
        rwkv_k_a_2, rwkv_r_k_2, rwkv_ln_g_2, mem_norm_g_2, mem_w_kv_2, mem_q_g_2, mem_k_g_2,
    )


_drawn_inputs = setup_inputs


def setup_inputs(seed=0):
    import zlib

    import numpy as np

    out = dict(_drawn_inputs(seed))
    spreads = {}
    factors = {'gla_b_a': 5.111,
     'gla_gn_g': 8.0,
     'sgu_norm_g_2': 24.543,
     'sgu_b_2': 11.357,
     'fox_q_g_2': 8.0,
     'fox_k_g_2': 8.0,
     'mlstm_conv_b_2': 24.234,
     'mlstm_i_b_2': 64.0,
     'mlstm_f_b_2': 39.76,
     'rwkv_w2_2': 7.352,
     'rwkv_a0_2': 6.832,
     'rwkv_k_k_2': 200.0,
     'rwkv_k_a_2': 3.127,
     'rwkv_ln_g_2': 9.198,
     'mem_norm_g_2': 8.0,
     'mem_q_g_2': 8.0,
     'mem_k_g_2': 8.0,
     'mlstm_out_g_2': 6.084}
    for name, (base, spread) in spreads.items():
        noise = np.random.default_rng([zlib.crc32(name.encode()), seed]).standard_normal(out[name].shape)
        drawn = base * np.exp(spread * noise) if base else spread * noise
        out[name] = jnp.asarray(drawn.astype(out[name].dtype))
    for name, factor in factors.items():
        out[name] = (out[name] * factor).astype(out[name].dtype)
    return out
```

```python
from contextlib import ExitStack

import numpy as np
import concourse.bass as bass
from concourse import mybir
from concourse.alu_op_type import AluOpType as ALU

F32 = mybir.dt.float32
F32R = mybir.dt.float32r
I32 = mybir.dt.int32
U32 = mybir.dt.uint32
ACT = mybir.ActivationFunctionType
AX = mybir.AxisListType.X

P = 128
T = 512
NT = T // P
D = 1024
KD = D // P
DI = 2048
KI = DI // P
COLS = 512
SEMAPHORES = 140
CHUNK = 256
RING = 2
DEPTH = 2
ALPHA = (2 * DEPTH) ** 0.25
LN_EPS = 1e-5
RMS_EPS = 1e-6

GLA_HEADS, GLA_DK, GLA_DV, GLA_RANK, GLA_CHUNK, GATE_NORM = 4, 256, 512, 16, 64, 16.0
NCH = T // GLA_CHUNK


class Semaphores(dict):

    def __init__(self, nc, ctx):
        self.nc, self.ctx = nc, ctx
        self.count = {}
        self.past = {}
        self.idle = {}

    def __missing__(self, name):
        if name in self.idle:
            made = self.idle.pop(name)
        elif len(self) + len(self.idle) < SEMAPHORES:
            made = self.ctx.enter_context(self.nc.semaphore(name)), 0
        else:
            made = self.idle.pop(next(iter(self.idle)))
        self[name], self.past[name] = made
        self.count[name] = self.past[name]
        return self[name]

    def add(self, name, n):
        self.count[name] += n
        return n

    def end_phase(self):
        for name in self:
            self.idle[name] = self[name], self.count[name]
        self.clear()


class Program:
    def __init__(self, nc, t, out):
        self.nc, self.t, self.out = nc, t, out
        self.ctx = ExitStack()
        self.sem = Semaphores(nc, self.ctx)

    def sb(self, stack, name, shape, dtype=F32, side="left"):
        return stack.enter_context(self.nc.sbuf_tensor(name, shape, dtype, side=side))

    def alias(self, name, shape, dtype, offset):
        return self.nc.alloc_sbuf_tensor_at(name, shape, dtype, offset=offset)

    def address(self):
        return -(-self.nc.sbuf_base // 32) * 32


    def make_ring(self, sb):
        self.ring_at = self.address()
        self.w_high = sb("w_high", [P, RING, KD, CHUNK], F32R)
        self.w_low = sb("w_low", [P, RING, KD, CHUNK], F32R)
        self.w_ring = sb("w_ring", [P, RING, KD, CHUNK], F32)
        self.w_landed = [self.ctx.enter_context(self.nc.semaphore(f"w_landed{i}")) for i in range(RING)]
        self.w_high_made, self.w_low_made = (self.ctx.enter_context(self.nc.semaphore(n)) for n in ("w_high_made", "w_low_made"))
        self.landed_count = [0] * RING
        self.chunks = []
        self.splits = []
        self.chunk_used = []
        self.loaded = self.highs = self.lows = 0
        self.load_limit = 0

    def add_chunk(self, w, ranges, row=0, split=True):
        rows = min(D, w.shape[0] - row)
        sources, at = [], 0
        for a, b in ranges:
            sources.append((w[row:row + rows, a:b].rearrange("(k p) n -> p k n", p=P), at, b - a))
            at += b - a
        n = len(self.chunks)
        self.landed_count[n % RING] += 16 * len(sources)
        self.chunks.append((sources, rows // P, at, len(self.splits) if split else None, self.landed_count[n % RING]))
        if split:
            self.splits.append(n)
        return n

    def add_chunks(self, w, a, b, split=True):
        first = len(self.chunks)
        for c in range(a, b, CHUNK):
            for row in range(0, w.shape[0], D):
                self.add_chunk(w, [(c, min(c + CHUNK, b))], row, split)
        return first

    def release(self, name):
        self.chunk_used.append((self.sem[name], self.sem.count[name]))

    def load_chunks(self, sp):
        upto = min(len(self.chunk_used) + 2 * RING, len(self.chunks), self.load_limit)
        for n in range(self.loaded, upto):
            sources, k, _, _, _ = self.chunks[n]
            if n >= RING:
                split = self.chunks[n - RING][3]
                if split is not None:
                    if split >= self.highs:
                        break
                    sp.wait_ge(self.w_low_made, split + 1)
                else:
                    if n - RING >= len(self.chunk_used):
                        break
                    used, products = self.chunk_used[n - RING]
                    sp.wait_ge(used, products)
            for src, at, cols in sources:
                sp.dma_start(self.w_ring[:, n % RING, 0:k, at:at + cols], src).then_inc(self.w_landed[n % RING], 16)
            self.loaded = n + 1

    def split_high(self, act, upto):
        while self.highs < len(self.splits) and self.splits[self.highs] < upto:
            i, n = self.highs, self.splits[self.highs]
            _, k, cols, _, landed = self.chunks[n]
            act.wait_ge(self.w_landed[n % RING], landed)
            if i >= RING:
                used, products = self.chunk_used[self.splits[i - RING]]
                act.wait_ge(used, products)
            self.nc.scalar.activation(self.w_high[:, i % RING, 0:k, 0:cols], self.w_ring[:, n % RING, 0:k, 0:cols], ACT.Copy).then_inc(self.w_high_made, 1)
            self.highs += 1

    def split_low(self, pool, upto=None):
        while self.lows < self.highs and (upto is None or self.splits[self.lows] < upto):
            i, n = self.lows, self.splits[self.lows]
            _, k, cols, _, _ = self.chunks[n]
            pool.wait_ge(self.w_high_made, i + 1)
            self.nc.gpsimd.tensor_tensor(self.w_low[:, i % RING, 0:k, 0:cols], self.w_ring[:, n % RING, 0:k, 0:cols],
                                         self.w_high[:, i % RING, 0:k, 0:cols].bitcast(F32), ALU.subtract).then_inc(self.w_low_made, 1)
            self.lows += 1

    def chunk(self, pe, n):
        _, k, cols, split, landed = self.chunks[n]
        if split is None:
            pe.wait_ge(self.w_landed[n % RING], landed)
            return self.w_ring[:, n % RING, 0:k, 0:cols]
        pe.wait_ge(self.w_low_made, split + 1)
        return [w[:, split % RING, 0:k, 0:cols] for w in (self.w_high, self.w_low)]


    def product(self, out, lhs, rhs, first=True, last=True, check=True):
        return self.nc.tensor.matmul(out, lhs, rhs, start=first, stop=last, skip_group_check=not check)

    def split_product(self, out, lhs, rhs, first, last):
        (lhs_high, lhs_low), (rhs_high, rhs_low) = lhs, rhs
        self.product(out, lhs_high, rhs_high, first, False)
        self.product(out, lhs_high, rhs_low, False, False)
        return self.product(out, lhs_low, rhs_high, False, last)


def to_feature_major_pe(g, pe, before, src, nk, nt, banks):
    nc, turned = g.nc, "turned"
    sem, past, add = g.sem, g.sem.past, g.sem.add
    done = ["turned_by_act", "turned_by_dve"]
    nb = len(banks)
    for k in range(nk):
        if k >= nb:
            q = k - nb
            pe.wait_ge(sem[done[q % 2]], past[done[q % 2]] + before[q % 2] + q // 2 + 1)
        for j in range(nt):
            ins = nc.tensor.transpose(g.ps[:, banks[k % nb], j * P:(j + 1) * P], src[:, j, k * P:(k + 1) * P], g.ident[:])
        ins.then_inc(sem[turned], add(turned, 1))


def to_feature_major_act(g, act, seen, dst, nk, n, banks, scale=None):
    sem, past, add = g.sem, g.sem.past, g.sem.add
    for k in range(0, nk, 2):
        act.wait_ge(sem["turned"], past["turned"] + seen + k + 1)
        s = 1.0 if scale is None else scale[:, k:k + 1]
        g.nc.scalar.activation(dst[:, k, 0:n], g.ps[:, banks[k % len(banks)], 0:n], ACT.Copy, scale=s).then_inc(sem["turned_by_act"], add("turned_by_act", 1))


def to_feature_major_dve(g, dve, seen, dst, nk, n, banks, scale=None):
    sem, past, add = g.sem, g.sem.past, g.sem.add
    for k in range(1, nk, 2):
        dve.wait_ge(sem["turned"], past["turned"] + seen + k + 1)
        src = g.ps[:, banks[k % len(banks)], 0:n]
        if scale is None:
            ins = g.nc.vector.tensor_copy(dst[:, k, 0:n], src)
        else:
            ins = g.nc.vector.tensor_scalar(dst[:, k, 0:n], src, scale[:, k:k + 1], None, ALU.mult)
        ins.then_inc(sem["turned_by_dve"], add("turned_by_dve", 1))


def columns(parts, k, cols=slice(None)):
    return [part[:, k, cols] for part in parts]


def split_feature_major_pe(g, pe, before, src, nk, nt, banks):
    sem, past, add = g.sem, g.sem.past, g.sem.add
    nb = len(banks)
    for k in range(nk):
        if k >= nb:
            pe.wait_ge(sem["turned_low"], past["turned_low"] + before + k - nb + 1)
        for j in range(nt):
            ins = g.nc.tensor.transpose(g.ps[:, banks[k % nb], j * P:(j + 1) * P], src[:, j, k * P:(k + 1) * P], g.ident[:])
        ins.then_inc(sem["turned_whole"], add("turned_whole", 1))


def split_feature_major_act(g, act, before, dst, nk, banks, scale=None):
    sem, past, add = g.sem, g.sem.past, g.sem.add
    for k in range(nk):
        act.wait_ge(sem["turned_whole"], past["turned_whole"] + before + k + 1)
        s = 1.0 if scale is None else scale[:, k:k + 1]
        g.nc.scalar.activation(dst[0][:, k, :], g.ps[:, banks[k % len(banks)], :], ACT.Copy, scale=s).then_inc(sem["turned_high"], add("turned_high", 1))


def split_feature_major_dve(g, dve, before, dst, nk, banks, scale=None):
    sem, past, add = g.sem, g.sem.past, g.sem.add
    for k in range(nk):
        dve.wait_ge(sem["turned_high"], past["turned_high"] + before + k + 1)
        s = 1.0 if scale is None else scale[:, k:k + 1]
        g.nc.vector.scalar_tensor_tensor(out=dst[1][:, k, :], in0=g.ps[:, banks[k % len(banks)], :], scalar=s, in1=dst[0][:, k, :].bitcast(F32),
                                         op0=ALU.mult, op1=ALU.subtract).then_inc(sem["turned_low"], add("turned_low", 1))


def phase_load(g):
    nc, t, ps = g.nc, g.t, g.ps
    NFQ = HALF + IDX_HALF
    sem, past, count, add = g.sem, g.sem.past, g.sem.count, g.sem.add
    x_landed, const_made, vecs_landed = "x_landed", "const_made", "vecs_landed"
    vecs_cleared, cols_turned, cols_made = "vecs_cleared", "cols_turned", "cols_made"
    banks = [0, 1, 2, 3, 4, 5]
    x_tiles = t["x"][0].rearrange("(j p) d -> p j d", p=P)
    with ExitStack() as stack:
        x_tok = g.sb(stack, "x_tok", [P, NT, D])
        vec_rows = g.sb(stack, "vec_rows", [P, P])
        pos_i = g.sb(stack, "pos_i", [P, NT], I32)
        pos = g.sb(stack, "pos", [P, NT])
        freq = g.sb(stack, "freq", [P, NFQ])
        angle = g.sb(stack, "angle", [P, NT, NFQ])
        turns = g.sb(stack, "turns", [P, NT, NFQ])
        wrap = g.sb(stack, "wrap", [P, NT, NFQ])
        both = g.sb(stack, "both", [P, 2, NT, NFQ])
        tab = g.sb(stack, "tab", [P, NT, 2 * P + 4 * HALF])
        idx_c, idx_s = tab[:, :, 0:P], tab[:, :, P:2 * P]
        head_c, head_s = tab[:, :, 2 * P:2 * P + 2 * HALF], tab[:, :, 2 * P + 2 * HALF:]
        with nc.Block("load", no_gpsimd_drain=True) as block:

            @block.sync
            def _(sp):
                sp.dma_start(pos_i[:], t["positions"][0].rearrange("(j p) -> p j", p=P), allow_slow_non_contiguous=True).then_inc(sem["pos_landed"], add("pos_landed", 16))
                for j in range(NT):
                    sp.dma_start(x_tok[:, j, :], x_tiles[:, j, :]).then_inc(sem[x_landed], add(x_landed, 16))
                g.load_chunks(sp)

            @block.scalar
            def _(act):
                act.wait_ge(sem[vecs_cleared], past[vecs_cleared] + 1)
                for name, view, row, rows, width in g.vec_rows:
                    act.dma_start(vec_rows[row:row + rows, 0:width], view).then_inc(sem[vecs_landed], add(vecs_landed, 16))
                act.wait_ge(sem["angles"], past["angles"] + 1)
                act.wait_ge(sem["rope_step"], count["rope_step"])
                nc.scalar.activation(both[:], both[:], ACT.Sin).then_inc(sem["sines"], add("sines", 1))
                split_feature_major_act(g, act, 0, g.xT, KD, banks)
                g.split_high(act, RING)

            @block.vector
            def _(dve):
                nc.vector.memset(vec_rows[:], 0.0).then_inc(sem[vecs_cleared], add(vecs_cleared, 1))
                step = "rope_step"

                def then(ins):
                    ins.then_inc(sem[step], add(step, 1))
                    dve.wait_ge(sem[step], count[step])

                for i, f in enumerate(inverse_frequencies()):
                    nc.vector.memset(freq[:, i:i + 1], f).then_inc(sem[step], add(step, 1))
                nc.vector.memset(tab[:, :, 0:P], 1.0).then_inc(sem[step], add(step, 1))
                nc.vector.memset(tab[:, :, P:2 * P], 0.0).then_inc(sem[step], add(step, 1))
                dve.wait_ge(sem["pos_landed"], past["pos_landed"] + 16)
                then(nc.vector.tensor_copy(pos[:], pos_i[:]))
                for j in range(NT):
                    then(nc.vector.tensor_scalar(angle[:, j, :], freq[:], pos[:, j:j + 1], None, ALU.mult))
                then(nc.vector.tensor_scalar(turns[:], angle[:], 1.0 / (2.0 * np.pi), None, ALU.mult))
                then(nc.vector.tensor_scalar(turns[:], turns[:], ROUND, None, ALU.add))
                then(nc.vector.tensor_scalar(turns[:], turns[:], ROUND, None, ALU.subtract))
                for part in TWO_PI_PARTS:
                    then(nc.vector.scalar_tensor_tensor(out=angle[:], in0=turns[:], scalar=-part, in1=angle[:], op0=ALU.mult, op1=ALU.add))
                then(nc.vector.tensor_scalar(both[:, 0], angle[:], np.pi / 2, None, ALU.add))
                then(nc.vector.tensor_scalar(wrap[:], both[:, 0], np.pi, -2.0 * np.pi, ALU.is_gt, ALU.mult))
                then(nc.vector.tensor_tensor(both[:, 0], both[:, 0], wrap[:], ALU.add))
                nc.vector.tensor_scalar(both[:, 0], both[:, 0], 3.1415925, -3.1415925, ALU.min, ALU.max).then_inc(sem[step], add(step, 1))
                nc.vector.tensor_scalar(both[:, 1], angle[:], 3.1415925, -3.1415925, ALU.min, ALU.max).then_inc(sem["angles"], add("angles", 1))
                blocks = "same64_made"
                nc.vector.memset(g.same64[:], 0.0).then_inc(sem[blocks], add(blocks, 1))
                nc.vector.memset(g.keep_state[:], 1.0).then_inc(sem[blocks], add(blocks, 1))
                dve.wait_ge(sem[blocks], past[blocks] + 2)
                for b in range(2):
                    nc.vector.memset(g.same64[64 * b:64 * b + 64, 64 * b:64 * b + 64], 1.0).then_inc(sem[blocks], add(blocks, 1))
                nc.vector.memset(g.keep_state[:].rearrange("p (c i) -> p c i", i=GLA_CHUNK)[:, :, 0:1], 0.0).then_inc(sem[blocks], add(blocks, 1))
                dve.wait_ge(sem[blocks], past[blocks] + 5)
                dve.wait_ge(sem[const_made], past[const_made] + 5)
                for out, m in ((g.not_before64, g.not_before), (g.after64, g.after)):
                    nc.vector.tensor_tensor(out[:], m[:], g.same64[:], ALU.mult).then_inc(sem["masks64"], add("masks64", 1))
                dve.wait_ge(sem["sines"], past["sines"] + 1)
                cos, sin = both[:, 0], both[:, 1]
                for out, src, f0, n, sign in ((head_c, cos, 0, HALF, 1.0), (head_s, sin, 0, HALF, -1.0)):
                    nc.vector.tensor_scalar(out[:, :, 0:n], src[:, :, f0:f0 + n], sign, None, ALU.mult).then_inc(sem["tables"], add("tables", 1))
                    nc.vector.tensor_copy(out[:, :, n:2 * n], src[:, :, f0:f0 + n]).then_inc(sem["tables"], add("tables", 1))
                for b in range(0, P, IDX_DIM):
                    for out, src, sign in ((idx_c, cos, 1.0), (idx_s, sin, -1.0)):
                        n = IDX_HALF
                        nc.vector.tensor_scalar(out[:, :, b:b + n], src[:, :, HALF:HALF + n], sign, None, ALU.mult).then_inc(sem["tables"], add("tables", 1))
                        nc.vector.tensor_copy(out[:, :, b + n:b + 2 * n], src[:, :, HALF:HALF + n]).then_inc(sem["tables"], add("tables", 1))
                split_feature_major_dve(g, dve, 0, g.xT, KD, banks)
                dve.wait_ge(sem[cols_turned], past[cols_turned] + 1)
                nc.vector.tensor_copy(g.cols[:], g.ps[:, 6, 0:P]).then_inc(sem[cols_made], add(cols_made, 1))
                dve.wait_ge(sem["tables_turned"], past["tables_turned"] + 1)
                for i, dst in enumerate((g.idx_cos, g.idx_sin)):
                    nc.vector.tensor_copy(dst[:], ps[:, i, :]).then_inc(sem["tables_copied"], add("tables_copied", 1))
                for i, dst in enumerate((g.head_cos, g.head_sin)):
                    nc.vector.tensor_copy(dst[:], ps[0:2 * HALF, 2 + i, :]).then_inc(sem["tables_copied"], add("tables_copied", 1))

            @block.tensor
            def _(pe):
                pe.wait_ge(sem[const_made], past[const_made] + 3)
                pe.wait_ge(sem[x_landed], past[x_landed] + 16 * NT)
                split_feature_major_pe(g, pe, 0, x_tok, KD, NT, banks)
                pe.wait_ge(sem[vecs_landed], past[vecs_landed] + 16 * len(g.vec_rows))
                nc.tensor.transpose(g.ps[:, 6, 0:P], vec_rows[:], g.ident[:]).then_inc(sem[cols_turned], add(cols_turned, 1))
                pe.wait_ge(sem["turned_low"], past["turned_low"] + KD)
                pe.wait_ge(sem["tables"], past["tables"] + 12)
                for i, src in enumerate((idx_c, idx_s, head_c, head_s)):
                    n = src.shape[2]
                    for j in range(NT):
                        ins = nc.tensor.transpose(ps[0:n, i, j * P:(j + 1) * P], src[:, j, :], g.ident[:])
                ins.then_inc(sem["tables_turned"], add("tables_turned", 1))

            @block.gpsimd
            def _(pool):
                nc.gpsimd.memset(g.ident[:], 0.0).then_inc(sem[const_made], add(const_made, 1))
                nc.gpsimd.memset(g.ones[:], 1.0).then_inc(sem[const_made], add(const_made, 1))
                pool.wait_ge(sem[const_made], past[const_made] + 2)
                nc.gpsimd.affine_select(out=g.ident[:], in_=g.ident[:], compare_op=ALU.not_equal, fill=1.0, base=0,
                                                      pattern=[[-1, P]], channel_multiplier=1).then_inc(sem[const_made], add(const_made, 1))
                for out, base, cm, step in ((g.not_before, 0, -1, 1), (g.after, -1, -1, 1)):
                    nc.gpsimd.affine_select(out=out[:], in_=g.ones[:], compare_op=ALU.is_ge, fill=0.0, base=base,
                                                          pattern=[[step, P]], channel_multiplier=cm).then_inc(sem[const_made], add(const_made, 1))

                for i, mask in enumerate(g.levelT + [g.level1]):
                    m = 2 ** i if i < len(g.levelT) else 1
                    n = P // (2 * m)
                    view = mask[:].rearrange("p (b x) -> p b x", x=2 * m)
                    up = 0 if i < len(g.levelT) else 1
                    for a, (base, cm, pattern) in enumerate(((-up * m, 1, [[-2 * m, n], [0, 2 * m]]), (up * m + m - 1, -1, [[2 * m, n], [0, 2 * m]]),
                                                            ((up - 1) * m, 0, [[0, n], [1 - 2 * up, 2 * m]]))):
                        src = g.ones[:].rearrange("p (b x) -> p b x", x=2 * m) if a == 0 else view
                        nc.gpsimd.affine_select(out=view, in_=src, compare_op=ALU.is_ge, fill=0.0, base=base, pattern=pattern, channel_multiplier=cm).then_inc(sem[const_made], add(const_made, 1))
                        pool.wait_ge(sem[const_made], count[const_made])
                g.split_low(pool)
    g.sem.end_phase()


def phase_gla(g, mix_a, mix_b, gT, first):
    nc, t = g.nc, g.t
    sem, past, count, add = g.sem, g.sem.past, g.sem.count, g.sem.add
    NF = GLA_HEADS * GLA_DK // P
    DT = GLA_DK // P
    with ExitStack() as stack:
        w_a = g.sb(stack, "w_a", [P, KD, GLA_RANK])
        w_a_parts = [g.sb(stack, f"w_a_{part}", [P, KD, GLA_RANK], F32R) for part in ("high", "low")]
        w_a2_room = g.sb(stack, "w_a2", [P, GLA_HEADS * GLA_DK])
        w_a2 = w_a2_room[0:GLA_RANK + 1, :]
        aT = g.sb(stack, "aT", [GLA_RANK + 1, T])
        decay_log = mix_b[:, 0:NF, :]
        ks_tok = mix_b[:, NF:, :].rearrange("p (j a) t -> p j (a t)", j=NT)
        v_tok = g.sb(stack, "v_tok", [P, NT, DI])
        chunk_decay = g.sb(stack, "chunk_decay", [P, NF, NCH])
        to_end = g.sb(stack, "to_end", [P, 2, T])
        attn = w_a2_room[:, 0:GLA_HEADS * P].rearrange("p (h s) -> p h s", h=GLA_HEADS)
        sq = w_a2_room[:, GLA_DV:2 * GLA_DV]
        sumsq = g.sb(stack, "sumsq", [P, NT * GLA_HEADS])
        root = g.sb(stack, "root", [P, NT * GLA_HEADS])
        rstd = g.sb(stack, "rstd", [P, NT * GLA_HEADS])
        z_silu = to_end
        qT, kT = mix_a[:, 0:NF, :], mix_a[:, NF:2 * NF, :]
        state = decay_log
        ps = g.ps
        HALVES = COLS // CHUNK
        c_v = first
        c_q = c_v + DI // CHUNK
        c_z = c_q + 2 * NF * P // CHUNK
        end = c_z + DI // CHUNK
        small_landed = "small_landed"
        w_in = t["gla_w_in"][0]
        a0 = 2 * GLA_HEADS * GLA_DK + 2 * DI

        with nc.Block("gla", no_gpsimd_drain=True) as block:

            @block.tensor
            def _(pe):
                def low_rank():
                    pe.wait_ge(sem[small_landed], past[small_landed] + 48)
                    pe.wait_ge(sem["w_a_split"], past["w_a_split"] + 2)
                    for k in range(KD):
                        ins = g.split_product(ps[0:GLA_RANK, 4, :], columns(w_a_parts, k), columns(g.xT, k), k == 0, k == KD - 1)
                    ins.then_inc(sem["aT_ready"], add("aT_ready", 1))

                def gates(b):
                    pe.wait_ge(sem["aT_copied"], past["aT_copied"] + 2)
                    for i in range(4):
                        if b:
                            pe.wait_ge(sem["log_gate"], past["log_gate"] + i + 1)
                        f = 4 * b + i
                        g.product(ps[:, 4 + i, :], w_a2[:, f * P:(f + 1) * P], aT[:]).then_inc(sem["u_ready"], add("u_ready", 1))

                for c in range(4):
                    for half in range(HALVES):
                        w = g.chunk(pe, c_v + HALVES * c + half)
                        done = "v_ready" if half == HALVES - 1 else "v_half"
                        for j in range(NT):
                            n = 4 * c + j
                            if half == 0 and n >= 4:
                                pe.wait_ge(sem["v_copied"], past["v_copied"] + n - 3)
                            for k in range(KD):
                                ins = g.split_product(ps[:, n % 4, half * CHUNK:(half + 1) * CHUNK], columns(g.xT, k, slice(j * P, (j + 1) * P)),
                                                      columns(w, k), k == 0, k == KD - 1)
                            ins.then_inc(sem[done], add(done, 1))
                        g.release(done)
                    if c == 0:
                        low_rank()
                    elif c < 3:
                        gates(c - 1)
                pe.wait_ge(sem["v_copied"], past["v_copied"] + 16)
                pe.wait_ge(sem["log_gate"], past["log_gate"] + 8)

                def turn_ks(f):
                    pe.wait_ge(sem["ks_made"], past["ks_made"] + f + 1)
                    if f >= 2:
                        pe.wait_ge(sem["ks_copied"], past["ks_copied"] + f - 1)
                    for j in range(NT):
                        ins = nc.tensor.transpose(ps[:, 6 + f % 2, j * P:(j + 1) * P], to_end[:, f % 2, j * P:(j + 1) * P], g.ident[:])
                    ins.then_inc(sem["ks_turned"], add("ks_turned", 1))

                for n in range(2 * NF):
                    if n % 2 == 0:
                        w = g.chunk(pe, c_q + n // 2)
                    if n >= 6:
                        pe.wait_ge(sem["qk_used"], past["qk_used"] + n - 5)
                    for k in range(KD):
                        ins = g.split_product(ps[:, n % 6, :], columns(w, k, slice((n % 2) * P, (n % 2 + 1) * P)), columns(g.xT, k), k == 0, k == KD - 1)
                    ins.then_inc(sem["qk_ready"], add("qk_ready", 1))
                    if n % 2 == 1:
                        g.release("qk_ready")
                    if n > NF:
                        turn_ks(n - NF - 1)
                turn_ks(NF - 1)

                pe.wait_ge(sem["qk_used"], past["qk_used"] + 2 * NF)
                pe.wait_ge(sem["ks_copied"], past["ks_copied"] + NF)
                update = 0
                for j in range(NT):
                    tile = slice(j * P, (j + 1) * P)
                    if j:
                        pe.wait_ge(sem["attn_masked"], past["attn_masked"] + j)
                    for h in range(GLA_HEADS):
                        for d in range(DT):
                            ins = g.product(ps[:, 7, h * P:(h + 1) * P], kT[:, DT * h + d, tile], qT[:, DT * h + d, tile],
                                            d == 0, d == DT - 1)
                    ins.then_inc(sem["attn_ready"], add("attn_ready", 1))
                    pe.wait_ge(sem["attn_masked"], past["attn_masked"] + j + 1)
                    for h in range(GLA_HEADS):
                        if j:
                            pe.wait_ge(sem["o_copied"], past["o_copied"] + 2 * (4 * (j - 1) + h) + 2)
                        ins = g.product(ps[:, h, :], attn[:, h, :], v_tok[:, j, h * GLA_DV:(h + 1) * GLA_DV], True, False, check=False)
                    ins.then_inc(sem["intra_done"], add("intra_done", 1))
                    for half in range(2):
                        c = 2 * j + half
                        rows = slice(half * GLA_CHUNK, (half + 1) * GLA_CHUNK)
                        toks = slice(c * GLA_CHUNK, (c + 1) * GLA_CHUNK)
                        for h in range(GLA_HEADS):
                            if c:
                                pe.wait_ge(sem["state_ready"], past["state_ready"] + DT * (4 * (c - 1) + h) + DT)
                                for d in range(DT):
                                    ins = g.product(ps[rows, h, :], qT[:, DT * h + d, toks], state[:, DT * h + d, :], False, d == DT - 1, check=False)
                                if half == 1:
                                    ins.then_inc(sem["o_ready"], add("o_ready", 1))
                            if c == NCH - 1:
                                continue
                            for d in range(DT):
                                f = DT * h + d
                                if update >= 3:
                                    pe.wait_ge(sem["state_ready"], past["state_ready"] + update - 2)
                                ins = g.product(ps[:, 4 + update % 3, :], ks_tok[rows, j, f * P:(f + 1) * P],
                                                v_tok[rows, j, h * GLA_DV:(h + 1) * GLA_DV])
                                ins.then_inc(sem["update_ready"], add("update_ready", 1))
                                update += 1

                for c in range(4):
                    for half in range(HALVES):
                        w = g.chunk(pe, c_z + HALVES * c + half)
                        done = "z_ready" if half == HALVES - 1 else "z_half"
                        for j in range(NT):
                            n = 4 * c + j
                            if half == 0 and n < 4:
                                pe.wait_ge(sem["o_copied"], past["o_copied"] + 2 * 16)
                            elif half == 0:
                                pe.wait_ge(sem["z_silu"], past["z_silu"] + n - 3)
                            for k in range(KD):
                                ins = g.split_product(ps[:, n % 4, half * CHUNK:(half + 1) * CHUNK], columns(g.xT, k, slice(j * P, (j + 1) * P)),
                                                      columns(w, k), k == 0, k == KD - 1)
                            ins.then_inc(sem[done], add(done, 1))
                        g.release(done)
                pe.wait_ge(sem["gated"], past["gated"] + 16)
                split_feature_major_pe(g, pe, 0, v_tok, KI, NT, [4, 5, 6, 7])

            @block.scalar
            def _(act):
                act.dma_start(w_a[:], w_in[:, a0:a0 + GLA_RANK].rearrange("(k p) n -> p k n", p=P)).then_inc(sem[small_landed], add(small_landed, 16))
                act.dma_start(w_a2[0:GLA_RANK, :], t["gla_w_a2"][0]).then_inc(sem[small_landed], add(small_landed, 16))
                act.dma_start(w_a2[GLA_RANK:GLA_RANK + 1, :], t["gla_b_a"]).then_inc(sem[small_landed], add(small_landed, 16))
                g.split_high(act, c_v + RING)
                act.wait_ge(sem[small_landed], past[small_landed] + 48)
                nc.scalar.activation(w_a_parts[0][:], w_a[:], ACT.Copy).then_inc(sem["w_a_split"], add("w_a_split", 1))
                def v_copy(c):
                    g.split_high(act, c_v + 2 * c + 3)
                    for j in range(NT):
                        n = 4 * c + j
                        act.wait_ge(sem["v_ready"], past["v_ready"] + n + 1)
                        nc.scalar.activation(v_tok[:, j, c * COLS:(c + 1) * COLS], ps[:, n % 4, :], ACT.Copy).then_inc(sem["v_copied"], add("v_copied", 1))
                    g.split_high(act, c_v + 2 * c + 4)

                v_copy(0)
                act.wait_ge(sem["aT_ready"], past["aT_ready"] + 1)
                act.wait_ge(sem["aT_copied"], past["aT_copied"] + 1)
                nc.scalar.activation(aT[0:GLA_RANK, :], ps[0:GLA_RANK, 4, :], ACT.Copy).then_inc(sem["aT_copied"], add("aT_copied", 1))
                v_copy(1)
                for b in range(2):
                    for i in range(4):
                        f = 4 * b + i
                        act.wait_ge(sem["u_ready"], past["u_ready"] + f + 1)
                        nc.scalar.activation(kT[:, f, :], ps[:, 4 + i, :], ACT.Abs).then_inc(sem["abs_u"], add("abs_u", 1))
                    for i in range(4):
                        f = 4 * b + i
                        act.wait_ge(sem["abs_u"], past["abs_u"] + f + 1)
                        nc.scalar.activation(kT[:, f, :], kT[:, f, :], ACT.Exp, scale=-1.0).then_inc(sem["exp_neg_abs"], add("exp_neg_abs", 1))
                    for i in range(4):
                        f = 4 * b + i
                        act.wait_ge(sem["exp_neg_abs"], past["exp_neg_abs"] + f + 1)
                        nc.scalar.activation(kT[:, f, :], kT[:, f, :], ACT.Ln, bias=1.0).then_inc(sem["log1p"], add("log1p", 1))
                    v_copy(2 + b)
                for f in range(NF):
                    if f >= 4 and f % 2 == 0:
                        g.split_high(act, c_q + f // 2 + 1)
                    act.wait_ge(sem["decay_log"], past["decay_log"] + f + 1)
                    nc.scalar.activation(qT[:, f, :], decay_log[:, f, :], ACT.Exp, scale=1.0 / GATE_NORM).then_inc(sem["decays"], add("decays", 1))
                    nc.scalar.activation(kT[:, f, :], decay_log[:, f, :], ACT.Exp, scale=-1.0 / GATE_NORM).then_inc(sem["decays"], add("decays", 1))
                    ends = decay_log[:, f, :].rearrange("p (c i) -> p c i", i=GLA_CHUNK)[:, :, GLA_CHUNK - 1]
                    nc.scalar.activation(chunk_decay[:, f, :], ends, ACT.Exp, scale=1.0 / GATE_NORM).then_inc(sem["decays"], add("decays", 1))

                def ks_copy(f):
                    act.wait_ge(sem["ks_turned"], past["ks_turned"] + f + 1)
                    nc.scalar.activation(ks_tok[:, :, f * P:(f + 1) * P],
                                                             ps[:, 6 + f % 2, :].rearrange("p (j i) -> p j i", i=P), ACT.Copy).then_inc(sem["ks_copied"], add("ks_copied", 1))

                g.split_high(act, c_q + 5)
                for f in range(NF):
                    if f % 2 == 0:
                        g.split_high(act, c_q + 6 + f // 2)
                    act.wait_ge(sem["rest_log"], past["rest_log"] + f + 1)
                    nc.scalar.activation(to_end[:, f % 2, :], to_end[:, f % 2, :], ACT.Exp, scale=1.0 / GATE_NORM).then_inc(sem["rest_decay"], add("rest_decay", 1))
                    if f:
                        ks_copy(f - 1)
                ks_copy(NF - 1)
                g.split_high(act, c_z + RING)
                for n in range(NT * GLA_HEADS):
                    j, h = n // GLA_HEADS, n % GLA_HEADS
                    act.wait_ge(sem["o_ready"], past["o_ready"] + n + 1)
                    if j < NT - 1:
                        act.wait_ge(sem["update_ready"], past["update_ready"] + DT * (4 * (2 * j + 1) + h + 1))
                    if n:
                        act.wait_ge(sem["o_copied"], past["o_copied"] + 2 * n)
                    nc.scalar.activation(sq[:], ps[:, h, :], ACT.Square, accum_out=sumsq[:, n:n + 1]).then_inc(sem["o_copied"], add("o_copied", 1))
                    nc.scalar.activation(v_tok[:, j, h * GLA_DV:(h + 1) * GLA_DV], ps[:, h, :], ACT.Copy).then_inc(sem["o_copied"], add("o_copied", 1))
                act.wait_ge(sem["mean_sq"], past["mean_sq"] + 1)
                nc.scalar.activation(root[:], root[:], ACT.Sqrt).then_inc(sem["root"], add("root", 1))
                for n in range(16):
                    if n % 4 == 0:
                        g.split_high(act, c_z + n // 2 + 3)
                    act.wait_ge(sem["z_ready"], past["z_ready"] + n + 1)
                    if n >= 2:
                        act.wait_ge(sem["gated"], past["gated"] + n - 1)
                    nc.scalar.activation(z_silu[:, n % 2, :], ps[:, n % 4, :], ACT.Silu).then_inc(sem["z_silu"], add("z_silu", 1))
                    if n % 4 == 3:
                        g.split_high(act, c_z + n // 2 + 3)
                split_feature_major_act(g, act, 0, gT, KI, [4, 5, 6, 7], scale=g.col("gla_gn_g"))

            @block.vector
            def _(dve):
                nc.vector.memset(aT[:], 1.0).then_inc(sem["aT_copied"], add("aT_copied", 1))
                dve.wait_ge(sem["w_a_split"], past["w_a_split"] + 1)
                nc.vector.tensor_tensor(w_a_parts[1][:], w_a[:], w_a_parts[0][:].bitcast(F32), ALU.subtract).then_inc(sem["w_a_split"], add("w_a_split", 1))
                for b in range(2):
                    for i in range(4):
                        f = 4 * b + i
                        dve.wait_ge(sem["log1p"], past["log1p"] + f + 1)
                        nc.vector.scalar_tensor_tensor(out=kT[:, f, :], in0=ps[:, 4 + i, :], scalar=0.0, in1=kT[:, f, :],
                                                                          op0=ALU.min, op1=ALU.subtract).then_inc(sem["log_gate"], add("log_gate", 1))
                        dve.wait_ge(sem["log_gate"], past["log_gate"] + f + 1)
                        nc.vector.tensor_tensor_scan(decay_log[:, f, :], g.keep_state[:], kT[:, f, :], 0.0, ALU.mult, ALU.add).then_inc(sem["decay_log"], add("decay_log", 1))
                for n in range(NF):
                    dve.wait_ge(sem["qk_ready"], past["qk_ready"] + n + 1)
                    dve.wait_ge(sem["decays"], past["decays"] + 3 * n + 3)
                    nc.vector.scalar_tensor_tensor(out=qT[:, n, :], in0=ps[:, n % 6, :], scalar=GLA_DK ** -0.5, in1=qT[:, n, :],
                                                                     op0=ALU.mult, op1=ALU.mult).then_inc(sem["qk_used"], add("qk_used", 1))
                for f in range(NF):
                    n = NF + f
                    if f >= 2:
                        dve.wait_ge(sem["ks_turned"], past["ks_turned"] + f - 1)
                    ends = decay_log[:, f, :].rearrange("p (c i) -> p c i", i=GLA_CHUNK)
                    nc.vector.tensor_tensor(to_end[:, f % 2, :].rearrange("p (c i) -> p c i", i=GLA_CHUNK),
                                                               ends[:, :, GLA_CHUNK - 1:GLA_CHUNK].to_broadcast([P, NCH, GLA_CHUNK]),
                                                               ends, ALU.subtract).then_inc(sem["rest_log"], add("rest_log", 1))
                    dve.wait_ge(sem["qk_ready"], past["qk_ready"] + n + 1)
                    dve.wait_ge(sem["rest_decay"], past["rest_decay"] + f + 1)
                    nc.vector.tensor_tensor(to_end[:, f % 2, :], ps[:, n % 6, :], to_end[:, f % 2, :], ALU.mult).then_inc(sem["ks_made"], add("ks_made", 1))
                    nc.vector.tensor_tensor(kT[:, f, :], ps[:, n % 6, :], kT[:, f, :], ALU.mult).then_inc(sem["qk_used"], add("qk_used", 1))
                update = 0
                for j in range(NT):
                    dve.wait_ge(sem["attn_ready"], past["attn_ready"] + j + 1)
                    if j:
                        dve.wait_ge(sem["intra_done"], past["intra_done"] + j)
                    nc.vector.tensor_tensor(attn[:], ps[:, 7, :].rearrange("p (h i) -> p h i", h=GLA_HEADS),
                                                                  g.not_before64[:].unsqueeze(1).to_broadcast([P, GLA_HEADS, P]), ALU.mult).then_inc(sem["attn_masked"], add("attn_masked", 1))
                    for half in range(2):
                        c = 2 * j + half
                        if c == NCH - 1:
                            continue
                        for f in range(NF):
                            dve.wait_ge(sem["update_ready"], past["update_ready"] + update + 1)
                            if c == 0:
                                ins = nc.vector.tensor_copy(state[:, f, :], ps[:, 4 + update % 3, :])
                            else:
                                ins = nc.vector.scalar_tensor_tensor(out=state[:, f, :], in0=state[:, f, :], scalar=chunk_decay[:, f, c:c + 1],
                                                                     in1=ps[:, 4 + update % 3, :], op0=ALU.mult, op1=ALU.add)
                            ins.then_inc(sem["state_ready"], add("state_ready", 1))
                            update += 1
                dve.wait_ge(sem["o_copied"], past["o_copied"] + 32)
                nc.vector.tensor_scalar(root[:], sumsq[:], 1.0 / GLA_DV, LN_EPS, ALU.mult, ALU.add).then_inc(sem["mean_sq"], add("mean_sq", 1))
                dve.wait_ge(sem["root"], past["root"] + 1)
                nc.vector.reciprocal(rstd[:], root[:]).then_inc(sem["rstd"], add("rstd", 1))
                dve.wait_ge(sem["rstd"], past["rstd"] + 1)
                for n in range(16):
                    h, j = n // 4, n % 4
                    dve.wait_ge(sem["z_silu"], past["z_silu"] + n + 1)
                    o = v_tok[:, j, h * GLA_DV:(h + 1) * GLA_DV]
                    i = j * GLA_HEADS + h
                    nc.vector.scalar_tensor_tensor(out=o, in0=o, scalar=rstd[:, i:i + 1], in1=z_silu[:, n % 2, :],
                                                                   op0=ALU.mult, op1=ALU.mult).then_inc(sem["gated"], add("gated", 1))
                split_feature_major_dve(g, dve, 0, gT, KI, [4, 5, 6, 7], scale=g.col("gla_gn_g"))

            @block.gpsimd
            def _(pool):
                g.split_low(pool)

            @block.sync
            def _(sp):
                g.load_chunks(sp)
    g.sem.end_phase()


def phase_post(g, layer, gT, first, then_norm, gT_at):
    nc, t = g.nc, g.t
    sem, past, count, add = g.sem, g.sem.past, g.sem.count, g.sem.add
    NH = D // COLS
    KP = 2
    HALVES = COLS // CHUNK
    ps = g.ps
    end = first + 2 * D // CHUNK + D // CHUNK
    x_from = t["x"][0].rearrange("(j p) d -> p j d", p=P) if layer == 0 else g.x_dram
    with ExitStack() as stack:
        x = r = g.sb(stack, f"x{layer}", [P, NT, D])
        w_ple = g.alias(f"w_ple{layer}", [P, KP, D], F32, gT_at)
        scaled = g.alias(f"x_scaled{layer}", [P, NT, D], F32, gT_at + 4 * KP * D)
        gain = g.sb(stack, f"gain{layer}", [P, D])
        shift = g.sb(stack, f"shift{layer}", [P, D])
        p_tok = g.sb(stack, f"p_tok{layer}", [P, NT, KP * P])
        pT = g.sb(stack, f"pT{layer}", [P, KP, T])
        gate = g.sb(stack, f"gate{layer}", [P, 2, COLS])
        stats = g.sb(stack, f"stats{layer}", [P, NT, NH, 6])
        moments = g.sb(stack, f"moments{layer}", [P, NT, 2])
        rstd = g.sb(stack, f"rstd_x{layer}", [P, NT])
        sumsq = g.sb(stack, f"sumsq_x{layer}", [P, NT])
        with nc.Block(f"post{layer}", no_gpsimd_drain=True) as block:

            @block.tensor
            def _(pe):
                for n in range(NH * HALVES):
                    cols = slice((n % HALVES) * CHUNK, (n % HALVES + 1) * CHUNK)
                    for c in range(2):
                        w = g.chunk(pe, first + 2 * n + c)
                        for j in range(NT):
                            for k in range(KD):
                                ins = g.split_product(ps[:, n // HALVES * NT + j, cols], columns(gT, c * KD + k, slice(j * P, (j + 1) * P)), columns(w, k),
                                                      c == 0 and k == 0, c == 1 and k == KD - 1)
                            ins.then_inc(sem["y_part"], add("y_part", 1))
                        g.release("y_part")
                pe.wait_ge(sem["p_landed"], past["p_landed"] + 16)
                pe.wait_ge(sem["y_added"], past["y_added"] + NH * NT)
                to_feature_major_pe(g, pe, (0, 0), p_tok, KP, NT, [6, 7])
                to_x = [0, 1, 2, 3, 4, 5]
                for j in range(NT):
                    pe.wait_ge(sem["normed"], past["normed"] + NT)
                split_feature_major_pe(g, pe, 0, r, KD, NT, to_x)
                pe.wait_ge(sem["w_ple_landed"], past["w_ple_landed"] + 16)
                pe.wait_ge(sem["turned_by_act"], past["turned_by_act"] + KP // 2)
                pe.wait_ge(sem["turned_by_dve"], past["turned_by_dve"] + KP // 2)
                pe.wait_ge(sem["turned_low"], past["turned_low"] + KD)
                for n in range(NH):
                    for half in range(HALVES):
                        w = g.chunk(pe, first + 2 * NH * HALVES + HALVES * n + half)
                        done = "gate_ready" if half == HALVES - 1 else "gate_half"
                        for j in range(NT):
                            i = n * NT + j
                            tile = slice(j * P, (j + 1) * P)
                            if half == 0:
                                if i >= 4:
                                    pe.wait_ge(sem["ple_gated"], past["ple_gated"] + i - 3)
                                for k in range(KP):
                                    g.product(ps[:, 4 + i % 4, :], pT[:, k, tile], w_ple[:, k, n * COLS:(n + 1) * COLS], k == 0, k == KP - 1)
                            for k in range(KD):
                                ins = g.split_product(ps[:, i % 4, half * CHUNK:(half + 1) * CHUNK], columns(g.xT, k, tile), columns(w, k), k == 0, k == KD - 1)
                            ins.then_inc(sem[done], add(done, 1))
                        g.release(done)
                pe.wait_ge(sem["ple_gated"], past["ple_gated"] + NH * NT)
                if then_norm:
                    pe.wait_ge(sem["x_scaled"], past["x_scaled"] + NT)
                else:
                    pe.wait_ge(sem["x_added"], past["x_added"] + NH * NT)
                split_feature_major_pe(g, pe, KD, scaled if then_norm else x, KD, NT, [0, 1, 2, 3, 4, 5])

            @block.scalar
            def _(act):
                act.dma_start(p_tok[:], t["p"][layer, 0].rearrange("(j p) d -> p j d", p=P)).then_inc(sem["p_landed"], add("p_landed", 16))
                act.dma_start(gain[:], t["ln_g"][layer:layer + 1, :].to_broadcast([P, D])).then_inc(sem["gain_landed"], add("gain_landed", 16))
                act.dma_start(shift[:], t["ln_b"][layer:layer + 1, :].to_broadcast([P, D])).then_inc(sem["gain_landed"], add("gain_landed", 16))
                for n in range(2 * NH * HALVES):
                    g.split_high(act, first + n + 1 + RING)
                act.wait_ge(sem["y_part"], past["y_part"] + 2 * NH * HALVES * NT)
                act.dma_start(w_ple[:], t["ple_w"][layer].rearrange("(k p) n -> p k n", p=P)).then_inc(sem["w_ple_landed"], add("w_ple_landed", 16))
                to_feature_major_act(g, act, 0, pT, KP, T, [6, 7])
                act.wait_ge(sem["variance"], past["variance"] + NT)
                nc.scalar.activation(rstd[:], rstd[:], ACT.Sqrt).then_inc(sem["deviation"], add("deviation", 1))
                split_feature_major_act(g, act, 0, g.xT, KD, [0, 1, 2, 3, 4, 5])
                gates = first + 2 * NH * HALVES
                for i in range(NH * NT):
                    if i % NT == 0:
                        g.split_high(act, gates + HALVES * (i // NT) + 1 + RING)
                    act.wait_ge(sem["gate_ready"], past["gate_ready"] + i + 1)
                    if i >= 2:
                        act.wait_ge(sem["ple_gated"], past["ple_gated"] + i - 1)
                        act.wait_ge(sem["x_added"], past["x_added"] + i - 1)
                    nc.scalar.activation(gate[:, i % 2, :], ps[:, i % 4, :], ACT.Sigmoid).then_inc(sem["gate_sigmoid"], add("gate_sigmoid", 1))
                g.split_high(act, end + RING)
                if then_norm:
                    for j in range(NT):
                        act.wait_ge(sem["x_added"], past["x_added"] + NT + j + 1)
                        nc.scalar.activation(scaled[:, j, :], x[:, j, :], ACT.Square, accum_out=sumsq[:, j:j + 1]).then_inc(sem["x_squared"], add("x_squared", 1))
                    act.wait_ge(sem["x_mean_sq"], past["x_mean_sq"] + 1)
                    nc.scalar.activation(sumsq[:], sumsq[:], ACT.Sqrt).then_inc(sem["x_root"], add("x_root", 1))
                    for j in range(NT):
                        act.wait_ge(sem["x_rstd"], past["x_rstd"] + 1)
                        nc.scalar.activation(scaled[:, j, :], x[:, j, :], ACT.Copy, scale=sumsq[:, j:j + 1]).then_inc(sem["x_scaled"], add("x_scaled", 1))
                split_feature_major_act(g, act, KD, g.xT, KD, [0, 1, 2, 3, 4, 5], scale=g.col("norm_g_2") if then_norm else None)

            @block.vector
            def _(dve):
                dve.wait_ge(sem["x_back"], past["x_back"] + 16)
                for n in range(NH):
                    for j in range(NT):
                        cols = slice(n * COLS, (n + 1) * COLS)
                        dve.wait_ge(sem["y_part"], past["y_part"] + 2 * NT * (HALVES * n + HALVES - 1) + NT + j + 1)
                        i = n * NT + j
                        nc.vector.scalar_tensor_tensor(out=r[:, j, cols], in0=x[:, j, cols], scalar=ALPHA, in1=ps[:, i, :],
                                                                         op0=ALU.mult, op1=ALU.add).then_inc(sem["y_added"], add("y_added", 1))
                        dve.wait_ge(sem["y_added"], past["y_added"] + i + 1)
                        nc.vector.bn_stats(stats[:, j, n, :], r[:, j, cols]).then_inc(sem["bn_stats"], add("bn_stats", 1))
                to_feature_major_dve(g, dve, 0, pT, KP, T, [6, 7])
                dve.wait_ge(sem["bn_stats"], past["bn_stats"] + NH * NT)
                for j in range(NT):
                    nc.vector.bn_aggr(moments[:, j, :], stats[:, j, :, :].rearrange("p a b -> p (a b)")).then_inc(sem["moments"], add("moments", 1))
                dve.wait_ge(sem["moments"], past["moments"] + NT)
                for j in range(NT):
                    nc.vector.tensor_scalar(rstd[:, j:j + 1], moments[:, j, 1:2], LN_EPS, None, ALU.add).then_inc(sem["variance"], add("variance", 1))
                dve.wait_ge(sem["deviation"], past["deviation"] + 1)
                nc.vector.reciprocal(rstd[:], rstd[:]).then_inc(sem["rstd_x"], add("rstd_x", 1))
                dve.wait_ge(sem["rstd_x"], past["rstd_x"] + 1)
                dve.wait_ge(sem["gain_landed"], past["gain_landed"] + 32)
                for j in range(NT):
                    nc.vector.tensor_scalar(r[:, j, :], r[:, j, :], moments[:, j, 0:1], rstd[:, j:j + 1], ALU.subtract, ALU.mult).then_inc(sem["centred"], add("centred", 1))
                for j in range(NT):
                    dve.wait_ge(sem["centred"], past["centred"] + j + 1)
                    nc.vector.tensor_tensor(r[:, j, :], r[:, j, :], gain[:], ALU.mult).then_inc(sem["gained"], add("gained", 1))
                for j in range(NT):
                    dve.wait_ge(sem["gained"], past["gained"] + j + 1)
                    nc.vector.tensor_tensor(r[:, j, :], r[:, j, :], shift[:], ALU.add).then_inc(sem["normed"], add("normed", 1))
                dve.wait_ge(sem["normed"], past["normed"] + NT)
                split_feature_major_dve(g, dve, 0, g.xT, KD, [0, 1, 2, 3, 4, 5])
                for i in range(NH * NT):
                    n, j = i // NT, i % NT
                    cols = slice(n * COLS, (n + 1) * COLS)
                    dve.wait_ge(sem["gate_sigmoid"], past["gate_sigmoid"] + i + 1)
                    nc.vector.tensor_tensor(gate[:, i % 2, :], gate[:, i % 2, :], ps[:, 4 + i % 4, :], ALU.mult).then_inc(sem["ple_gated"], add("ple_gated", 1))
                    dve.wait_ge(sem["ple_gated"], past["ple_gated"] + i + 1)
                    nc.vector.tensor_tensor(x[:, j, cols], r[:, j, cols], gate[:, i % 2, :], ALU.add).then_inc(sem["x_added"], add("x_added", 1))
                if then_norm:
                    dve.wait_ge(sem["x_squared"], past["x_squared"] + NT)
                    nc.vector.tensor_scalar(sumsq[:], sumsq[:], 1.0 / D, RMS_EPS, ALU.mult, ALU.add).then_inc(sem["x_mean_sq"], add("x_mean_sq", 1))
                    dve.wait_ge(sem["x_root"], past["x_root"] + 1)
                    nc.vector.reciprocal(sumsq[:], sumsq[:]).then_inc(sem["x_rstd"], add("x_rstd", 1))
                split_feature_major_dve(g, dve, KD, g.xT, KD, [0, 1, 2, 3, 4, 5], scale=g.col("norm_g_2") if then_norm else None)

            @block.gpsimd
            def _(pool):
                g.split_low(pool)

            @block.sync
            def _(sp):
                sp.dma_start(x[:], x_from).then_inc(sem["x_back"], add("x_back", 16))
                g.load_chunks(sp)
                sp.wait_ge(sem["x_added"], past["x_added"] + NH * NT)
                sp.dma_start(g.x_dram, x[:]).then_inc(sem["x_saved"], add("x_saved", 16))
                sp.wait_ge(sem["x_saved"], past["x_saved"] + 16)
    g.sem.end_phase()

DSA_HEADS, DH, IDX_HEADS, IDX_DIM, TOPK = 16, 128, 8, 64, 128
HALF, IDX_HALF = DH // 8, IDX_DIM // 8
ROPE_THETA = 500000.0
ATTN_SCALE = DH ** -0.5
INDEX_SCALE = IDX_HEADS ** -0.5 * IDX_DIM ** -0.5
MASKED, TAKEN = -1e30, -3e38
SWAP_HEAD = [(i + HALF) % (2 * HALF) for i in range(32)]
SWAP_IDX = [(i + IDX_HALF) % (2 * IDX_HALF) if i < 2 * IDX_HALF else i for i in range(32)]
TWO_PI_PARTS = (6.28125, 0.0019350051879882812, 3.0199159819e-07)
ROUND = 1.5 * 2.0 ** 23


def inverse_frequencies():
    return [float(np.float32(ROPE_THETA ** (-2.0 * i / (2 * n)))) for n in (HALF, IDX_HALF) for i in range(n)]


def phase_dsa(g, qT, zT, gT, first):
    nc, t, ps = g.nc, g.t, g.ps
    sem, past, count, add = g.sem, g.sem.past, g.sem.count, g.sem.add
    IT = IDX_HEADS * IDX_DIM // P
    with ExitStack() as stack:
        kT = g.sb(stack, "dsa_kT", [P, T])
        v = g.sb(stack, "dsa_v", [P, NT, DH])
        rot = g.sb(stack, "rot", [P, 2, T])
        kiT = g.sb(stack, "kiT", [P, T])
        wi = g.sb(stack, "wi", [P, NT, IDX_HEADS])
        left = g.sb(stack, "left", [P, NT, T])
        top8 = g.sb(stack, "top8", [P, 8])
        prob = g.sb(stack, "prob", [P, 2, NT, T])
        score, qiT = prob[:, 0], prob[:, 1]
        probT = g.sb(stack, "probT", [P, NT, T])
        relu = probT[:, 0:2]
        peak = g.sb(stack, "peak", [P, 2 * NT])
        shift = g.sb(stack, "peak_shift", [P, 2 * NT])
        total = g.sb(stack, "total", [P, 2 * NT])
        inv = g.sb(stack, "inv_total", [P, 2 * NT])
        bias = left
        gated = g.sb(stack, "dsa_gated", [P, 2, T])
        wiT = gated[0:IDX_HEADS, 0, :]
        c_kv, c_qi = first, first + 1
        c_ki = c_qi + IDX_HEADS * IDX_DIM // CHUNK
        c_heads = c_ki + 1
        PER = CHUNK // P
        n_tiles = 2 * DSA_HEADS
        n_scores = DSA_HEADS // 2
        n_early = DSA_HEADS + 2
        score_tiles = range(1, NT)
        pairs = [(j, h) for j in score_tiles for h in range(IDX_HEADS)]
        with nc.Block("dsa", no_gpsimd_drain=True) as block:

            @block.tensor
            def _(pe):
                w = g.chunk(pe, c_kv)
                for k in range(KD):
                    ins = g.split_product(ps[:, 0, :], columns(w, k, slice(0, DH)), columns(g.xT, k), k == 0, k == KD - 1)
                ins.then_inc(sem["kT_ready"], add("kT_ready", 1))
                for j in range(NT):
                    for k in range(KD):
                        ins = g.split_product(ps[:, 1, j * DH:(j + 1) * DH], columns(g.xT, k, slice(j * P, (j + 1) * P)), columns(w, k, slice(DH, 2 * DH)), k == 0, k == KD - 1)
                ins.then_inc(sem["v_tok_ready"], add("v_tok_ready", 1))
                g.release("v_tok_ready")
                for i in range(IT):
                    if i % PER == 0:
                        w = g.chunk(pe, c_qi + i // PER)
                    for k in range(KD):
                        ins = g.split_product(ps[:, 2 + i, :], columns(w, k, slice(i % PER * P, (i % PER + 1) * P)), columns(g.xT, k), k == 0, k == KD - 1)
                    ins.then_inc(sem["qi_ready"], add("qi_ready", 1))
                    if i % PER == PER - 1:
                        g.release("qi_ready")
                w = g.chunk(pe, c_ki)
                for k in range(KD):
                    ins = g.split_product(ps[:, 6, :], columns(w, k, slice(0, 2 * IDX_DIM)), columns(g.xT, k), k == 0, k == KD - 1)
                ins.then_inc(sem["ki_ready"], add("ki_ready", 1))
                for k in range(KD):
                    ins = g.split_product(ps[0:IDX_HEADS, 7, :], columns(w, k, slice(2 * IDX_DIM, 2 * IDX_DIM + IDX_HEADS)), columns(g.xT, k), k == 0, k == KD - 1)
                ins.then_inc(sem["wiT_ready"], add("wiT_ready", 1))
                g.release("wiT_ready")

                chunk = [None]

                def project(n):
                    if n % PER == 0:
                        chunk[0] = g.chunk(pe, c_heads + n // PER)
                    w = chunk[0]
                    if n < 2:
                        pe.wait_ge(sem["kiT_ready" if n == 0 else "wi_copied"], past["kiT_ready" if n == 0 else "wi_copied"] + 1)
                    else:
                        b = n - 2
                        done = "q_copied" if b < DSA_HEADS else "z_gated"
                        pe.wait_ge(sem[done], past[done] + b % DSA_HEADS + 1)
                    for k in range(KD):
                        ins = g.split_product(ps[:, 6 + n % 2, :], columns(w, k, slice(n % PER * P, (n % PER + 1) * P)), columns(g.xT, k), k == 0, k == KD - 1)
                    ins.then_inc(sem["head_ready"], add("head_ready", 1))
                    if n % PER == PER - 1:
                        g.release("head_ready")

                project(0)
                pe.wait_ge(sem["wiT_copied"], past["wiT_copied"] + 1)
                for j in range(NT):
                    ins = nc.tensor.transpose(ps[:, 7, j * IDX_HEADS:(j + 1) * IDX_HEADS], wiT[:, j * P:(j + 1) * P], g.ident[0:IDX_HEADS, 0:IDX_HEADS])
                ins.then_inc(sem["wi_ready"], add("wi_ready", 1))
                for n in range(1, 4):
                    project(n)
                pe.wait_ge(sem["qiT_ready"], past["qiT_ready"] + IT)
                pe.wait_ge(sem["kiT_ready"], past["kiT_ready"] + 2)
                for m, (j, h) in enumerate(pairs):
                    if m >= 2:
                        pe.wait_ge(sem["relu"], past["relu"] + m - 1)
                    rows = slice((h % 2) * IDX_DIM, (h % 2 + 1) * IDX_DIM)
                    n = (j + 1) * P
                    g.product(ps[:, m % 2, 0:n], qiT[rows, h // 2, j * P:(j + 1) * P], kiT[rows, 0:n]).then_inc(sem["index_ready"], add("index_ready", 1))
                    if m % 6 == 5 and 4 + m // 6 < n_scores:
                        project(4 + m // 6)
                for n in range(n_scores, n_early):
                    project(n)

                def logits(h):
                    pe.wait_ge(sem["q_rotated"], past["q_rotated"] + h + 1)
                    if h == 0:
                        pe.wait_ge(sem["kT_rotated"], past["kT_rotated"] + 1)
                        pe.wait_ge(sem["relu"], past["relu"] + len(pairs))
                    for j in range(NT):
                        m = NT * h + j
                        if m >= 2:
                            pe.wait_ge(sem["masked"], past["masked"] + m - 1)
                        n = (j + 1) * P
                        g.product(ps[:, m % 2, 0:n], qT[:, h, j * P:(j + 1) * P], kT[:, 0:n]).then_inc(sem["logits_ready"], add("logits_ready", 1))

                logits(0)
                logits(1)
                for h in range(DSA_HEADS):
                    for j in range(NT):
                        m = NT * h + j
                        pe.wait_ge(sem["prob_ready"], past["prob_ready"] + m + 1)
                        if m >= 2:
                            b = m - 2
                            done = "probT_by_dve" if b % 2 else "probT_by_act"
                            pe.wait_ge(sem[done], past[done] + b // 2 + 1)
                        for i in range(j + 1):
                            ins = nc.tensor.transpose(ps[:, 2 + m % 2, i * P:(i + 1) * P], prob[:, h % 2, j, i * P:(i + 1) * P], g.ident[:])
                        ins.then_inc(sem["prob_turned"], add("prob_turned", 1))
                    if n_early + h < n_tiles:
                        project(n_early + h)
                    if h + 2 < DSA_HEADS:
                        logits(h + 2)
                    pe.wait_ge(sem["probT_by_act"], past["probT_by_act"] + 2 * h + 2)
                    pe.wait_ge(sem["probT_by_dve"], past["probT_by_dve"] + 2 * h + 2)
                    if h >= 2:
                        pe.wait_ge(sem["head_done"], past["head_done"] + h - 1)
                    for i in range(NT):
                        ins = g.product(ps[:, 4 + h % 2, i * P:T], v[:, i, :], probT[:, i, i * P:T], i == 0, i == NT - 1, check=False)
                    ins.then_inc(sem["o_head"], add("o_head", 1))

            @block.scalar
            def _(act):
                g.split_high(act, c_kv + RING)
                act.wait_ge(sem["kT_ready"], past["kT_ready"] + 1)
                nc.scalar.activation(kT[:], ps[:, 0, :], ACT.Copy).then_inc(sem["kT_copied"], add("kT_copied", 1))
                act.wait_ge(sem["v_tok_ready"], past["v_tok_ready"] + 1)
                nc.scalar.activation(v[:], ps[:, 1, :].rearrange("p (j d) -> p j d", j=NT), ACT.Copy).then_inc(sem["v_tok_copied"], add("v_tok_copied", 1))
                g.split_high(act, c_kv + 1 + RING)
                for i in range(IT):
                    act.wait_ge(sem["qi_ready"], past["qi_ready"] + i + 1)
                    nc.scalar.activation(qiT[:, i, :], ps[:, 2 + i, :], ACT.Copy).then_inc(sem["qi_copied"], add("qi_copied", 1))
                    if i % PER == PER - 1:
                        g.split_high(act, c_qi + i // PER + 1 + RING)
                act.wait_ge(sem["ki_ready"], past["ki_ready"] + 1)
                nc.scalar.activation(kiT[:], ps[:, 6, :], ACT.Copy).then_inc(sem["kiT_ready"], add("kiT_ready", 1))
                act.wait_ge(sem["wiT_ready"], past["wiT_ready"] + 1)
                nc.scalar.activation(wiT[:], ps[0:IDX_HEADS, 7, :], ACT.Copy).then_inc(sem["wiT_copied"], add("wiT_copied", 1))
                g.split_high(act, c_ki + 1 + RING)
                act.wait_ge(sem["wi_ready"], past["wi_ready"] + 1)
                nc.scalar.activation(wi[:], ps[:, 7, 0:NT * IDX_HEADS].rearrange("p (j h) -> p j h", j=NT), ACT.Copy,
                                                         scale=INDEX_SCALE).then_inc(sem["wi_copied"], add("wi_copied", 1))
                g.split_high(act, c_ki + 1 + RING)

                def project(n):
                    h = n % DSA_HEADS
                    act.wait_ge(sem["head_ready"], past["head_ready"] + n + 1)
                    src = ps[:, 6 + n % 2, :]
                    if n < DSA_HEADS:
                        nc.scalar.activation(qT[:, h, :], src, ACT.Copy).then_inc(sem["q_copied"], add("q_copied", 1))
                    else:
                        nc.scalar.activation(zT[:, h, :], src, ACT.Tanh, scale=0.5).then_inc(sem["z_tanh"], add("z_tanh", 1))
                    if n % PER == PER - 1:
                        g.split_high(act, c_heads + n // PER + 1 + RING)

                for n in range(4):
                    project(n)
                for m, (j, h) in enumerate(pairs):
                    n = (j + 1) * P
                    act.wait_ge(sem["index_ready"], past["index_ready"] + m + 1)
                    if m >= 2:
                        act.wait_ge(sem["summed"], past["summed"] + m - 1)
                    nc.scalar.activation(relu[:, m % 2, 0:n], ps[:, m % 2, 0:n], ACT.Relu).then_inc(sem["relu"], add("relu", 1))
                    if m % 6 == 5 and 4 + m // 6 < n_scores:
                        project(4 + m // 6)
                for n in range(n_scores, n_early):
                    project(n)

                def exps(h):
                    for j in range(NT):
                        m = NT * h + j
                        i = m % (2 * NT)
                        act.wait_ge(sem["peak_shift"], past["peak_shift"] + m + 1)
                        row = prob[:, h % 2, j, 0:(j + 1) * P]
                        nc.scalar.activation(row, row, ACT.Exp, bias=shift[:, i:i + 1], scale=ATTN_SCALE, accum_out=total[:, i:i + 1]).then_inc(sem["exps"], add("exps", 1))

                def high(h):
                    act.wait_ge(sem["head_done"], past["head_done"] + h + 1)
                    nc.scalar.activation(gT[0][:, h, :], gated[:, h % 2, :], ACT.Copy).then_inc(sem["head_high"], add("head_high", 1))

                exps(0)
                exps(1)
                for h in range(DSA_HEADS):
                    for j in range(0, NT, 2):
                        m = NT * h + j
                        act.wait_ge(sem["prob_turned"], past["prob_turned"] + m + 1)
                        if h:
                            act.wait_ge(sem["o_head"], past["o_head"] + h)
                        nc.scalar.activation(probT[:, 0:j + 1, j * P:(j + 1) * P],
                                                                    ps[:, 2 + m % 2, 0:(j + 1) * P].rearrange("p (i t) -> p i t", t=P), ACT.Copy).then_inc(sem["probT_by_act"], add("probT_by_act", 1))
                    if n_early + h < n_tiles:
                        project(n_early + h)
                    if h + 2 < DSA_HEADS:
                        exps(h + 2)
                    if h:
                        high(h - 1)
                high(DSA_HEADS - 1)

            @block.vector
            def _(dve):
                done_of = ["kT_rotated", "kiT_ready"] + ["qiT_ready"] * IT + ["q_rotated"] * DSA_HEADS
                swaps = [0]

                def swap(x, rows, mask):
                    n = swaps[0]
                    swaps[0] += 1
                    if n >= 2:
                        name = done_of[n - 2]
                        turns = done_of[:n - 1].count(name) + (name == "kiT_ready")
                        dve.wait_ge(sem[name], past[name] + turns)
                    nc.vector.stream_shuffle(rot[0:rows, n % 2, :], x, mask).then_inc(sem["swapped"], add("swapped", 1))

                R = 2 * HALF
                nc.vector.tensor_scalar(bias[:, 0, 0:P], g.after[:], MASKED, None, ALU.mult).then_inc(sem["causal_bias"], add("causal_bias", 1))
                dve.wait_ge(sem["kT_copied"], past["kT_copied"] + 1)
                swap(kT[0:R, :], R, SWAP_HEAD)
                dve.wait_ge(sem["kiT_ready"], past["kiT_ready"] + 1)
                swap(kiT[:], P, SWAP_IDX)
                for i in range(IT):
                    dve.wait_ge(sem["qi_copied"], past["qi_copied"] + i + 1)
                    swap(qiT[:, i, :], P, SWAP_IDX)

                def swap_query(h):
                    dve.wait_ge(sem["q_copied"], past["q_copied"] + h + 1)
                    swap(qT[0:R, h, :], R, SWAP_HEAD)

                def project(n):
                    h = n - DSA_HEADS
                    dve.wait_ge(sem["z_tanh"], past["z_tanh"] + h + 1)
                    nc.vector.scalar_tensor_tensor(out=zT[:, h, :], in0=zT[:, h, :], scalar=1.0, in1=ps[:, 6 + n % 2, :],
                                                   op0=ALU.add, op1=ALU.mult).then_inc(sem["z_gated"], add("z_gated", 1))

                for n in range(4):
                    swap_query(n)
                dve.wait_ge(sem["wi_copied"], past["wi_copied"] + 1)
                for m, (j, h) in enumerate(pairs):
                    n = (j + 1) * P
                    dve.wait_ge(sem["relu"], past["relu"] + m + 1)
                    r, w, s = relu[:, m % 2, 0:n], wi[:, j, h:h + 1], score[:, j, 0:n]
                    if h == 0:
                        ins = nc.vector.tensor_scalar(s, r, w, None, ALU.mult)
                    else:
                        dve.wait_ge(sem["summed"], past["summed"] + m)
                        ins = nc.vector.scalar_tensor_tensor(out=s, in0=r, scalar=w, in1=s, op0=ALU.mult, op1=ALU.add)
                    ins.then_inc(sem["summed"], add("summed", 1))
                    if m % 6 == 5 and 4 + m // 6 < n_scores:
                        swap_query(4 + m // 6)
                dve.wait_ge(sem["summed"], past["summed"] + len(pairs))
                step = "top_step"

                def then(ins):
                    ins.then_inc(sem[step], add(step, 1))
                    dve.wait_ge(sem[step], count[step])

                for j in score_tiles:
                    then(nc.vector.tensor_tensor(score[:, j, j * P:(j + 1) * P], score[:, j, j * P:(j + 1) * P], bias[:, 0, 0:P], ALU.add))
                    n = (j + 1) * P
                    for r in range(TOPK // 8):
                        src = (left if r else score)[:, j, 0:n]
                        then(nc.vector.max(top8[:], src))
                        then(nc.vector.match_replace(left[:, j, 0:n], top8[:], src, TAKEN))
                    then(nc.vector.tensor_tensor(left[:, j, 0:n], left[:, j, 0:n], score[:, j, 0:n], ALU.is_equal))
                    then(nc.vector.tensor_scalar(bias[:, j, 0:n], left[:, j, 0:n], MASKED, None, ALU.mult))

                def mask(h):
                    for j in range(NT):
                        m = NT * h + j
                        i = m % (2 * NT)
                        n = (j + 1) * P
                        dve.wait_ge(sem["logits_ready"], past["logits_ready"] + m + 1)
                        if h >= 2:
                            dve.wait_ge(sem["prob_turned"], past["prob_turned"] + m - 2 * NT + 1)
                        nc.vector.tensor_tensor_reduce(out=prob[:, h % 2, j, 0:n], in0=ps[:, m % 2, 0:n], in1=bias[:, j, 0:n],
                                                                        scale=1.0, scalar=TAKEN, op0=ALU.add, op1=ALU.max, accum_out=peak[:, i:i + 1]).then_inc(sem["masked"], add("masked", 1))
                        dve.wait_ge(sem["masked"], past["masked"] + m + 1)
                        nc.vector.tensor_scalar(shift[:, i:i + 1], peak[:, i:i + 1], -ATTN_SCALE, None, ALU.mult).then_inc(sem["peak_shift"], add("peak_shift", 1))

                def normalise(h):
                    for j in range(NT):
                        m = NT * h + j
                        i = m % (2 * NT)
                        dve.wait_ge(sem["exps"], past["exps"] + m + 1)
                        nc.vector.reciprocal(inv[:, i:i + 1], total[:, i:i + 1]).then_inc(sem["inv_total"], add("inv_total", 1))
                    for j in range(NT):
                        m = NT * h + j
                        i = m % (2 * NT)
                        dve.wait_ge(sem["inv_total"], past["inv_total"] + m + 1)
                        row = prob[:, h % 2, j, 0:(j + 1) * P]
                        nc.vector.tensor_scalar(row, row, inv[:, i:i + 1], None, ALU.mult).then_inc(sem["prob_ready"], add("prob_ready", 1))

                for n in range(DSA_HEADS, n_early):
                    project(n)
                for h in range(2):
                    mask(h)
                    normalise(h)
                for h in range(DSA_HEADS):
                    for j in range(1, NT, 2):
                        m = NT * h + j
                        dve.wait_ge(sem["prob_turned"], past["prob_turned"] + m + 1)
                        if h:
                            dve.wait_ge(sem["o_head"], past["o_head"] + h)
                        nc.vector.tensor_copy(probT[:, 0:j + 1, j * P:(j + 1) * P],
                                                                     ps[:, 2 + m % 2, 0:(j + 1) * P].rearrange("p (i t) -> p i t", t=P)).then_inc(sem["probT_by_dve"], add("probT_by_dve", 1))
                    if h + 2 < DSA_HEADS:
                        mask(h + 2)
                    if n_scores + h < DSA_HEADS:
                        swap_query(n_scores + h)
                    if n_early + h < n_tiles:
                        project(n_early + h)
                    if h + 2 < DSA_HEADS:
                        normalise(h + 2)
                    dve.wait_ge(sem["o_head"], past["o_head"] + h + 1)
                    if h >= 2:
                        dve.wait_ge(sem["head_low"], past["head_low"] + h - 1)
                    nc.vector.scalar_tensor_tensor(out=gated[:, h % 2, :], in0=ps[:, 4 + h % 2, :], scalar=0.5, in1=zT[:, h, :],
                                                                       op0=ALU.mult, op1=ALU.mult).then_inc(sem["head_done"], add("head_done", 1))
                dve.wait_ge(sem["head_low"], past["head_low"] + DSA_HEADS)

            @block.gpsimd
            def _(pool):
                def rotate(x, slot, cos, sin, done):
                    nc.gpsimd.tensor_tensor(x, x, cos, ALU.mult).then_inc(sem["rope_parts"], add("rope_parts", 1))
                    nc.gpsimd.tensor_tensor(slot, slot, sin, ALU.mult).then_inc(sem["rope_parts"], add("rope_parts", 1))
                    pool.wait_ge(sem["rope_parts"], count["rope_parts"])
                    nc.gpsimd.tensor_tensor(x, x, slot, ALU.add).then_inc(sem[done], add(done, 1))
                    pool.wait_ge(sem[done], count[done])

                def low(h):
                    pool.wait_ge(sem["head_high"], past["head_high"] + h + 1)
                    nc.gpsimd.tensor_tensor(gT[1][:, h, :], gated[:, h % 2, :], gT[0][:, h, :].bitcast(F32), ALU.subtract).then_inc(sem["head_low"], add("head_low", 1))

                R = 2 * HALF
                turns = [0]

                def turn(x, rows, done):
                    n = turns[0]
                    turns[0] += 1
                    pool.wait_ge(sem["swapped"], past["swapped"] + n + 1)
                    cos, sin = (g.head_cos, g.head_sin) if rows == R else (g.idx_cos, g.idx_sin)
                    rotate(x, rot[0:rows, n % 2, :], cos[:], sin[:], done)

                def project(n):
                    if n % PER == PER - 1:
                        g.split_low(pool, c_heads + n // PER + 1 + RING)

                def turn_query(h):
                    turn(qT[0:R, h, :], R, "q_rotated")

                g.split_low(pool, c_ki)
                turn(kT[0:R, :], R, "kT_rotated")
                g.split_low(pool, c_heads)
                turn(kiT[:], P, "kiT_ready")
                g.split_low(pool, c_heads + RING)
                for i in range(IT):
                    turn(qiT[:, i, :], P, "qiT_ready")
                for n in range(n_early):
                    project(n)
                    if n < n_scores:
                        turn_query(n)
                for h in range(DSA_HEADS):
                    if n_early + h < n_tiles:
                        project(n_early + h)
                    if n_scores + h < DSA_HEADS:
                        turn_query(n_scores + h)
                    low(h)
                g.split_low(pool)

            @block.sync
            def _(sp):
                g.load_chunks(sp)
    g.sem.end_phase()

GH, HD = 4, 64
GW = GH * HD
N_MEM = 256
MT = N_MEM // P
CONV_K = 4
RANK2 = 16
HEAD_SCALE = HD ** -0.5
DECAY_SCALE = float(np.exp(np.float32(-0.5)))
A0, B0 = 0, 3 * GW
C0 = B0 + 4 * GW + GH
D0 = C0 + 5 * GW + 2 * GH
M0 = D0 + 4 * GW + 2 * RANK2
IN2 = M0 + 2 * GW
GATES = 3 * GH
MIX_TILES = 5 * GW // P
SECOND_CHUNKS = {"uA": [(A0, A0 + GW)], "vA": [(A0 + GW, A0 + 2 * GW)], "zA": [(A0 + 2 * GW, B0)],
                 "qB": [(B0, B0 + GW)], "kB": [(B0 + GW, B0 + 2 * GW)], "vB": [(B0 + 2 * GW, B0 + 3 * GW)],
                 "small": [(B0 + 3 * GW, B0 + 3 * GW + GH), (C0 + 3 * GW + GH, C0 + 3 * GW + 2 * GH), (C0 + 3 * GW, C0 + 3 * GW + GH),
                           (D0 + GW, D0 + GW + RANK2), (D0 + 3 * GW + RANK2, D0 + 3 * GW + 2 * RANK2)],
                 "zB": [(B0 + 3 * GW + GH, C0)],
                 "qC": [(C0, C0 + GW)], "kC": [(C0 + GW, C0 + 2 * GW)], "vC": [(C0 + 2 * GW, C0 + 3 * GW)],
                 "oC": [(C0 + 3 * GW + 2 * GH, C0 + 4 * GW + 2 * GH)], "zC": [(C0 + 4 * GW + 2 * GH, D0)],
                 "rD": [(D0, D0 + GW)], "kD": [(D0 + GW + RANK2, D0 + 2 * GW + RANK2)], "vD": [(D0 + 2 * GW + RANK2, D0 + 3 * GW + RANK2)],
                 "zD": [(D0 + 3 * GW + 2 * RANK2, M0)], "qM": [(M0, M0 + GW)], "zM": [(M0 + GW, IN2)]}


def phase_project(g, s, first):
    nc, t, ps = g.nc, g.t, g.ps
    sem, past, count, add = g.sem, g.sem.past, g.sem.count, g.sem.add
    w2 = {name: i for i, name in enumerate(SECOND_CHUNKS)}
    c_in = first
    end = first + len(w2)
    tiles = []

    def tok(c, col, width, engine, what):
        tiles.extend((w2[c], col, width, j, engine, what) for j in range(NT))

    def fm(c, col, n, engine, what, width=P):
        tiles.extend((w2[c], col + i * width, width, None, engine, (what, i)) for i in range(n))

    tok("uA", 0, GW, "act", "u")
    tok("vA", 0, GW, "act", "v")
    fm("zA", 0, 2, "act", "zA")
    for name in ("qB", "kB", "vB"):
        tok(name, 0, GW, "dve", name)
    fm("small", 0, 1, "dve", "gates", GATES)
    fm("small", GATES, 1, "dve", "wlo", RANK2)
    fm("small", GATES + RANK2, 1, "dve", "alo", RANK2)
    tiles.append((w2["small"], 0, 0, None, "dve", ("gates_turned", 0)))
    fm("zB", 0, 2, "act", "zB")
    fm("qC", 0, 2, "dve", "qC")
    fm("kC", 0, 2, "dve", "kC")
    tok("vC", 0, GW, "dve", "vC")
    tok("oC", 0, GW, "act", "oC")
    fm("zC", 0, 2, "act", "zC")
    for name in ("rD", "kD", "vD", "zD"):
        fm(name, 0, 2, "dve", name)
    tok("qM", 0, GW, "dve", "qM")
    fm("zM", 0, 2, "act", "zM")
    nth = []
    for i, tile in enumerate(tiles):
        nth.append(sum(x[4] == tile[4] for x in tiles[:i + 1]))
    NB = 6
    with ExitStack() as stack:
        per = D // T
        mem = s.mixT[:, 0:MT * per, :].rearrange("p (j k) n -> p j (k n)", j=MT)
        memT = s.mixT[:, 2 * MT:4 * MT, :].rearrange("p a (b n) -> p (a b) n", n=N_MEM)
        msq = s.mixT[:, 4 * MT:4 * MT + per, :].rearrange("p a n -> p (a n)")
        gatesT = msq[0:GATES, 0:T]
        mss = g.sb(stack, "mss", [P, MT])
        with nc.Block("project", no_gpsimd_drain=True) as block:

            @block.tensor
            def _(pe):
                for i, (c, col, width, j, engine, what) in enumerate(tiles):
                    if i == 0 or c != tiles[i - 1][0]:
                        w = g.chunk(pe, c_in + c)
                    if i >= NB:
                        pe.wait_ge(sem["projected_by_" + tiles[i - NB][4]], past["projected_by_" + tiles[i - NB][4]] + nth[i - NB])
                    if what[0] == "gates_turned":
                        pe.wait_ge(sem["projected_by_dve"], past["projected_by_dve"] + nth[i - 3])
                        for j in range(NT):
                            ins = nc.tensor.transpose(ps[:, i % NB, j * GATES:(j + 1) * GATES], gatesT[:, j * P:(j + 1) * P], g.ident[0:GATES, 0:GATES])
                    for k in range(KD if width else 0):
                        if j is None:
                            ins = g.split_product(ps[0:width, i % NB, :], columns(w, k, slice(col, col + width)), columns(g.xT, k), k == 0, k == KD - 1)
                        else:
                            ins = g.split_product(ps[:, i % NB, 0:width], columns(g.xT, k, slice(j * P, (j + 1) * P)), columns(w, k, slice(col, col + width)), k == 0, k == KD - 1)
                    ins.then_inc(sem["projected"], add("projected", 1))
                    if i + 1 == len(tiles) or tiles[i + 1][0] != c:
                        g.release("projected")
                pe.wait_ge(sem["mem_scaled"], past["mem_scaled"] + MT)
                to_feature_major_pe(g, pe, (0, 0), mem, KD, MT, [6, 7])
                pe.wait_ge(sem["turned_by_act"], past["turned_by_act"] + KD // 2)
                pe.wait_ge(sem["turned_by_dve"], past["turned_by_dve"] + KD // 2)
                for half in range(2):
                    w = g.chunk(pe, end + half)
                    done = "mem_kv" if half else "mem_k"
                    for j in range(MT):
                        for k in range(KD):
                            ins = g.product(ps[:, 6 + j, half * GW:(half + 1) * GW], memT[:, k, j * P:(j + 1) * P], w[:, k, :], k == 0, k == KD - 1)
                        ins.then_inc(sem[done], add(done, 1))
                    g.release(done)

            @block.scalar
            def _(act):
                act.dma_start(mem[:], t["mem_2"][0].rearrange("(j p) d -> p j d", p=P)).then_inc(sem["mem_landed"], add("mem_landed", 16))
                act.dma_start(s.w_sgu[:], t["sgu_w_2"][0].rearrange("g t s -> t g s")).then_inc(sem["w_sgu_landed"], add("w_sgu_landed", 16))
                rows = ((s.gains[:, 0, :].rearrange("p (h d) -> p h d", h=1), t["sgu_norm_g_2"]),
                        (s.gains[:, 1, :].rearrange("p (h d) -> p h d", h=GH), t["fox_q_g_2"]),
                        (s.gains[:, 2, :].rearrange("p (h d) -> p h d", h=GH), t["fox_k_g_2"]),
                        (s.gains[:, 3, :].rearrange("p (h d) -> p h d", h=GH), t["mem_q_g_2"]),
                        (s.gains[:, 4, :].rearrange("p (h d) -> p h d", h=GH), t["mem_k_g_2"]),
                        (s.gains[:, 5, :].rearrange("p (h d) -> p h d", h=1), t["mlstm_out_g_2"]),
                        (s.gains[:, 6, :].rearrange("p (h d) -> p h d", h=1), t["rwkv_ln_g_2"]))
                for dst, v in rows:
                    for h in range(dst.shape[1]):
                        act.dma_start(dst[:, h, :], v.to_broadcast([P, dst.shape[2]])).then_inc(sem["gains_landed"], add("gains_landed", 16))
                for i, name in enumerate(("fox_f_b_2", "mlstm_f_b_2", "mlstm_i_b_2")):
                    act.dma_start(s.gate_bias[:, i * GH:(i + 1) * GH], t[name].to_broadcast([P, GH])).then_inc(sem["gate_bias_landed"], add("gate_bias_landed", 16))
                act.dma_start(s.w2_decay[:], t["rwkv_w2_2"][0]).then_inc(sem["low_rank_landed"], add("low_rank_landed", 16))
                act.dma_start(s.w2_a[:], t["rwkv_a2_2"][0]).then_inc(sem["low_rank_landed"], add("low_rank_landed", 16))
                act.wait_ge(sem["mem_landed"], past["mem_landed"] + 16)
                for j in range(MT):
                    if j:
                        act.wait_ge(sem["mem_squared"], past["mem_squared"] + j)
                    nc.scalar.activation(msq[:], mem[:, j, :], ACT.Square, accum_out=mss[:, j:j + 1]).then_inc(sem["mem_squared"], add("mem_squared", 1))
                act.wait_ge(sem["mem_mean_sq"], past["mem_mean_sq"] + 1)
                nc.scalar.activation(mss[:], mss[:], ACT.Sqrt).then_inc(sem["mem_root"], add("mem_root", 1))
                act.wait_ge(sem["mem_rstd"], past["mem_rstd"] + 1)
                for j in range(MT):
                    nc.scalar.activation(mem[:, j, :], mem[:, j, :], ACT.Copy, scale=mss[:, j:j + 1]).then_inc(sem["mem_scaled"], add("mem_scaled", 1))
                g.split_high(act, c_in + RING)
                last = 0
                for i, (c, col, width, j, engine, what) in enumerate(tiles):
                    if c != last:
                        g.split_high(act, c_in + c + RING)
                        last = c
                    if engine != "act":
                        continue
                    src = ps[:, i % NB, :]
                    act.wait_ge(sem["projected"], past["projected"] + i + 1)
                    if what in ("u", "v"):
                        ins = nc.scalar.activation(s.heads[:, j, int(what == "v"), :], src[:, 0:GW], ACT.Gelu_apprx_tanh)
                    elif what == "oC":
                        ins = nc.scalar.activation(s.o_sig[:, j, :], src[:, 0:GW], ACT.Sigmoid)
                    else:
                        tile = {"zA": 0, "zB": 2, "zC": 4, "zM": 6}[what[0]] + what[1]
                        ins = nc.scalar.activation(s.zT[:, tile, :], src, ACT.Silu)
                    ins.then_inc(sem["projected_by_act"], add("projected_by_act", 1))
                to_feature_major_act(g, act, 0, memT, KD, N_MEM, [6, 7], scale=g.col("mem_norm_g_2"))
                for j in range(MT):
                    act.wait_ge(sem["mem_kv"], past["mem_kv"] + j + 1)
                    nc.scalar.activation(s.mem_kv[:, j, :], ps[:, 6 + j, :], ACT.Copy).then_inc(sem["mem_kv_copied"], add("mem_kv_copied", 1))

            @block.vector
            def _(dve):
                nc.vector.memset(s.conv_in[:, :, 0:CONV_K - 1], 0.0).then_inc(sem["pads"], add("pads", 1))
                nc.vector.memset(s.raw[:, :, 0:1], 0.0).then_inc(sem["pads"], add("pads", 1))
                nc.vector.memset(s.low[:, :, 0:1], 0.0).then_inc(sem["pads"], add("pads", 1))
                nc.vector.memset(s.vC[:, :, :, HD:HD + 1], 1.0).then_inc(sem["pads"], add("pads", 1))
                dve.wait_ge(sem["mem_squared"], past["mem_squared"] + MT)
                nc.vector.tensor_scalar(mss[:], mss[:], 1.0 / D, RMS_EPS, ALU.mult, ALU.add).then_inc(sem["mem_mean_sq"], add("mem_mean_sq", 1))
                dve.wait_ge(sem["mem_root"], past["mem_root"] + 1)
                nc.vector.reciprocal(mss[:], mss[:]).then_inc(sem["mem_rstd"], add("mem_rstd", 1))
                dve.wait_ge(sem["gate_bias_landed"], past["gate_bias_landed"] + 48)
                for i, (c, col, width, j, engine, what) in enumerate(tiles):
                    if engine != "dve":
                        continue
                    src = ps[:, i % NB, :]
                    dve.wait_ge(sem["projected"], past["projected"] + i + 1)
                    done = "projected_by_dve"
                    part = "projected_part"
                    if what == "qB":
                        nc.vector.tensor_copy(s.heads[:, j, 2, :], src[:, 0:GW]).then_inc(sem[done], add(done, 1))
                    elif what == "kB":
                        nc.vector.tensor_copy(s.heads[:, j, 3, :], src[:, 0:GW]).then_inc(sem[done], add(done, 1))
                    elif what == "vB":
                        nc.vector.tensor_copy(s.vB[:, j, :], src[:, 0:GW]).then_inc(sem[done], add(done, 1))
                    elif what[0] == "gates":
                        nc.vector.tensor_copy(gatesT, src[0:GATES, :]).then_inc(sem[done], add(done, 1))
                    elif what[0] == "gates_turned":
                        nc.vector.tensor_tensor(s.gates[:], src[:, 0:NT * GATES].rearrange("p (j a) -> p j a", j=NT),
                                                s.gate_bias[:].unsqueeze(1).to_broadcast([P, NT, GATES]), ALU.add).then_inc(sem[done], add(done, 1))
                    elif what == "vC":
                        nc.vector.tensor_copy(s.vC[:, j, :, 0:HD], src[:, 0:GW].rearrange("p (h d) -> p h d", h=GH)).then_inc(sem[done], add(done, 1))
                    elif what == "qM":
                        nc.vector.tensor_copy(s.heads[:, j, 4, :], src[:, 0:GW]).then_inc(sem[done], add(done, 1))
                    elif what[0] in ("qC", "kC"):
                        nc.vector.tensor_copy(s.conv_in[:, 2 * int(what[0] == "kC") + what[1], CONV_K - 1:], src).then_inc(sem[done], add(done, 1))
                    elif what[0] in ("wlo", "alo"):
                        nc.vector.tensor_copy(s.low[:, int(what[0] == "alo"), 1:], src[0:RANK2, :]).then_inc(sem[done], add(done, 1))
                    else:
                        tile = {"rD": 0, "kD": 2, "vD": 4, "zD": 6}[what[0]] + what[1]
                        nc.vector.tensor_copy(s.raw[:, tile, 1:], src).then_inc(sem[done], add(done, 1))
                to_feature_major_dve(g, dve, 0, memT, KD, N_MEM, [6, 7], scale=g.col("mem_norm_g_2"))
                dve.wait_ge(sem["gains_landed"], count["gains_landed"])
                dve.wait_ge(sem["low_rank_landed"], past["low_rank_landed"] + 32)
                dve.wait_ge(sem["w_sgu_landed"], past["w_sgu_landed"] + 16)

            @block.gpsimd
            def _(pool):
                g.split_low(pool)

            @block.sync
            def _(sp):
                g.load_chunks(sp)
    g.sem.end_phase()


def phase_heads(g, s):
    nc, t, ps = g.nc, g.t, g.ps
    sem, past, count, add = g.sem, g.sem.past, g.sem.count, g.sem.add
    with ExitStack() as stack:
        sq = s.mixT[:, 0:2 * NT, :].rearrange("p (j a) (b d) -> p j (a b) d", j=NT, d=GW)
        ksq = s.mixT[:, 2 * NT, :].rearrange("p (j d) -> p j d", j=MT)
        NG = 4 * GH
        ss = g.sb(stack, "head_ss", [P, NT * NG + MT * GH])
        la = g.sb(stack, "log_abs", [P, NT, 2 * GH])
        lg = g.sb(stack, "log_gates", [P, NT, 2 * GH])
        conv = g.room[:, 0, 0:2, :]
        n_main = NT * NG
        x = s.heads[:, :, 1:5, :]
        k_mem = s.mem_kv[:, :, 0:GW]
        with nc.Block("heads", no_gpsimd_drain=True) as block:

            @block.scalar
            def _(act):
                nc.scalar.activation(la[:], s.gates[:, :, 0:2 * GH], ACT.Abs).then_inc(sem["gate_abs"], add("gate_abs", 1))
                act.wait_ge(sem["gate_abs"], past["gate_abs"] + 1)
                nc.scalar.activation(la[:], la[:], ACT.Exp, scale=-1.0).then_inc(sem["gate_exp"], add("gate_exp", 1))
                act.wait_ge(sem["gate_exp"], past["gate_exp"] + 1)
                nc.scalar.activation(la[:], la[:], ACT.Ln, bias=1.0).then_inc(sem["gate_ln"], add("gate_ln", 1))
                for j in range(NT):
                    nc.scalar.activation(sq[:, j], x[:, j], ACT.Square).then_inc(sem["head_squared"], add("head_squared", 1))
                nc.scalar.activation(ksq[:], k_mem, ACT.Square).then_inc(sem["head_squared"], add("head_squared", 1))
                act.wait_ge(sem["head_mean_sq"], past["head_mean_sq"] + 1)
                nc.scalar.activation(ss[:], ss[:], ACT.Sqrt).then_inc(sem["head_root"], add("head_root", 1))
                for i in range(4):
                    act.wait_ge(sem["convolved"], past["convolved"] + CONV_K * (i + 1))
                    nc.scalar.activation(s.qkT[:, i, :], conv[:, i % 2, :], ACT.Silu, bias=g.col("conv_b")[:, i:i + 1]).then_inc(sem["conv_silu"], add("conv_silu", 1))

            @block.tensor
            def _(pe):
                pe.wait_ge(sem["log_gates"], past["log_gates"] + 1)
                for j in range(NT):
                    for i in range(j + 1):
                        ins = g.product(ps[:, 0, j * 2 * GH:(j + 1) * 2 * GH], (g.ones if i < j else g.not_before)[:], lg[:, i, :], i == 0, i == j, check=False)
                ins.then_inc(sem["cum_ready"], add("cum_ready", 1))
                for h in range(GH):
                    ins = nc.tensor.transpose(ps[:, 1, h * P:(h + 1) * P], s.w_sgu[:, h, :], g.ident[:])
                ins.then_inc(sem["w_sgu_turned"], add("w_sgu_turned", 1))

            @block.vector
            def _(dve):
                dve.wait_ge(sem["gate_ln"], past["gate_ln"] + 1)
                nc.vector.scalar_tensor_tensor(out=lg[:], in0=s.gates[:, :, 0:2 * GH], scalar=0.0, in1=la[:],
                                                                   op0=ALU.min, op1=ALU.subtract).then_inc(sem["log_gates"], add("log_gates", 1))
                for j in range(NT):
                    dve.wait_ge(sem["head_squared"], past["head_squared"] + j + 1)
                    nc.vector.tensor_reduce(ss[:, j * NG:(j + 1) * NG], sq[:, j].rearrange("p a (h d) -> p (a h) d", d=HD), AX, ALU.add).then_inc(sem["head_sums"], add("head_sums", 1))
                dve.wait_ge(sem["head_squared"], past["head_squared"] + NT + 1)
                nc.vector.tensor_reduce(ss[:, n_main:], ksq[:].rearrange("p j (h d) -> p (j h) d", d=HD), AX, ALU.add).then_inc(sem["head_sums"], add("head_sums", 1))
                dve.wait_ge(sem["head_sums"], past["head_sums"] + NT + 1)
                nc.vector.tensor_scalar(ss[:], ss[:], 1.0 / HD, RMS_EPS, ALU.mult, ALU.add).then_inc(sem["head_mean_sq"], add("head_mean_sq", 1))
                dve.wait_ge(sem["head_root"], past["head_root"] + 1)
                nc.vector.reciprocal(ss[:], ss[:]).then_inc(sem["head_rstd"], add("head_rstd", 1))
                dve.wait_ge(sem["head_rstd"], past["head_rstd"] + 1)
                for j in range(NT):
                    y = x[:, j].rearrange("p a (h d) -> p (a h) d", d=HD)
                    nc.vector.tensor_tensor(y, y, ss[:, j * NG:(j + 1) * NG].unsqueeze(2).to_broadcast([P, NG, HD]), ALU.mult).then_inc(sem["head_scaled"], add("head_scaled", 1))
                y = k_mem.rearrange("p j (h d) -> p j h d", d=HD)
                for j in range(MT):
                    nc.vector.tensor_tensor(y[:, j], y[:, j], ss[:, n_main + j * GH:n_main + (j + 1) * GH].unsqueeze(2).to_broadcast([P, GH, HD]), ALU.mult).then_inc(sem["head_scaled"], add("head_scaled", 1))
                for j in range(NT):
                    dve.wait_ge(sem["head_scaled"], past["head_scaled"] + j + 1)
                    nc.vector.tensor_tensor(x[:, j], x[:, j], s.gains[:, 0:4, :], ALU.mult).then_inc(sem["head_gained"], add("head_gained", 1))
                for j in range(MT):
                    dve.wait_ge(sem["head_scaled"], past["head_scaled"] + NT + j + 1)
                    nc.vector.tensor_tensor(k_mem[:, j, :], k_mem[:, j, :], s.gains[:, 4, :], ALU.mult).then_inc(sem["head_gained"], add("head_gained", 1))
                dve.wait_ge(sem["w_sgu_turned"], past["w_sgu_turned"] + 1)
                nc.vector.tensor_tensor(s.w_sguT[:], ps[:, 1, :].rearrange("p (h t) -> p h t", h=GH),
                                                               g.not_before[:].unsqueeze(1).to_broadcast([P, GH, P]), ALU.mult).then_inc(sem["w_sgu_masked"], add("w_sgu_masked", 1))
                dve.wait_ge(sem["cum_ready"], past["cum_ready"] + 1)
                nc.vector.tensor_copy(s.cum[:], ps[:, 0, 0:NT * 2 * GH].rearrange("p (j h) -> p j h", j=NT)).then_inc(sem["cum_copied"], add("cum_copied", 1))
                taps = g.col("conv_w")
                for i in range(4):
                    if i >= 2:
                        dve.wait_ge(sem["conv_silu"], past["conv_silu"] + i - 1)
                    for a in range(CONV_K):
                        src = s.conv_in[:, i, a:a + T]
                        w = taps[:, a * 4 + i:a * 4 + i + 1]
                        if a == 0:
                            ins = nc.vector.tensor_scalar(conv[:, i % 2, :], src, w, None, ALU.mult)
                        else:
                            dve.wait_ge(sem["convolved"], past["convolved"] + CONV_K * i + a)
                            ins = nc.vector.scalar_tensor_tensor(out=conv[:, i % 2, :], in0=src, scalar=w, in1=conv[:, i % 2, :], op0=ALU.mult, op1=ALU.add)
                        ins.then_inc(sem["convolved"], add("convolved", 1))
                q, k = s.fox_qk[:, :, 0], s.fox_qk[:, :, 1]
                dve.wait_ge(sem["head_gained"], past["head_gained"] + NT)
                dve.wait_ge(sem["cum_copied"], past["cum_copied"] + 1)
                for j in range(NT):
                    f = s.cum[:, j, 0:GH].unsqueeze(2)
                    nc.vector.tensor_scalar(q[:, j, :, 0:HD], s.heads[:, j, 2, :].rearrange("p (h d) -> p h d", h=GH), HEAD_SCALE, None, ALU.mult).then_inc(sem["fox_parts"], add("fox_parts", 1))
                    nc.vector.tensor_copy(k[:, j, :, 0:HD], s.heads[:, j, 3, :].rearrange("p (h d) -> p h d", h=GH)).then_inc(sem["fox_parts"], add("fox_parts", 1))
                    nc.vector.tensor_copy(q[:, j, :, HD:HD + 1], f).then_inc(sem["fox_parts"], add("fox_parts", 1))
                    nc.vector.tensor_scalar(k[:, j, :, HD + 1:HD + 2], f, -1.0, None, ALU.mult).then_inc(sem["fox_parts"], add("fox_parts", 1))
                    nc.vector.memset(q[:, j, :, HD + 1:HD + 2], 1.0).then_inc(sem["fox_parts"], add("fox_parts", 1))
                    nc.vector.memset(k[:, j, :, HD:HD + 1], 1.0).then_inc(sem["fox_parts"], add("fox_parts", 1))
                for i in range(2, 4):
                    dve.wait_ge(sem["conv_silu"], past["conv_silu"] + i + 1)
                    nc.vector.tensor_scalar(s.qkT[:, i, :], s.qkT[:, i, :], HEAD_SCALE, None, ALU.mult).then_inc(sem["k_scaled"], add("k_scaled", 1))
                nc.vector.tensor_tensor(s.a_tok[:], s.gates[:, :, 2 * GH:3 * GH], s.cum[:, :, GH:2 * GH], ALU.subtract).then_inc(sem["a_made"], add("a_made", 1))

            @block.sync
            def _(sp):
                g.load_chunks(sp)
    g.sem.end_phase()


def phase_sgu(g, s):
    nc, t, ps = g.nc, g.t, g.ps
    sem, past, count, add = g.sem, g.sem.past, g.sem.count, g.sem.add
    with nc.Block("sgu", no_gpsimd_drain=True) as block:

        @block.tensor
        def _(pe):
            for j in range(NT):
                for h in range(GH):
                    ins = g.product(ps[:, j // 2, (j % 2) * GW + h * HD:(j % 2) * GW + (h + 1) * HD], s.w_sguT[:, h, :], s.heads[:, j, 1, h * HD:(h + 1) * HD])
            ins.then_inc(sem["sgu_mixed"], add("sgu_mixed", 1))
            pe.wait_ge(sem["sgu_y"], past["sgu_y"] + GH)
            to_gated(g, pe, s.heads[:, :, 0, :], [2, 3])

        @block.vector
        def _(dve):
            dve.wait_ge(sem["sgu_mixed"], past["sgu_mixed"] + 1)
            for h in range(GH):
                u = s.heads[:, :, 0, h * HD:(h + 1) * HD]
                m = ps[:, 0:2, :].rearrange("p b (j d) -> p (b j) d", j=2)[:, :, h * HD:(h + 1) * HD]
                nc.vector.scalar_tensor_tensor(out=u, in0=m, scalar=g.col("sgu_b")[:, h:h + 1], in1=u, op0=ALU.add, op1=ALU.mult).then_inc(sem["sgu_y"], add("sgu_y", 1))
            gate_turned(g, dve, s, 0, 0, [2, 3])

        @block.sync
        def _(sp):
            g.load_chunks(sp)
    g.sem.end_phase()


def to_gated(g, pe, y, banks):
    sem, add = g.sem, g.sem.add
    for i in range(2):
        for j in range(NT):
            ins = g.nc.tensor.transpose(g.ps[:, banks[i], j * P:(j + 1) * P], y[:, j, i * P:(i + 1) * P], g.ident[:])
        ins.then_inc(sem["y_turned"], add("y_turned", 1))


def gate_turned(g, dve, s, mix_tile, z_tile, banks):
    sem, past, add = g.sem, g.sem.past, g.sem.add
    for i in range(2):
        dve.wait_ge(sem["y_turned"], past["y_turned"] + i + 1)
        g.nc.vector.tensor_tensor(s.mixT[:, mix_tile + i, :], g.ps[:, banks[i], :], s.zT[:, z_tile + i, :], ALU.mult).then_inc(sem["y_gated"], add("y_gated", 1))


def phase_fox(g, s):
    nc, t, ps = g.nc, g.t, g.ps
    sem, past, count, add = g.sem, g.sem.past, g.sem.count, g.sem.add
    K = HD + 2
    with ExitStack() as stack:
        prob = g.room[:, 0].rearrange("p (b j) n -> p b j n", b=2)
        probT = g.room[:, 1, 0:NT]
        qT, kT = g.room[0:K, 1, NT:NT + GH], g.room[0:K, 2, 0:GH]
        bias = g.sb(stack, "fox_bias", [P, T])
        peak = g.sb(stack, "fox_peak", [P, GH * NT])
        shift = g.sb(stack, "fox_shift", [P, GH * NT])
        total = g.sb(stack, "fox_total", [P, GH * NT])
        inv = g.sb(stack, "fox_inv", [P, GH * NT])
        with nc.Block("fox", no_gpsimd_drain=True) as block:

            @block.tensor
            def _(pe):
                for h in range(GH):
                    for a in range(2):
                        n = 2 * h + a
                        if n >= 2:
                            pe.wait_ge(sem["fox_T_copied"], past["fox_T_copied"] + n - 1)
                        for j in range(NT):
                            ins = nc.tensor.transpose(ps[0:K, 6 + n % 2, j * P:(j + 1) * P], s.fox_qk[:, j, a, h, :], g.ident[:])
                        ins.then_inc(sem["fox_turned"], add("fox_turned", 1))

                def logits(h):
                    pe.wait_ge(sem["fox_T_copied"], past["fox_T_copied"] + 2 * h + 2)
                    for j in range(NT):
                        m = NT * h + j
                        if m >= 2:
                            pe.wait_ge(sem["fox_masked"], past["fox_masked"] + m - 1)
                        n = (j + 1) * P
                        g.product(ps[:, m % 2, 0:n], qT[:, h, j * P:(j + 1) * P], kT[:, h, 0:n]).then_inc(sem["fox_logits"], add("fox_logits", 1))

                logits(0)
                for h in range(GH):
                    if h + 1 < GH:
                        logits(h + 1)
                    for j in range(NT):
                        m = NT * h + j
                        pe.wait_ge(sem["fox_prob"], past["fox_prob"] + m + 1)
                        if m >= 2:
                            pe.wait_ge(sem["fox_probT"], past["fox_probT"] + m - 1)
                        for i in range(j + 1):
                            ins = nc.tensor.transpose(ps[:, 2 + m % 2, i * P:(i + 1) * P], prob[:, h % 2, j, i * P:(i + 1) * P], g.ident[:])
                        ins.then_inc(sem["fox_prob_turned"], add("fox_prob_turned", 1))
                    pe.wait_ge(sem["fox_probT"], past["fox_probT"] + NT * h + NT)
                    if h >= 2:
                        pe.wait_ge(sem["fox_done"], past["fox_done"] + h - 1)
                    rows = slice((h % 2) * HD, (h % 2 + 1) * HD)
                    for i in range(NT):
                        ins = g.product(ps[rows, 4 + h % 2, i * P:T], s.vB[:, i, h * HD:(h + 1) * HD], probT[:, i, i * P:T], i == 0, i == NT - 1, check=False)
                    ins.then_inc(sem["fox_o"], add("fox_o", 1))

            @block.scalar
            def _(act):
                for h in range(GH):
                    for j in range(NT):
                        m = NT * h + j
                        row = prob[:, h % 2, j, 0:(j + 1) * P]
                        act.wait_ge(sem["fox_shift"], past["fox_shift"] + m + 1)
                        nc.scalar.activation(row, row, ACT.Exp, bias=shift[:, m:m + 1], accum_out=total[:, m:m + 1]).then_inc(sem["fox_exp"], add("fox_exp", 1))
                    for j in range(NT):
                        m = NT * h + j
                        act.wait_ge(sem["fox_prob_turned"], past["fox_prob_turned"] + m + 1)
                        if h:
                            act.wait_ge(sem["fox_o"], past["fox_o"] + h)
                        nc.scalar.activation(probT[:, 0:j + 1, j * P:(j + 1) * P],
                                                                 ps[:, 2 + m % 2, 0:(j + 1) * P].rearrange("p (i t) -> p i t", t=P), ACT.Copy).then_inc(sem["fox_probT"], add("fox_probT", 1))

            @block.vector
            def _(dve):
                nc.vector.memset(bias[:, 0:T - P], 0.0).then_inc(sem["fox_bias"], add("fox_bias", 1))
                nc.vector.tensor_scalar(bias[:, T - P:T], g.after[:], MASKED, None, ALU.mult).then_inc(sem["fox_bias"], add("fox_bias", 1))
                for n in range(2 * GH):
                    dve.wait_ge(sem["fox_turned"], past["fox_turned"] + n + 1)
                    nc.vector.tensor_copy((kT if n % 2 else qT)[:, n // 2, :], ps[0:K, 6 + n % 2, :]).then_inc(sem["fox_T_copied"], add("fox_T_copied", 1))
                dve.wait_ge(sem["fox_bias"], past["fox_bias"] + 2)

                def mask(h):
                    for j in range(NT):
                        m = NT * h + j
                        n = (j + 1) * P
                        dve.wait_ge(sem["fox_logits"], past["fox_logits"] + m + 1)
                        if h >= 2:
                            dve.wait_ge(sem["fox_prob_turned"], past["fox_prob_turned"] + m - 2 * NT + 1)
                        nc.vector.tensor_tensor_reduce(out=prob[:, h % 2, j, 0:n], in0=ps[:, m % 2, 0:n], in1=bias[:, T - n:T],
                                                                            scale=1.0, scalar=TAKEN, op0=ALU.add, op1=ALU.max, accum_out=peak[:, m:m + 1]).then_inc(sem["fox_masked"], add("fox_masked", 1))
                        dve.wait_ge(sem["fox_masked"], past["fox_masked"] + m + 1)
                        nc.vector.tensor_scalar(shift[:, m:m + 1], peak[:, m:m + 1], -1.0, None, ALU.mult).then_inc(sem["fox_shift"], add("fox_shift", 1))

                def normalise(h):
                    for j in range(NT):
                        m = NT * h + j
                        dve.wait_ge(sem["fox_exp"], past["fox_exp"] + m + 1)
                        nc.vector.reciprocal(inv[:, m:m + 1], total[:, m:m + 1]).then_inc(sem["fox_inv"], add("fox_inv", 1))
                        dve.wait_ge(sem["fox_inv"], past["fox_inv"] + m + 1)
                        row = prob[:, h % 2, j, 0:(j + 1) * P]
                        nc.vector.tensor_scalar(row, row, inv[:, m:m + 1], None, ALU.mult).then_inc(sem["fox_prob"], add("fox_prob", 1))

                mask(0)
                normalise(0)
                for h in range(GH):
                    if h + 1 < GH:
                        mask(h + 1)
                        normalise(h + 1)
                    rows = slice((h % 2) * HD, (h % 2 + 1) * HD)
                    dve.wait_ge(sem["fox_o"], past["fox_o"] + h + 1)
                    nc.vector.tensor_tensor(s.mixT[rows, 2 + h // 2, :], ps[rows, 4 + h % 2, :], s.zT[rows, 2 + h // 2, :], ALU.mult).then_inc(sem["fox_done"], add("fox_done", 1))

            @block.gpsimd
            def _(pool):
                for i in range(8):
                    x, previous = s.raw[:, i, 1:], s.raw[:, i, 0:T]
                    out = s.shifted[:, i, :]
                    nc.gpsimd.tensor_tensor(out, previous, x, ALU.subtract).then_inc(sem["shift_step"], add("shift_step", 1))
                    pool.wait_ge(sem["shift_step"], count["shift_step"])
                    nc.gpsimd.tensor_scalar(out, out, g.col("mu")[:, i:i + 1], None, ALU.mult).then_inc(sem["shift_step"], add("shift_step", 1))
                    pool.wait_ge(sem["shift_step"], count["shift_step"])
                    nc.gpsimd.tensor_tensor(out, out, x, ALU.add).then_inc(sem["shifted"], add("shifted", 1))

            @block.sync
            def _(sp):
                g.load_chunks(sp)
                sp.wait_ge(sem["shifted"], past["shifted"] + 8)
    g.sem.end_phase()


def phase_mem(g, s):
    nc, t, ps = g.nc, g.t, g.ps
    sem, past, count, add = g.sem, g.sem.past, g.sem.count, g.sem.add
    PAIRS = GH // 2
    with ExitStack() as stack:
        qT = g.room[:, 1, 2:2 + PAIRS, :]
        kT = g.room[:, 1, 4, :].rearrange("p (a m) -> p a m", a=PAIRS)
        prob = g.room[:, 0, 0:NT].rearrange("p (b j) (i m) -> p b (j i) m", b=2, m=N_MEM)
        probT = g.room[:, 1, 0:MT]
        peak = g.sb(stack, "mem_peak", [P, GH, NT])
        total = g.sb(stack, "mem_total", [P, GH * NT])
        inv = g.sb(stack, "mem_inv", [P, GH, NT])
        with nc.Block("memory", no_gpsimd_drain=True) as block:

            @block.tensor
            def _(pe):
                for i in range(PAIRS):
                    for j in range(NT):
                        ins = nc.tensor.transpose(ps[:, 6, j * P:(j + 1) * P], s.heads[:, j, 4, i * P:(i + 1) * P], g.ident[:])
                    for j in range(MT):
                        ins = nc.tensor.transpose(ps[:, 7, j * P:(j + 1) * P], s.mem_kv[:, j, i * P:(i + 1) * P], g.ident[:])
                    ins.then_inc(sem["mem_turned"], add("mem_turned", 1))
                    pe.wait_ge(sem["mem_T_copied"], past["mem_T_copied"] + 2 * i + 2)

                def logits(h):
                    rows = slice((h % 2) * HD, (h % 2 + 1) * HD)
                    for j in range(NT):
                        b = 2 * h + j // 2
                        if b >= 4 and j % 2 == 0:
                            pe.wait_ge(sem["mem_exp"], past["mem_exp"] + 2 * (b - 4) + 2)
                        ins = g.product(ps[:, b % 4, (j % 2) * N_MEM:(j % 2 + 1) * N_MEM], qT[rows, h // 2, j * P:(j + 1) * P], kT[rows, h // 2, :])
                        if j % 2:
                            ins.then_inc(sem["mem_logits"], add("mem_logits", 1))

                logits(0)
                for h in range(GH):
                    if h + 1 < GH:
                        logits(h + 1)
                    for i in range(MT):
                        n = MT * h + i
                        if n >= 2:
                            pe.wait_ge(sem["mem_probT"], past["mem_probT"] + n - 1)
                        pe.wait_ge(sem["mem_prob"], past["mem_prob"] + h + 1)
                        for j in range(NT):
                            ins = nc.tensor.transpose(ps[:, 4 + n % 2, j * P:(j + 1) * P], prob[:, h % 2, j, i * P:(i + 1) * P], g.ident[:])
                        ins.then_inc(sem["mem_prob_turned"], add("mem_prob_turned", 1))
                    pe.wait_ge(sem["mem_probT"], past["mem_probT"] + MT * h + MT)
                    if h >= 2:
                        pe.wait_ge(sem["mem_done"], past["mem_done"] + h - 1)
                    rows = slice((h % 2) * HD, (h % 2 + 1) * HD)
                    for i in range(MT):
                        ins = g.product(ps[rows, 6 + h % 2, :], s.mem_kv[:, i, GW + h * HD:GW + (h + 1) * HD], probT[:, i, :], i == 0, i == MT - 1)
                    ins.then_inc(sem["mem_o"], add("mem_o", 1))

            @block.scalar
            def _(act):
                def exps(h):
                    act.wait_ge(sem["mem_peak"], past["mem_peak"] + 2 * h + 2)
                    for j in range(NT):
                        if h >= 2:
                            act.wait_ge(sem["mem_prob_turned"], past["mem_prob_turned"] + MT * (h - 2) + MT)
                        b = 2 * h + j // 2
                        nc.scalar.activation(prob[:, h % 2, j, :], ps[:, b % 4, (j % 2) * N_MEM:(j % 2 + 1) * N_MEM], ACT.Exp,
                                                               bias=peak[:, h, j:j + 1], scale=HEAD_SCALE, accum_out=total[:, h * NT + j:h * NT + j + 1]).then_inc(sem["mem_exp"], add("mem_exp", 1))

                exps(0)
                for h in range(GH):
                    if h + 1 < GH:
                        exps(h + 1)
                    for i in range(MT):
                        act.wait_ge(sem["mem_prob_turned"], past["mem_prob_turned"] + MT * h + i + 1)
                        if h:
                            act.wait_ge(sem["mem_o"], past["mem_o"] + h)
                        nc.scalar.activation(probT[:, i, :], ps[:, 4 + (MT * h + i) % 2, :], ACT.Copy).then_inc(sem["mem_probT"], add("mem_probT", 1))

            @block.vector
            def _(dve):
                for i in range(PAIRS):
                    dve.wait_ge(sem["mem_turned"], past["mem_turned"] + i + 1)
                    nc.vector.tensor_copy(qT[:, i, :], ps[:, 6, :]).then_inc(sem["mem_T_copied"], add("mem_T_copied", 1))
                    nc.vector.tensor_copy(kT[:, i, :], ps[:, 7, 0:N_MEM]).then_inc(sem["mem_T_copied"], add("mem_T_copied", 1))

                def peaks(h):
                    for b in range(2):
                        dve.wait_ge(sem["mem_logits"], past["mem_logits"] + 2 * h + b + 1)
                        nc.vector.tensor_reduce(peak[:, h, 2 * b:2 * b + 2], ps[:, (2 * h + b) % 4, :].rearrange("p (j m) -> p j m", j=2), AX, ALU.max).then_inc(sem["mem_max"], add("mem_max", 1))
                    for b in range(2):
                        dve.wait_ge(sem["mem_max"], past["mem_max"] + 2 * h + b + 1)
                        nc.vector.tensor_scalar(peak[:, h, 2 * b:2 * b + 2], peak[:, h, 2 * b:2 * b + 2], -HEAD_SCALE, None, ALU.mult).then_inc(sem["mem_peak"], add("mem_peak", 1))

                def normalise(h):
                    dve.wait_ge(sem["mem_exp"], past["mem_exp"] + NT * h + NT)
                    nc.vector.reciprocal(inv[:, h, :], total[:, h * NT:(h + 1) * NT]).then_inc(sem["mem_inv"], add("mem_inv", 1))
                    dve.wait_ge(sem["mem_inv"], past["mem_inv"] + h + 1)
                    nc.vector.tensor_tensor(prob[:, h % 2], prob[:, h % 2], inv[:, h, :].unsqueeze(2).to_broadcast([P, NT, N_MEM]), ALU.mult).then_inc(sem["mem_prob"], add("mem_prob", 1))

                peaks(0)
                normalise(0)
                for h in range(GH):
                    if h + 1 < GH:
                        peaks(h + 1)
                        normalise(h + 1)
                    rows = slice((h % 2) * HD, (h % 2 + 1) * HD)
                    dve.wait_ge(sem["mem_o"], past["mem_o"] + h + 1)
                    nc.vector.tensor_tensor(s.mixT[rows, 8 + h // 2, :], ps[rows, 6 + h % 2, :], s.zT[rows, 6 + h // 2, :], ALU.mult).then_inc(sem["mem_done"], add("mem_done", 1))

            @block.sync
            def _(sp):
                g.load_chunks(sp)
    g.sem.end_phase()


def phase_mlstm(g, s):
    nc, t, ps = g.nc, g.t, g.ps
    sem, past, count, add = g.sem, g.sem.past, g.sem.count, g.sem.add
    PAIRS = GH // 2
    with ExitStack() as stack:
        a_row, mu_row = g.room[0:GH, 2, 4, :], g.room[0:GH, 2, 5, :]
        pick = g.room[0:GH, 2, 6, :].rearrange("p (h t) -> p h t", h=GH)
        mu = g.sb(stack, "mu", [P, NT, GH])
        floor = g.sb(stack, "floor", [P, NT, GH])
        weight, score = (g.room[:, i].rearrange("p (b j) n -> p b j n", b=2) for i in range(2))
        den = g.sb(stack, "den", [P, NT, GH])
        y, sq = (g.room[:, 2, 2 * i:2 * i + 2, :].rearrange("p a (b d) -> p (a b) d", d=GW) for i in range(2))
        ss = g.sb(stack, "mlstm_ss", [P, NT * GH])
        W = HD + 1
        with nc.Block("mlstm", no_gpsimd_drain=True) as block:

            @block.tensor
            def _(pe):
                for j in range(NT):
                    ins = nc.tensor.transpose(ps[0:GH, 0, j * P:(j + 1) * P], s.a_tok[:, j, :], g.ident[:])
                ins.then_inc(sem["a_turned"], add("a_turned", 1))
                pe.wait_ge(sem["mu_row"], past["mu_row"] + 1)
                for j in range(NT):
                    ins = nc.tensor.transpose(ps[:, 1, j * GH:(j + 1) * GH], mu_row[:, j * P:(j + 1) * P], g.ident[0:GH, 0:GH])
                ins.then_inc(sem["mu_turned"], add("mu_turned", 1))
                pe.wait_ge(sem["mu_copied"], past["mu_copied"] + 1)
                pe.wait_ge(sem["pick"], past["pick"] + GH)

                def spread(h):
                    if h:
                        pe.wait_ge(sem["weight_log"], past["weight_log"] + NT * h)
                    g.product(ps[:, 0, :], pick[:, h, :], mu_row[:]).then_inc(sem["mu_spread"], add("mu_spread", 1))

                def products(h):
                    rows = slice((h % 2) * HD, (h % 2 + 1) * HD)
                    for i in range(NT):
                        m = NT * h + i
                        if m >= 3:
                            pe.wait_ge(sem["weighted"], past["weighted"] + m - 2)
                        g.product(ps[:, 1 + m % 3, i * P:T], s.qkT[rows, 2 + h // 2, i * P:(i + 1) * P], s.qkT[rows, h // 2, i * P:T]).then_inc(sem["mlstm_scores"], add("mlstm_scores", 1))

                spread(0)
                spread(1)
                products(0)
                for h in range(GH):
                    if h + 2 < GH:
                        spread(h + 2)
                    if h + 1 < GH:
                        products(h + 1)
                    pe.wait_ge(sem["weighted"], past["weighted"] + NT * h + NT)
                    for j in range(NT):
                        for i in range(j + 1):
                            ins = g.product(ps[:, 4 + j, h * W:(h + 1) * W], score[:, h % 2, i, j * P:(j + 1) * P], s.vC[:, i, h, :], i == 0, i == j, check=False)
                    ins.then_inc(sem["mlstm_num"], add("mlstm_num", 1))
                pe.wait_ge(sem["mlstm_gained"], past["mlstm_gained"] + 1)
                to_gated(g, pe, y, [0, 1])

            @block.scalar
            def _(act):
                act.wait_ge(sem["m_made"], past["m_made"] + 1)
                nc.scalar.activation(floor[:], floor[:], ACT.Exp, scale=-1.0).then_inc(sem["floor"], add("floor", 1))
                for h in range(GH):
                    for i in range(NT):
                        m = NT * h + i
                        act.wait_ge(sem["weight_log"], past["weight_log"] + m + 1)
                        w = weight[:, h % 2, i, i * P:T]
                        nc.scalar.activation(w, w, ACT.Exp).then_inc(sem["weight"], add("weight", 1))
                act.wait_ge(sem["mlstm_num"], past["mlstm_num"] + GH)
                for j in range(NT):
                    nc.scalar.activation(den[:, j, :], ps[:, 4 + j, 0:GH * W].rearrange("p (h d) -> p h d", h=GH)[:, :, HD], ACT.Abs).then_inc(sem["den_abs"], add("den_abs", 1))
                act.wait_ge(sem["mlstm_y"], past["mlstm_y"] + NT + 1)
                nc.scalar.activation(sq[:], y[:], ACT.Square).then_inc(sem["mlstm_sq"], add("mlstm_sq", 1))
                act.wait_ge(sem["mlstm_mean_sq"], past["mlstm_mean_sq"] + 1)
                nc.scalar.activation(ss[:], ss[:], ACT.Sqrt).then_inc(sem["mlstm_root"], add("mlstm_root", 1))

            @block.gpsimd
            def _(pool):
                for h in range(GH):
                    for i in range(NT):
                        m = NT * h + i
                        pool.wait_ge(sem["weight"], past["weight"] + m + 1)
                        w = weight[:, h % 2, i, i * P:(i + 1) * P]
                        nc.gpsimd.tensor_tensor(w, w, g.not_before[:], ALU.mult).then_inc(sem["weight_masked"], add("weight_masked", 1))

            @block.vector
            def _(dve):
                for h in range(GH):
                    nc.vector.tensor_scalar(pick[:, h, :], g.ident[0:GH, h:h + 1].to_broadcast([GH, P]), -1.0, None, ALU.mult).then_inc(sem["pick"], add("pick", 1))
                dve.wait_ge(sem["a_turned"], past["a_turned"] + 1)
                nc.vector.tensor_copy(a_row[:], ps[0:GH, 0, :]).then_inc(sem["a_row"], add("a_row", 1))
                dve.wait_ge(sem["a_row"], past["a_row"] + 1)
                nc.vector.tensor_tensor_scan(mu_row[:], a_row[:], a_row[:], 0.0, ALU.max, ALU.max).then_inc(sem["mu_row"], add("mu_row", 1))
                dve.wait_ge(sem["mu_turned"], past["mu_turned"] + 1)
                nc.vector.tensor_copy(mu[:], ps[:, 1, 0:NT * GH].rearrange("p (j h) -> p j h", j=NT)).then_inc(sem["mu_copied"], add("mu_copied", 1))
                dve.wait_ge(sem["mu_copied"], past["mu_copied"] + 1)
                nc.vector.tensor_tensor(floor[:], mu[:], s.cum[:, :, GH:2 * GH], ALU.add).then_inc(sem["m_made"], add("m_made", 1))

                def logs(h):
                    dve.wait_ge(sem["mu_spread"], past["mu_spread"] + h + 1)
                    for i in range(NT):
                        if h >= 2:
                            dve.wait_ge(sem["weighted"], past["weighted"] + NT * (h - 2) + i + 1)
                        nc.vector.tensor_scalar(weight[:, h % 2, i, i * P:T], ps[:, 0, i * P:T], s.a_tok[:, i, h:h + 1], 0.0, ALU.add, ALU.min).then_inc(sem["weight_log"], add("weight_log", 1))

                logs(0)
                for h in range(GH):
                    if h + 1 < GH:
                        logs(h + 1)
                    for i in range(NT):
                        m = NT * h + i
                        dve.wait_ge(sem["mlstm_scores"], past["mlstm_scores"] + m + 1)
                        dve.wait_ge(sem["weight_masked"], past["weight_masked"] + m + 1)
                        if h >= 2:
                            dve.wait_ge(sem["mlstm_num"], past["mlstm_num"] + h - 1)
                        nc.vector.tensor_tensor(score[:, h % 2, i, i * P:T], ps[:, 1 + m % 3, i * P:T], weight[:, h % 2, i, i * P:T], ALU.mult).then_inc(sem["weighted"], add("weighted", 1))
                dve.wait_ge(sem["den_abs"], past["den_abs"] + NT)
                dve.wait_ge(sem["floor"], past["floor"] + 1)
                nc.vector.tensor_tensor(den[:], den[:], floor[:], ALU.max).then_inc(sem["den"], add("den", 1))
                dve.wait_ge(sem["den"], past["den"] + 1)
                nc.vector.reciprocal(den[:], den[:]).then_inc(sem["den"], add("den", 1))
                dve.wait_ge(sem["den"], past["den"] + 2)
                for j in range(NT):
                    num = ps[:, 4 + j, 0:GH * W].rearrange("p (h d) -> p h d", h=GH)[:, :, 0:HD]
                    nc.vector.tensor_tensor(y[:, j, :].rearrange("p (h d) -> p h d", h=GH), num, den[:, j, :].unsqueeze(2).to_broadcast([P, GH, HD]), ALU.mult).then_inc(sem["mlstm_y"], add("mlstm_y", 1))
                dve.wait_ge(sem["mlstm_y"], past["mlstm_y"] + NT)
                nc.vector.tensor_tensor(y[:], y[:], s.o_sig[:], ALU.mult).then_inc(sem["mlstm_y"], add("mlstm_y", 1))
                dve.wait_ge(sem["mlstm_sq"], past["mlstm_sq"] + 1)
                nc.vector.tensor_reduce(ss[:], sq[:].rearrange("p j (h d) -> p (j h) d", d=HD), AX, ALU.add).then_inc(sem["mlstm_sums"], add("mlstm_sums", 1))
                dve.wait_ge(sem["mlstm_sums"], past["mlstm_sums"] + 1)
                nc.vector.tensor_scalar(ss[:], ss[:], 1.0 / HD, RMS_EPS, ALU.mult, ALU.add).then_inc(sem["mlstm_mean_sq"], add("mlstm_mean_sq", 1))
                dve.wait_ge(sem["mlstm_root"], past["mlstm_root"] + 1)
                nc.vector.reciprocal(ss[:], ss[:]).then_inc(sem["mlstm_rstd"], add("mlstm_rstd", 1))
                dve.wait_ge(sem["mlstm_rstd"], past["mlstm_rstd"] + 1)
                v = y[:].rearrange("p j (h d) -> p (j h) d", d=HD)
                nc.vector.tensor_tensor(v, v, ss[:].unsqueeze(2).to_broadcast([P, NT * GH, HD]), ALU.mult).then_inc(sem["mlstm_scaled"], add("mlstm_scaled", 1))
                dve.wait_ge(sem["mlstm_scaled"], past["mlstm_scaled"] + 1)
                nc.vector.tensor_tensor(y[:], y[:], s.gains[:, 5, :].unsqueeze(1).to_broadcast([P, NT, GW]), ALU.mult).then_inc(sem["mlstm_gained"], add("mlstm_gained", 1))
                gate_turned(g, dve, s, 4, 4, [0, 1])

            @block.sync
            def _(sp):
                g.load_chunks(sp)
    g.sem.end_phase()


def phase_rwkv(g, s):
    nc, t, ps = g.nc, g.t, g.ps
    sem, past, count, add = g.sem, g.sem.past, g.sem.count, g.sem.add
    C = 64
    PAIRS = GH // 2
    LEVELS = 6
    with ExitStack() as stack:
        new = lambda name, shape: g.sb(stack, name, shape)
        shifted = s.shifted
        low = new("low_shifted", [RANK2, 2, T])
        ar = new("ar", [P, PAIRS, NT, 2, P])
        bt = new("bt", [P, PAIRS, T])
        kt = new("kt", [P, PAIRS, T])
        end_decay = new("end_decay", [P, PAIRS, NCH])
        tok = new("rwkv_tok", [P, 4, NT, GW])
        bonus = new("bonus", [P, NT, GH])
        WT = new("WT", [P, PAIRS, T])
        U = new("U", [P, NT, GW])
        sa = new("sa", [P, NT, GW])
        state = new("rwkv_state", [P, NCH + 1, PAIRS, C])
        LT = new("LT", [P, NT, GH, P])
        RBT = new("RBT", [P, NT, GH, P])
        MTt = new("MTt", [P, NT, GH, P])
        rooms = [g.room[:, i, h * NT:(h + 1) * NT].rearrange("p j (h t) -> p j h t", t=P) for i in range(2) for h in range(2)]
        RKT, Ti, TiT = rooms[:3]
        ss = new("rwkv_ss", [P, NT * GH])
        flat = lambda x, i: x[:].rearrange("p j h t -> p (j h t)")[:, i * PAIRS * T:(i + 1) * PAIRS * T].rearrange("p (a t) -> p a t", a=PAIRS)
        sg, cl = flat(Ti, 0), flat(Ti, 1)
        av, kk = flat(TiT, 0), flat(TiT, 1)
        e1, e2 = flat(LT, 0), flat(LT, 1)
        norm, tmp = flat(RBT, 0), flat(RBT, 1)
        hats = flat(MTt, 0), flat(MTt, 1)
        X = shifted[:, 0:4, :].rearrange("p a (h t) -> p a h t", h=GH)
        Cm = rooms[3][:, 0:2]
        y = U
        r_, k_, v_, z_ = (shifted[:, PAIRS * i:PAIRS * (i + 1), :] for i in range(4))
        ch = lambda x: x.rearrange("p a (c i) -> p a c i", i=C)
        col = lambda name: g.col(name)
        with nc.Block("rwkv_prep", no_gpsimd_drain=True) as block:

            @block.vector
            def _(dve):
                step = "rwkv_step"

                def then(ins):
                    ins.then_inc(sem[step], add(step, 1))
                    dve.wait_ge(sem[step], count[step])

                for i in range(2):
                    mu = col("mu_wlo" if i == 0 else "mu_alo")[0:RANK2, 0:1]
                    then(nc.vector.tensor_tensor(low[:, i, :], s.low[:, i, 0:T], s.low[:, i, 1:], ALU.subtract))
                    nc.vector.scalar_tensor_tensor(out=low[:, i, :], in0=low[:, i, :], scalar=mu, in1=s.low[:, i, 1:], op0=ALU.mult, op1=ALU.add).then_inc(sem["low_shifted"], add("low_shifted", 1))
                for i in range(PAIRS):
                    nc.vector.tensor_scalar(kk[:, i, :], k_[:, i, :], col("k_k")[:, i:i + 1], None, ALU.mult).then_inc(sem["kk"], add("kk", 1))
                for i in range(PAIRS):
                    dve.wait_ge(sem["decay_sigmoid"], past["decay_sigmoid"] + i + 1)
                    nc.vector.tensor_tensor_scan(cl[:, i, :], g.keep_state[:], sg[:, i, :], 0.0, ALU.mult, ALU.add).then_inc(sem["cl"], add("cl", 1))
                dve.wait_ge(sem["cl"], past["cl"] + PAIRS)
                nc.vector.tensor_tensor(sg, cl, sg, ALU.subtract).then_inc(sem["before"], add("before", 1))
                dve.wait_ge(sem["kk_norm"], past["kk_norm"] + PAIRS)
                then(nc.vector.tensor_scalar(norm, norm, 1e-12, None, ALU.max))
                then(nc.vector.reciprocal(norm, norm))
                then(nc.vector.tensor_tensor(kk, kk, norm, ALU.mult))
                dve.wait_ge(sem["a_sigmoid"], past["a_sigmoid"] + PAIRS)
                for i in range(PAIRS):
                    then(nc.vector.tensor_scalar(tmp[:, i, :], av[:, i, :], 1.0, col("k_a")[:, i:i + 1], ALU.subtract, ALU.mult))
                then(nc.vector.scalar_tensor_tensor(out=k_, in0=tmp, scalar=1.0, in1=k_, op0=ALU.add, op1=ALU.mult))
                for i in range(PAIRS):
                    nc.vector.scalar_tensor_tensor(out=tmp[:, i, :], in0=r_[:, i, :], scalar=col("r_k")[:, i:i + 1], in1=k_[:, i, :], op0=ALU.mult, op1=ALU.mult).then_inc(sem["rk"], add("rk", 1))
                tiles = lambda x: x.rearrange("p a (j t) -> p a j t", j=NT)
                dve.wait_ge(sem["decays2"], past["decays2"] + 1)
                for i in range(PAIRS):
                    nc.vector.tensor_tensor(ar[:, i, :, 0, :], tiles(kk)[:, i], tiles(sg)[:, i], ALU.mult).then_inc(sem["at"], add("at", 1))
                dve.wait_ge(sem["decays2"], past["decays2"] + 2)
                for i in range(PAIRS):
                    nc.vector.tensor_tensor(ar[:, i, :, 1, :], tiles(r_)[:, i], tiles(e1)[:, i], ALU.mult).then_inc(sem["rt"], add("rt", 1))
                dve.wait_ge(sem["at"], past["at"] + PAIRS)
                then(nc.vector.tensor_tensor(kk, kk, av, ALU.mult))
                dve.wait_ge(sem["decays2"], past["decays2"] + 4)
                nc.vector.tensor_tensor(bt[:], kk, e2, ALU.mult).then_inc(sem["bt"], add("bt", 1))
                nc.vector.tensor_tensor(kt[:], k_, e2, ALU.mult).then_inc(sem["kt"], add("kt", 1))
                dve.wait_ge(sem["bt"], past["bt"] + 1)
                dve.wait_ge(sem["kt"], past["kt"] + 1)
                for x, h in ((bt, hats[0]), (kt, hats[1])):
                    for i in range(PAIRS):
                        nc.vector.tensor_tensor(ch(h)[:, i], ch(x[:])[:, i], end_decay[:, i, :].unsqueeze(2).to_broadcast([P, NCH, C]), ALU.mult).then_inc(sem["hats"], add("hats", 1))
                nc.vector.memset(state[:, 0], 0.0).then_inc(sem["state_zero"], add("state_zero", 1))
                for n in range(4 * NT // 2):
                    dve.wait_ge(sem["tok_turned"], past["tok_turned"] + n + 1)
                    which, j2 = n // 2, n % 2
                    nc.vector.tensor_copy(tok[:, which, 2 * j2:2 * j2 + 2, :], ps[:, 4 + n % 4, :].rearrange("p (j d) -> p j d", j=2)).then_inc(sem["tok_copied"], add("tok_copied", 1))
                dve.wait_ge(sem["bonus_ready"], past["bonus_ready"] + 1)
                nc.vector.tensor_copy(bonus[:], ps[:, 3, 0:NT * GH].rearrange("p (j h) -> p j h", j=NT)).then_inc(sem["bonus_copied"], add("bonus_copied", 1))

            @block.scalar
            def _(act):
                act.wait_ge(sem["low_shifted"], past["low_shifted"] + 1)
                nc.scalar.activation(low[:, 0, :], low[:, 0, :], ACT.Tanh).then_inc(sem["low_tanh"], add("low_tanh", 1))
                for i in range(PAIRS):
                    act.wait_ge(sem["decay_in"], past["decay_in"] + i + 1)
                    nc.scalar.activation(sg[:, i, :], ps[:, i, :], ACT.Sigmoid, bias=col("w0")[:, i:i + 1]).then_inc(sem["decay_sigmoid"], add("decay_sigmoid", 1))
                for i in range(PAIRS):
                    act.wait_ge(sem["a_in"], past["a_in"] + i + 1)
                    nc.scalar.activation(av[:, i, :], ps[:, 2 + i, :], ACT.Sigmoid, bias=col("a0")[:, i:i + 1]).then_inc(sem["a_sigmoid"], add("a_sigmoid", 1))
                nc.scalar.activation(s.zD[:], z_, ACT.Silu).then_inc(sem["z_silu2"], add("z_silu2", 1))
                for i in range(PAIRS):
                    act.wait_ge(sem["kk"], past["kk"] + i + 1)
                    nc.scalar.activation(e1[:, i, :], kk[:, i, :], ACT.Square).then_inc(sem["kk_sq"], add("kk_sq", 1))
                for i in range(PAIRS):
                    act.wait_ge(sem["kk_sums"], past["kk_sums"] + i + 1)
                    nc.scalar.activation(norm[:, i, :], ps[:, 4 + i, :], ACT.Sqrt).then_inc(sem["kk_norm"], add("kk_norm", 1))
                act.wait_ge(sem["before"], past["before"] + 1)
                nc.scalar.activation(sg, sg, ACT.Exp, scale=-DECAY_SCALE).then_inc(sem["decays2"], add("decays2", 1))
                act.wait_ge(sem["kk_sums"], past["kk_sums"] + PAIRS)
                nc.scalar.activation(e1, cl, ACT.Exp, scale=-DECAY_SCALE).then_inc(sem["decays2"], add("decays2", 1))
                nc.scalar.activation(end_decay[:], ch(cl)[:, :, :, C - 1], ACT.Exp, scale=-DECAY_SCALE).then_inc(sem["decays2"], add("decays2", 1))
                nc.scalar.activation(e2, cl, ACT.Exp, scale=DECAY_SCALE).then_inc(sem["decays2"], add("decays2", 1))

            @block.tensor
            def _(pe):
                pe.wait_ge(sem["low_tanh"], past["low_tanh"] + 1)
                for i in range(PAIRS):
                    g.product(ps[:, i, :], s.w2_decay[:, i * P:(i + 1) * P], low[:, 0, :]).then_inc(sem["decay_in"], add("decay_in", 1))
                pe.wait_ge(sem["low_shifted"], past["low_shifted"] + 2)
                for i in range(PAIRS):
                    g.product(ps[:, 2 + i, :], s.w2_a[:, i * P:(i + 1) * P], low[:, 1, :]).then_inc(sem["a_in"], add("a_in", 1))
                for i in range(PAIRS):
                    pe.wait_ge(sem["kk_sq"], past["kk_sq"] + i + 1)
                    g.product(ps[:, 4 + i, :], g.same64[:], e1[:, i, :]).then_inc(sem["kk_sums"], add("kk_sums", 1))
                pe.wait_ge(sem["kk_norm"], past["kk_norm"] + PAIRS)
                pe.wait_ge(sem["a_sigmoid"], past["a_sigmoid"] + PAIRS)
                for n in range(4 * NT // 2):
                    which, j2 = n // 2, n % 2
                    if n >= 4:
                        pe.wait_ge(sem["tok_copied"], past["tok_copied"] + n - 3)
                    if which < 2:
                        pe.wait_ge(sem["hats"], past["hats"] + PAIRS * (which + 1))
                    elif which == 3:
                        pe.wait_ge(sem["at"], past["at"] + PAIRS)
                    for j in (2 * j2, 2 * j2 + 1):
                        for i in range(PAIRS):
                            src = (hats[0][:, i, j * P:(j + 1) * P], hats[1][:, i, j * P:(j + 1) * P], v_[:, i, j * P:(j + 1) * P], ar[:, i, j, 0, :])[which]
                            at = (j - 2 * j2) * GW + i * P
                            ins = nc.tensor.transpose(ps[:, 4 + n % 4, at:at + P], src, g.ident[:])
                    ins.then_inc(sem["tok_turned"], add("tok_turned", 1))
                pe.wait_ge(sem["rk"], past["rk"] + PAIRS)
                for j in range(NT):
                    for i in range(PAIRS):
                        ins = g.product(ps[:, 3, j * GH + 2 * i:j * GH + 2 * i + 2], tmp[:, i, j * P:(j + 1) * P], g.same64[:, 0:P:HD])
                ins.then_inc(sem["bonus_ready"], add("bonus_ready", 1))

            @block.sync
            def _(sp):
                g.load_chunks(sp)
        g.sem.end_phase()

        y_in = lambda j: ps[:, 4 + 2 * (j // 2):6 + 2 * (j // 2), (j % 2) * P:(j % 2 + 1) * P].rearrange("p b (i d) -> p b i d", d=HD)
        by_parity = lambda x: x.rearrange("p (i b d) -> p b i d", b=2, d=HD)
        with nc.Block("rwkv", no_gpsimd_drain=True) as block:

            @block.tensor
            def _(pe):
                for j in range(NT):
                    tile = slice(j * P, (j + 1) * P)
                    for a, x in enumerate((bt, kt)):
                        for i in range(PAIRS):
                            n = 2 * PAIRS * j + PAIRS * a + i
                            if n >= 2:
                                pe.wait_ge(sem["pair_masked"], past["pair_masked"] + 2 * (n - 2) + 2)
                            for b in range(2):
                                rows = slice(b * HD, (b + 1) * HD)
                                ins = g.product(ps[:, 2 * (n % 2) + b, 0:2 * P], x[rows, i, tile], ar[rows, i, j].rearrange("p a t -> p (a t)"))
                            ins.then_inc(sem["pair_ready"], add("pair_ready", 1))
                    if j >= 2:
                        pe.wait_ge(sem["Ti_init"], past["Ti_init"] + j - 1)
                    for h in range(GH):
                        rows = slice((h % 2) * HD, (h % 2 + 1) * HD)
                        ins = g.product(ps[:, 4 + 2 * (j % 2) + h % 2, (h // 2) * P:(h // 2 + 1) * P], ar[rows, h // 2, j, 0, :], bt[rows, h // 2, tile])
                    ins.then_inc(sem["L_ready"], add("L_ready", 1))
                units = [(m, j) for m in range(1, LEVELS) for j in range(NT)]

                def first_product(n):
                    m, j = units[n]
                    pe.wait_ge(sem["Cm_made"], past["Cm_made"] + n + 1)
                    if m > 1:
                        pe.wait_ge(sem["TiT_new"], past["TiT_new"] + n - NT + 1)
                    else:
                        pe.wait_ge(sem["TiT_init"], past["TiT_init"] + j + 1)
                        pe.wait_ge(sem["Ti_init"], past["Ti_init"] + NT)
                        pe.wait_ge(sem["pair_masked"], past["pair_masked"] + 2 * 2 * PAIRS * NT)
                    if n >= 2:
                        pe.wait_ge(sem["X_copied"], past["X_copied"] + n - 1)
                    for h in range(GH):
                        ins = g.product(ps[:, n % 2, h * P:(h + 1) * P], Cm[:, n % 2, h, :], Ti[:, j, h, :])
                    ins.then_inc(sem["X_ready"], add("X_ready", 1))

                first_product(0)
                for n, (m, j) in enumerate(units):
                    if n + 1 < len(units):
                        first_product(n + 1)
                    pe.wait_ge(sem["X_copied"], past["X_copied"] + n + 1)
                    if n >= 2:
                        pe.wait_ge(sem["TiT_new"], past["TiT_new"] + n - 1)
                    if m < LEVELS - 1:
                        if n >= 2:
                            pe.wait_ge(sem["Ti_new"], past["Ti_new"] + n - 1)
                        for h in range(GH):
                            ins = g.product(ps[:, 2 + n % 2, h * P:(h + 1) * P], TiT[:, j, h, :], X[:, j, h, :])
                        ins.then_inc(sem["Y_ready"], add("Y_ready", 1))
                    for h in range(GH):
                        ins = g.product(ps[:, 4 + n % 2, h * P:(h + 1) * P], X[:, j, h, :], TiT[:, j, h, :])
                    ins.then_inc(sem["YT_ready"], add("YT_ready", 1))
                for j in range(NT):
                    pe.wait_ge(sem["TiT_new"], past["TiT_new"] + NT * (LEVELS - 2) + j + 1)
                    if j == 0:
                        pe.wait_ge(sem["X_copied"], past["X_copied"] + NT * (LEVELS - 1))
                        pe.wait_ge(sem["TiT_new"], past["TiT_new"] + NT * (LEVELS - 1))
                    for h in range(GH):
                        rows = slice((h % 2) * HD, (h % 2 + 1) * HD)
                        at = (h // 2) * T + j * P
                        ins = g.product(ps[rows, h // 2, j * P:(j + 1) * P], tok[:, 3, j, h * HD:(h + 1) * HD], TiT[:, j, h, :])
                    ins.then_inc(sem["WT_ready"], add("WT_ready", 1))
                    for h in range(GH):
                        ins = g.product(ps[:, 2 + j // 2, (j % 2) * GW + h * HD:(j % 2) * GW + (h + 1) * HD], MTt[:, j, h, :], tok[:, 2, j, h * HD:(h + 1) * HD])
                    ins.then_inc(sem["Mv_ready"], add("Mv_ready", 1))
                for j in range(NT):
                    pe.wait_ge(sem["Mv_copied"], past["Mv_copied"] + j + 1)
                    for h in range(GH):
                        ins = g.product(ps[:, 4 + j // 2, (j % 2) * GW + h * HD:(j % 2) * GW + (h + 1) * HD], TiT[:, j, h, :], sa[:, j, h * HD:(h + 1) * HD])
                    ins.then_inc(sem["U_ready"], add("U_ready", 1))
                pe.wait_ge(sem["WT_copied"], past["WT_copied"] + PAIRS)
                pe.wait_ge(sem["U_copied"], past["U_copied"] + NT)
                outputs = [(j, h) for j in range(NT) for h in range(GH)]

                def output(j, h):
                    cols = slice(h * HD, (h + 1) * HD)
                    rows = slice((h % 2) * HD, (h % 2 + 1) * HD)
                    bank = 4 + 2 * (j // 2) + h % 2
                    at = slice(((j % 2) * PAIRS + h // 2) * HD, ((j % 2) * PAIRS + h // 2 + 1) * HD)
                    g.product(ps[:, bank, at], RKT[:, j, h, :], tok[:, 2, j, cols], True, False, check=False)
                    g.product(ps[:, bank, at], RBT[:, j, h, :], sa[:, j, cols], False, False, check=False)
                    for half in range(2):
                        out = slice(half * C, (half + 1) * C)
                        ins = g.product(ps[out, bank, at], ar[rows, h // 2, j, 1, out], state[rows, 2 * j + half, h // 2, :], False, half == 1, check=False)
                    if h == GH - 1:
                        ins.then_inc(sem["y_ready"], add("y_ready", 1))

                for c in range(NCH):
                    j, b = c // 2, c % 2
                    toks = slice(b * C, (b + 1) * C)
                    if c:
                        pe.wait_ge(sem["state_new"], past["state_new"] + PAIRS * c)
                    for h in range(GH):
                        rows = slice((h % 2) * HD, (h % 2 + 1) * HD)
                        ins = g.product(ps[toks, h % 2, (h // 2) * HD:(h // 2 + 1) * HD], WT[rows, h // 2, c * C:(c + 1) * C], state[rows, c, h // 2, :])
                    ins.then_inc(sem["WS_ready"], add("WS_ready", 1))
                    place = [(slice(h * HD, (h + 1) * HD), ps[(h % 2) * HD:(h % 2 + 1) * HD, 2 + h // 2, 0:C]) for h in range(GH)]
                    for cols, out in place:
                        g.product(out, tok[toks, 1, j, cols], tok[toks, 2, j, cols], True, False, check=False)
                    for n in range(2 * (c - 2), 2 * (c - 1)):
                        if n >= 0:
                            output(*outputs[n])
                    pe.wait_ge(sem["sa_ready"], past["sa_ready"] + 2 * c + 2)
                    for cols, out in place:
                        ins = g.product(out, tok[toks, 0, j, cols], sa[toks, j, cols], False, True, check=False)
                    ins.then_inc(sem["S_ready"], add("S_ready", 1))
                for n in range(2 * (NCH - 2), len(outputs)):
                    output(*outputs[n])
                pe.wait_ge(sem["y_final"], past["y_final"] + NT)
                to_gated(g, pe, y, [0, 1])

            @block.scalar
            def _(act):
                for m in range(1, LEVELS):
                    for j in range(NT):
                        n = NT * (m - 1) + j
                        act.wait_ge(sem["X_ready"], past["X_ready"] + n + 1)
                        if m > 1:
                            act.wait_ge(sem["YT_ready"], past["YT_ready"] + n - NT + 1)
                        nc.scalar.activation(X[:, j], ps[:, n % 2, :].rearrange("p (h t) -> p h t", h=GH), ACT.Copy).then_inc(sem["X_copied"], add("X_copied", 1))
                act.wait_ge(sem["WT_ready"], past["WT_ready"] + NT)
                for i in range(PAIRS):
                    nc.scalar.activation(WT[:, i, :], ps[:, i, :], ACT.Copy).then_inc(sem["WT_copied"], add("WT_copied", 1))
                for j in range(NT):
                    act.wait_ge(sem["Mv_ready"], past["Mv_ready"] + j - j % 2 + 2)
                    nc.scalar.activation(sa[:, j, :], ps[:, 2 + j // 2, (j % 2) * GW:(j % 2 + 1) * GW], ACT.Copy).then_inc(sem["Mv_copied"], add("Mv_copied", 1))
                for j in range(NT):
                    act.wait_ge(sem["U_ready"], past["U_ready"] + j - j % 2 + 2)
                    nc.scalar.activation(U[:, j, :], ps[:, 4 + j // 2, (j % 2) * GW:(j % 2 + 1) * GW], ACT.Copy).then_inc(sem["U_copied"], add("U_copied", 1))
                for j in range(NT):
                    act.wait_ge(sem["y_ready"], past["y_ready"] + j - j % 2 + 2)
                    sq = RBT[:, j, 0:2, :].rearrange("p h t -> p (h t)").rearrange("p (i b d) -> p b i d", b=2, d=HD)
                    nc.scalar.activation(sq, y_in(j), ACT.Square).then_inc(sem["y_sq"], add("y_sq", 1))
                act.wait_ge(sem["y_mean_sq"], past["y_mean_sq"] + 1)
                nc.scalar.activation(ss[:], ss[:], ACT.Sqrt).then_inc(sem["y_root"], add("y_root", 1))

            @block.vector
            def _(dve):
                for j in range(NT):
                    for a, dsts in enumerate(((LT, RBT), (MTt, RKT))):
                        for i in range(PAIRS):
                            n = 2 * PAIRS * j + PAIRS * a + i
                            dve.wait_ge(sem["pair_ready"], past["pair_ready"] + n + 1)
                            both = ps[:, 2 * (n % 2):2 * (n % 2) + 2, 0:2 * P].rearrange("p b (w t) -> p b w t", w=2)
                            for w, (dst, mask) in enumerate(zip(dsts, (g.after64, g.not_before64))):
                                nc.vector.tensor_tensor(dst[:, j, 2 * i:2 * i + 2, :], both[:, :, w, :],
                                                                              mask[:].unsqueeze(1).to_broadcast([P, 2, P]), ALU.mult).then_inc(sem["pair_masked"], add("pair_masked", 1))
                    dve.wait_ge(sem["L_ready"], past["L_ready"] + j + 1)
                    wide = lambda x: x[:].unsqueeze(1).to_broadcast([P, GH, P])
                    step = "Ti_step"
                    for b in range(2):
                        nc.vector.tensor_tensor(Ti[:, j, b:GH:2, :], ps[:, 4 + 2 * (j % 2) + b, 0:PAIRS * P].rearrange("p (h t) -> p h t", h=PAIRS),
                                                        g.level1[:].unsqueeze(1).to_broadcast([P, PAIRS, P]), ALU.mult).then_inc(sem[step], add(step, 1))
                    dve.wait_ge(sem["pair_masked"], past["pair_masked"] + 2 * (2 * PAIRS * (j + 1)))
                    nc.vector.tensor_tensor(TiT[:, j], LT[:, j], wide(g.levelT[0]), ALU.mult).then_inc(sem[step], add(step, 1))
                    dve.wait_ge(sem[step], past[step] + 3 * j + 3)
                    nc.vector.tensor_tensor(Ti[:, j], wide(g.ident), Ti[:, j], ALU.subtract).then_inc(sem["Ti_init"], add("Ti_init", 1))
                    nc.vector.tensor_tensor(TiT[:, j], wide(g.ident), TiT[:, j], ALU.subtract).then_inc(sem["TiT_init"], add("TiT_init", 1))

                def mask(n):
                    m, j = n // NT + 1, n % NT
                    if n >= 2:
                        dve.wait_ge(sem["X_ready"], past["X_ready"] + n - 1)
                    nc.vector.tensor_tensor(Cm[:, n % 2], LT[:, j], g.levelT[m][:].unsqueeze(1).to_broadcast([P, GH, P]), ALU.mult).then_inc(sem["Cm_made"], add("Cm_made", 1))

                total = NT * (LEVELS - 1)
                mask(0)
                mask(1)
                for n in range(total):
                    m, j = n // NT + 1, n % NT
                    if n + 2 < total:
                        mask(n + 2)
                    if m < LEVELS - 1:
                        dve.wait_ge(sem["Y_ready"], past["Y_ready"] + n + 1)
                        if n >= NT:
                            dve.wait_ge(sem["Ti_new"], past["Ti_new"] + n - NT + 1)
                        else:
                            dve.wait_ge(sem["Ti_init"], past["Ti_init"] + NT)
                        nc.vector.tensor_tensor(Ti[:, j], Ti[:, j], ps[:, 2 + n % 2, :].rearrange("p (h t) -> p h t", h=GH), ALU.subtract).then_inc(sem["Ti_new"], add("Ti_new", 1))
                    dve.wait_ge(sem["YT_ready"], past["YT_ready"] + n + 1)
                    if n >= NT:
                        dve.wait_ge(sem["TiT_new"], past["TiT_new"] + n - NT + 1)
                    else:
                        dve.wait_ge(sem["TiT_init"], past["TiT_init"] + NT)
                    nc.vector.tensor_tensor(TiT[:, j], TiT[:, j], ps[:, 4 + n % 2, :].rearrange("p (h t) -> p h t", h=GH), ALU.subtract).then_inc(sem["TiT_new"], add("TiT_new", 1))
                for c in range(NCH):
                    j, b = c // 2, c % 2
                    toks = slice(b * C, (b + 1) * C)
                    dve.wait_ge(sem["WS_ready"], past["WS_ready"] + c + 1)
                    dve.wait_ge(sem["U_copied"], past["U_copied"] + NT)
                    for odd in range(2):
                        nc.vector.scalar_tensor_tensor(out=by_parity(sa[toks, j, :])[:, odd], scalar=-1.0, in1=by_parity(U[toks, j, :])[:, odd],
                                                                          in0=ps[toks, odd, 0:PAIRS * HD].rearrange("p (i d) -> p i d", d=HD),
                                                                          op0=ALU.mult, op1=ALU.subtract).then_inc(sem["sa_ready"], add("sa_ready", 1))
                    dve.wait_ge(sem["S_ready"], past["S_ready"] + c + 1)
                    if c:
                        dve.wait_ge(sem["state_new"], past["state_new"] + PAIRS * c)
                    for i in range(PAIRS):
                        nc.vector.scalar_tensor_tensor(out=state[:, c + 1, i, :], in0=state[:, c, i, :], scalar=end_decay[:, i, c:c + 1],
                                                                           in1=ps[:, 2 + i, 0:C], op0=ALU.mult, op1=ALU.add).then_inc(sem["state_new"], add("state_new", 1))
                for j in range(NT):
                    dve.wait_ge(sem["y_sq"], past["y_sq"] + j + 1)
                    sq = RBT[:, j, 0:2, :].rearrange("p h t -> p (h t)")
                    nc.vector.tensor_reduce(ss[:, j * GH:(j + 1) * GH], sq.rearrange("p (h d) -> p h d", d=HD), AX, ALU.add).then_inc(sem["y_sums"], add("y_sums", 1))
                dve.wait_ge(sem["y_sums"], past["y_sums"] + NT)
                nc.vector.tensor_scalar(ss[:], ss[:], 1.0 / HD, RMS_EPS, ALU.mult, ALU.add).then_inc(sem["y_mean_sq"], add("y_mean_sq", 1))
                dve.wait_ge(sem["y_root"], past["y_root"] + 1)
                nc.vector.reciprocal(ss[:], ss[:]).then_inc(sem["y_rstd"], add("y_rstd", 1))
                dve.wait_ge(sem["y_rstd"], past["y_rstd"] + 1)
                heads = lambda x: x.rearrange("p (h d) -> p h d", d=HD)
                n = 0
                for j in range(NT):
                    nc.vector.tensor_tensor(by_parity(y[:, j, :]), y_in(j),
                                                              ss[:, j * GH:(j + 1) * GH].rearrange("p (i b) -> p b i", b=2).unsqueeze(3).to_broadcast([P, 2, PAIRS, HD]), ALU.mult).then_inc(sem["y_steps"], add("y_steps", 1))
                    nc.vector.tensor_tensor(heads(sa[:, j, :]), heads(tok[:, 2, j, :]), bonus[:, j, :].unsqueeze(2).to_broadcast([P, GH, HD]), ALU.mult).then_inc(sem["y_steps"], add("y_steps", 1))
                for j in range(NT):
                    dve.wait_ge(sem["y_steps"], past["y_steps"] + 2 * j + 2)
                    nc.vector.tensor_tensor(y[:, j, :], y[:, j, :], s.gains[:, 6, :], ALU.mult).then_inc(sem["y_gain"], add("y_gain", 1))
                for j in range(NT):
                    dve.wait_ge(sem["y_gain"], past["y_gain"] + j + 1)
                    nc.vector.tensor_tensor(y[:, j, :], y[:, j, :], sa[:, j, :], ALU.add).then_inc(sem["y_final"], add("y_final", 1))
                for i in range(2):
                    dve.wait_ge(sem["y_turned"], past["y_turned"] + i + 1)
                    nc.vector.tensor_tensor(s.mixT[:, 6 + i, :], ps[:, i, :], s.zD[:, i, :], ALU.mult).then_inc(sem["y_gated"], add("y_gated", 1))

            @block.sync
            def _(sp):
                g.load_chunks(sp)
        g.sem.end_phase()


def phase_out(g, s, first):
    nc, t, ps = g.nc, g.t, g.ps
    sem, past, count, add = g.sem, g.sem.past, g.sem.count, g.sem.add
    with nc.Block("out", no_gpsimd_drain=True) as block:

        @block.tensor
        def _(pe):
            for n in range(D // CHUNK):
                bank, cols = n * CHUNK // COLS * NT, slice(n % 2 * CHUNK, (n % 2 + 1) * CHUNK)
                for c in range(2):
                    w = g.chunk(pe, first + 2 * n + c)
                    nk = w.shape[1]
                    for j in range(NT):
                        for k in range(nk):
                            ins = g.product(ps[:, bank + j, cols], s.mixT[:, c * KD + k, j * P:(j + 1) * P], w[:, k, :], c == 0 and k == 0, c == 1 and k == nk - 1)
                        ins.then_inc(sem["out_part"], add("out_part", 1))
                    g.release("out_part")

        @block.vector
        def _(dve):
            dve.wait_ge(sem["x_back"], past["x_back"] + 16)
            for n in range(D // COLS):
                for j in range(NT):
                    cols = slice(n * COLS, (n + 1) * COLS)
                    dve.wait_ge(sem["out_part"], past["out_part"] + 2 * NT * (COLS // CHUNK * (n + 1) - 1) + NT + j + 1)
                    nc.vector.tensor_tensor(s.x_back[:, j, cols], s.x_back[:, j, cols], ps[:, n * NT + j, :], ALU.add).then_inc(sem["out_added"], add("out_added", 1))

        @block.sync
        def _(sp):
            sp.dma_start(s.x_back[:], g.x_dram).then_inc(sem["x_back"], add("x_back", 16))
            g.load_chunks(sp)
            out_tiles = g.out[0].rearrange("(j p) d -> p j d", p=P)
            for n in range(D // COLS):
                for j in range(NT):
                    sp.wait_ge(sem["out_added"], past["out_added"] + n * NT + j + 1)
                    sp.dma_start(out_tiles[:, j, n * COLS:(n + 1) * COLS], s.x_back[:, j, n * COLS:(n + 1) * COLS]).then_inc(sem["out_landed"], add("out_landed", 16))
            sp.wait_ge(sem["out_landed"], past["out_landed"] + 16 * NT * (D // COLS))
    g.sem.end_phase()


def second_block(g, first):
    class Store:
        pass

    s = Store()
    with ExitStack() as kept:
        new = lambda name, shape: g.sb(kept, name, shape)
        s.mixT = new("mixT", [P, MIX_TILES, T])
        s.zD = new("zD", [P, 2, T])
        s.gains = new("gains", [P, 7, GW])
        s.w2_decay, s.w2_a = new("w2_decay", [RANK2, GW]), new("w2_a", [RANK2, GW])
        with ExitStack() as raw:
            s.raw = g.sb(raw, "raw", [P, 8, T + 1])
            s.low = g.sb(raw, "low", [RANK2, 2, T + 1])
            with ExitStack() as mid:
                new = lambda name, shape: g.sb(mid, name, shape)
                s.zT = new("zT", [P, 8, T])
                s.heads = new("heads", [P, NT, 5, GW])
                s.vB = new("vB", [P, NT, GW])
                s.gates, s.gate_bias = new("gates", [P, NT, GATES]), new("gate_bias", [P, GATES])
                s.conv_in = new("conv_in", [P, 4, CONV_K - 1 + T])
                s.vC = new("vC", [P, NT, GH, HD + 1])
                s.o_sig = new("o_sig", [P, NT, GW])
                s.mem_kv = new("mem_kv", [P, MT, 2 * GW])
                s.w_sgu = new("w_sgu", [P, GH, P])
                phase_project(g, s, first)
                g.x_stack.close()
                s.shifted = g.sb(kept, "shifted", [P, 8, T], side="right")
                s.w_sguT = g.room[:, 0, 2, :].rearrange("p (h t) -> p h t", h=GH)
                s.cum = new("cum", [P, NT, 2 * GH])
                s.a_tok = new("a_tok", [P, NT, GH])
                s.qkT = new("qkT", [P, 4, T])
                s.fox_qk = new("fox_qk", [P, NT, 2, GH, HD + 2])
                phase_heads(g, s)
                phase_sgu(g, s)
                phase_fox(g, s)
                phase_mem(g, s)
                phase_mlstm(g, s)
            g.load_limit += RING
            phase_rwkv(g, s)
        g.load_limit = len(g.chunks)
        s.x_back = g.sb(kept, "x_back", [P, NT, D])
        phase_out(g, s, first + len(SECOND_CHUNKS) + 2 * GW // CHUNK)


def build(nc, t, out, upto=99, dump=None):
    g = Program(nc, t, out)
    with g.ctx:
        sb = lambda name, shape: g.sb(g.ctx, name, shape)
        sb_typed = lambda name, shape, dtype: g.sb(g.ctx, name, shape, dtype)
        g.make_ring(sb_typed)
        g.room = g.alias("branch_room", [P, 3, KD, COLS], F32, g.ring_at)
        names = ("ident", "ones", "not_before", "after", "same64", "not_before64", "after64")
        g.ident, g.ones, g.not_before, g.after, g.same64, g.not_before64, g.after64 = (sb(name, [P, P]) for name in names)
        g.keep_state = sb("keep_state", [P, T])
        g.cols = sb("cols", [P, P])
        g.level1 = sb("level1", [P, P])
        g.levelT = [sb(f"levelT{i}", [P, P]) for i in range(6)]
        g.x_stack = g.ctx.enter_context(ExitStack())
        g.xT = [g.sb(g.x_stack, f"xT_{part}", [P, KD, T], F32R, side="right") for part in ("high", "low")]
        rope_stack = g.ctx.enter_context(ExitStack())
        g.idx_cos, g.idx_sin = (g.sb(rope_stack, n, [P, T]) for n in ("idx_cos", "idx_sin"))
        g.head_cos, g.head_sin = (g.sb(rope_stack, n, [2 * HALF, T]) for n in ("head_cos", "head_sin"))
        g.x_dram = nc.dram_tensor("x_scratch", [P, NT, D], F32, kind="Internal").ap()
        g.ps = g.ctx.enter_context(nc.psum_tensor("ps", [P, 8, COLS], F32))
        g.vec_rows, at = [], {}
        row = 0

        def vec(name, view, width=P):
            nonlocal row
            rows = view.shape[0]
            g.vec_rows.append((name, view, row, rows, width))
            at[name] = (row, rows)
            row += rows

        def rows_of(v):
            return v.rearrange("a (f p) -> (a f) p", p=P)

        vec("gla_gn_g", rows_of(t["gla_gn_g"]))
        vec("norm_g_2", rows_of(t["norm_g_2"]))
        vec("mem_norm_g_2", rows_of(t["mem_norm_g_2"]))
        vec("conv_w", t["mlstm_conv_w_2"][0].rearrange("a (f p) -> (a f) p", p=P))
        vec("conv_b", rows_of(t["mlstm_conv_b_2"]))
        mu = t["rwkv_mu_2"]
        for name, a, n in (("mu", 0, 1), ("mu_k", GW + RANK2, 2), ("mu_z", 3 * GW + 2 * RANK2, 1)):
            vec(name, rows_of(mu[:, a:a + n * GW]))
        at["mu"] = (at["mu"][0], 4 * GW // P)
        vec("mu_wlo", mu[:, GW:GW + RANK2], RANK2)
        vec("mu_alo", mu[:, 3 * GW + RANK2:3 * GW + 2 * RANK2], RANK2)
        for name in ("w0", "a0", "k_k", "k_a"):
            vec(name, rows_of(t[f"rwkv_{name}_2"]))
        vec("r_k", t["rwkv_r_k_2"].rearrange("a (i h) d -> (a i) (h d)", h=2))
        vec("sgu_b", t["sgu_b_2"][0])
        g.col = lambda name: g.cols[:, at[name][0]:at[name][0] + at[name][1]]

        w = t["gla_w_in"][0]
        qk = GLA_HEADS * GLA_DK
        gla_first = g.add_chunks(w, 2 * qk, 2 * qk + DI)
        g.add_chunks(w, 0, 2 * qk)
        g.add_chunks(w, 2 * qk + DI, 2 * qk + 2 * DI)
        post_first = [g.add_chunks(t["gla_w_out"][0], 0, D)]
        g.add_chunks(t["ple_gate_w"][0], 0, D)
        w = t["dsa_w_in"][0]
        dq, dkv = DSA_HEADS * DH, 2 * DH
        qi = 2 * dq + dkv
        ki = qi + IDX_HEADS * IDX_DIM
        dsa_first = g.add_chunks(w, dq, dq + dkv)
        g.add_chunks(w, qi, ki)
        g.add_chunk(w, [(ki, ki + IDX_DIM), (ki, ki + IDX_DIM), (ki + IDX_DIM, w.shape[1])])
        g.add_chunks(w, 0, dq)
        g.add_chunks(w, dq + dkv, 2 * dq + dkv)
        post_first.append(g.add_chunks(t["dsa_w_out"][0], 0, D))
        g.add_chunks(t["ple_gate_w"][1], 0, D)
        second_first = len(g.chunks)
        for name in SECOND_CHUNKS:
            g.add_chunk(t["w_in_2"][0], SECOND_CHUNKS[name])
        g.add_chunks(t["mem_w_kv_2"][0], 0, 2 * GW, split=False)
        g.load_limit = len(g.chunks)
        g.add_chunks(t["w_out_2"][0], 0, D, split=False)
        phase_load(g)
        with ExitStack() as stack:
            mix_at = g.address()
            mix_a, mix_b = (g.sb(stack, f"mix_{n}", [P, KI, T]) for n in "ab")
            gT = [g.alias(f"gT_{part}", [P, KI, T], F32R, mix_at + 4 * KI * T * i) for i, part in enumerate(("high", "low"))]
            if upto >= 1:
                phase_gla(g, mix_a, mix_b, gT, gla_first)
            if upto >= 2:
                phase_post(g, 0, gT, post_first[0], False, mix_at)
            if upto >= 3:
                phase_dsa(g, mix_a, mix_b, gT, dsa_first)
            if upto >= 4:
                phase_post(g, 1, gT, post_first[1], True, mix_at)
        rope_stack.close()
        if upto >= 5:
            second_block(g, second_first)
        if dump:
            dump(g)


_INS = ["x", "p", "positions", "gla_w_in", "gla_w_a2", "gla_b_a", "gla_gn_g", "gla_w_out", "dsa_w_in", "dsa_w_out", "ln_g", "ln_b", "ple_w",
        "ple_gate_w", "mem_2", "norm_g_2", "w_in_2", "w_out_2", "sgu_norm_g_2", "sgu_w_2", "sgu_b_2", "fox_q_g_2", "fox_k_g_2", "fox_f_b_2",
        "mlstm_conv_w_2", "mlstm_conv_b_2", "mlstm_i_b_2", "mlstm_f_b_2", "mlstm_out_g_2", "rwkv_mu_2", "rwkv_w0_2", "rwkv_w2_2", "rwkv_a0_2",
        "rwkv_a2_2", "rwkv_k_k_2", "rwkv_k_a_2", "rwkv_r_k_2", "rwkv_ln_g_2", "mem_norm_g_2", "mem_w_kv_2", "mem_q_g_2", "mem_k_g_2"]


def kernel(**inputs):
    import numpy as _np
    import concourse.bacc as _bacc
    from concourse import mybir as _mybir
    from concourse.bass_utils import run_bass_kernel_spmd as _run

    nc = _bacc.Bacc("TRN2", target_bir_lowering=False, num_devices=1)
    arrays, tensors = {}, {}
    for name in _INS:
        a = _np.ascontiguousarray(inputs[name])
        arrays[f"in_{name}_dram"] = a
        tensors[name] = nc.dram_tensor(f"in_{name}_dram", a.shape, _mybir.dt.from_np(a.dtype), kind="ExternalInput").ap()
    out = nc.dram_tensor("out_0_dram", (1, T, D), _mybir.dt.float32, kind="ExternalOutput").ap()
    build(nc, tensors, out)
    r = _run(nc, [arrays], core_ids=[0])
    return r.results[0]["out_0_dram"]
```

```python
from contextlib import ExitStack

import numpy as np
import concourse.bass as bass
from concourse import mybir
from concourse.alu_op_type import AluOpType as ALU

F32 = mybir.dt.float32
F32R = mybir.dt.float32r
I32 = mybir.dt.int32
U32 = mybir.dt.uint32
ACT = mybir.ActivationFunctionType
AX = mybir.AxisListType.X

P = 128
T = 512
NT = T // P
D = 1024
KD = D // P
DI = 2048
KI = DI // P
COLS = 512
SEMAPHORES = 140
CHUNK = 256
RING = 2
DEPTH = 2
ALPHA = (2 * DEPTH) ** 0.25
LN_EPS = 1e-5
RMS_EPS = 1e-6

GLA_HEADS, GLA_DK, GLA_DV, GLA_RANK, GLA_CHUNK, GATE_NORM = 4, 256, 512, 16, 64, 16.0
NCH = T // GLA_CHUNK


class Semaphores(dict):

    def __init__(self, nc, ctx):
        self.nc, self.ctx = nc, ctx
        self.count = {}
        self.past = {}
        self.idle = {}

    def __missing__(self, name):
        if name in self.idle:
            made = self.idle.pop(name)
        elif len(self) + len(self.idle) < SEMAPHORES:
            made = self.ctx.enter_context(self.nc.semaphore(name)), 0
        else:
            made = self.idle.pop(next(iter(self.idle)))
        self[name], self.past[name] = made
        self.count[name] = self.past[name]
        return self[name]

    def add(self, name, n):
        self.count[name] += n
        return n

    def end_phase(self):
        for name in self:
            self.idle[name] = self[name], self.count[name]
        self.clear()


class Program:
    def __init__(self, nc, t, out):
        self.nc, self.t, self.out = nc, t, out
        self.ctx = ExitStack()
        self.sem = Semaphores(nc, self.ctx)

    def sb(self, stack, name, shape, dtype=F32, side="left"):
        return stack.enter_context(self.nc.sbuf_tensor(name, shape, dtype, side=side))

    def alias(self, name, shape, dtype, offset):
        return self.nc.alloc_sbuf_tensor_at(name, shape, dtype, offset=offset)

    def address(self):
        return -(-self.nc.sbuf_base // 32) * 32


    def make_ring(self, sb):
        self.ring_at = self.address()
        self.w_high = sb("w_high", [P, RING, KD, CHUNK], F32R)
        self.w_low = sb("w_low", [P, RING, KD, CHUNK], F32R)
        self.w_ring = sb("w_ring", [P, RING, KD, CHUNK], F32)
        self.w_landed = [self.ctx.enter_context(self.nc.semaphore(f"w_landed{i}")) for i in range(RING)]
        self.w_high_made, self.w_low_made = (self.ctx.enter_context(self.nc.semaphore(n)) for n in ("w_high_made", "w_low_made"))
        self.landed_count = [0] * RING
        self.chunks = []
        self.splits = []
        self.chunk_used = []
        self.loaded = self.highs = self.lows = 0
        self.load_limit = 0

    def add_chunk(self, w, ranges, row=0, split=True, most=D):
        rows = min(most, w.shape[0] - row)
        sources, at = [], 0
        for a, b in ranges:
            sources.append((w[row:row + rows, a:b].rearrange("(k p) n -> p k n", p=P), at, b - a))
            at += b - a
        n = len(self.chunks)
        self.landed_count[n % RING] += 16 * len(sources)
        self.chunks.append((sources, rows // P, at, len(self.splits) if split else None, self.landed_count[n % RING]))
        if split:
            self.splits.append(n)
        return n

    def add_chunks(self, w, a, b, split=True, most=D):
        first = len(self.chunks)
        for c in range(a, b, CHUNK):
            for row in range(0, w.shape[0], most):
                self.add_chunk(w, [(c, min(c + CHUNK, b))], row, split, most)
        return first

    def release(self, name):
        self.chunk_used.append((self.sem[name], self.sem.count[name]))

    def load_chunks(self, sp, upto=None):
        upto = min(len(self.chunk_used) + 2 * RING, self.load_limit, len(self.chunks) if upto is None else upto)
        for n in range(self.loaded, upto):
            sources, k, _, _, _ = self.chunks[n]
            if n >= RING:
                split = self.chunks[n - RING][3]
                if split is not None:
                    if split >= self.highs:
                        break
                    sp.wait_ge(self.w_low_made, split + 1)
                else:
                    if n - RING >= len(self.chunk_used):
                        break
                    used, products = self.chunk_used[n - RING]
                    sp.wait_ge(used, products)
            for src, at, cols in sources:
                sp.dma_start(self.w_ring[:, n % RING, 0:k, at:at + cols], src).then_inc(self.w_landed[n % RING], 16)
            self.loaded = n + 1

    def split_high(self, act, upto):
        while self.highs < len(self.splits) and self.splits[self.highs] < min(upto, self.load_limit):
            i, n = self.highs, self.splits[self.highs]
            _, k, cols, _, landed = self.chunks[n]
            act.wait_ge(self.w_landed[n % RING], landed)
            if i >= RING:
                used, products = self.chunk_used[self.splits[i - RING]]
                act.wait_ge(used, products)
            self.nc.scalar.activation(self.w_high[:, i % RING, 0:k, 0:cols], self.w_ring[:, n % RING, 0:k, 0:cols], ACT.Copy).then_inc(self.w_high_made, 1)
            self.highs += 1

    def split_low(self, pool, upto=None):
        while self.lows < self.highs and (upto is None or self.splits[self.lows] < upto):
            i, n = self.lows, self.splits[self.lows]
            _, k, cols, _, _ = self.chunks[n]
            pool.wait_ge(self.w_high_made, i + 1)
            self.nc.gpsimd.tensor_tensor(self.w_low[:, i % RING, 0:k, 0:cols], self.w_ring[:, n % RING, 0:k, 0:cols],
                                         self.w_high[:, i % RING, 0:k, 0:cols].bitcast(F32), ALU.subtract).then_inc(self.w_low_made, 1)
            self.lows += 1

    def chunk(self, pe, n):
        _, k, cols, split, landed = self.chunks[n]
        if split is None:
            pe.wait_ge(self.w_landed[n % RING], landed)
            return self.w_ring[:, n % RING, 0:k, 0:cols]
        pe.wait_ge(self.w_low_made, split + 1)
        return [w[:, split % RING, 0:k, 0:cols] for w in (self.w_high, self.w_low)]


    def product(self, out, lhs, rhs, first=True, last=True, check=True):
        return self.nc.tensor.matmul(out, lhs, rhs, start=first, stop=last, skip_group_check=not check)

    def split_product(self, out, lhs, rhs, first, last):
        (lhs_high, lhs_low), (rhs_high, rhs_low) = lhs, rhs
        self.product(out, lhs_high, rhs_high, first, False)
        self.product(out, lhs_high, rhs_low, False, False)
        return self.product(out, lhs_low, rhs_high, False, last)


def to_feature_major_pe(g, pe, before, src, nk, nt, banks):
    nc, turned = g.nc, "turned"
    sem, past, add = g.sem, g.sem.past, g.sem.add
    done = ["turned_by_act", "turned_by_dve"]
    nb = len(banks)
    for k in range(nk):
        if k >= nb:
            q = k - nb
            pe.wait_ge(sem[done[q % 2]], past[done[q % 2]] + before[q % 2] + q // 2 + 1)
        for j in range(nt):
            ins = nc.tensor.transpose(g.ps[:, banks[k % nb], j * P:(j + 1) * P], src[:, j, k * P:(k + 1) * P], g.ident[:])
        ins.then_inc(sem[turned], add(turned, 1))


def to_feature_major_act(g, act, seen, dst, nk, n, banks, scale=None):
    sem, past, add = g.sem, g.sem.past, g.sem.add
    for k in range(0, nk, 2):
        act.wait_ge(sem["turned"], past["turned"] + seen + k + 1)
        s = 1.0 if scale is None else scale[:, k:k + 1]
        g.nc.scalar.activation(dst[:, k, 0:n], g.ps[:, banks[k % len(banks)], 0:n], ACT.Copy, scale=s).then_inc(sem["turned_by_act"], add("turned_by_act", 1))


def to_feature_major_dve(g, dve, seen, dst, nk, n, banks, scale=None):
    sem, past, add = g.sem, g.sem.past, g.sem.add
    for k in range(1, nk, 2):
        dve.wait_ge(sem["turned"], past["turned"] + seen + k + 1)
        src = g.ps[:, banks[k % len(banks)], 0:n]
        if scale is None:
            ins = g.nc.vector.tensor_copy(dst[:, k, 0:n], src)
        else:
            ins = g.nc.vector.tensor_scalar(dst[:, k, 0:n], src, scale[:, k:k + 1], None, ALU.mult)
        ins.then_inc(sem["turned_by_dve"], add("turned_by_dve", 1))


def columns(parts, k, cols=slice(None)):
    return [part[:, k, cols] for part in parts]


def split_feature_major_pe(g, pe, before, src, nk, nt, banks):
    sem, past, add = g.sem, g.sem.past, g.sem.add
    nb = len(banks)
    for k in range(nk):
        if k >= nb:
            pe.wait_ge(sem["turned_low"], past["turned_low"] + before + k - nb + 1)
        for j in range(nt):
            ins = g.nc.tensor.transpose(g.ps[:, banks[k % nb], j * P:(j + 1) * P], src[:, j, k * P:(k + 1) * P], g.ident[:])
        ins.then_inc(sem["turned_whole"], add("turned_whole", 1))


def split_feature_major_act(g, act, before, dst, nk, banks, scale=None):
    sem, past, add = g.sem, g.sem.past, g.sem.add
    for k in range(nk):
        act.wait_ge(sem["turned_whole"], past["turned_whole"] + before + k + 1)
        s = 1.0 if scale is None else scale[:, k:k + 1]
        g.nc.scalar.activation(dst[0][:, k, :], g.ps[:, banks[k % len(banks)], :], ACT.Copy, scale=s).then_inc(sem["turned_high"], add("turned_high", 1))


def split_feature_major_dve(g, dve, before, dst, nk, banks, scale=None):
    sem, past, add = g.sem, g.sem.past, g.sem.add
    for k in range(nk):
        dve.wait_ge(sem["turned_high"], past["turned_high"] + before + k + 1)
        s = 1.0 if scale is None else scale[:, k:k + 1]
        g.nc.vector.scalar_tensor_tensor(out=dst[1][:, k, :], in0=g.ps[:, banks[k % len(banks)], :], scalar=s, in1=dst[0][:, k, :].bitcast(F32),
                                         op0=ALU.mult, op1=ALU.subtract).then_inc(sem["turned_low"], add("turned_low", 1))


def phase_load(g):
    nc, t, ps = g.nc, g.t, g.ps
    NFQ = HALF + IDX_HALF
    sem, past, count, add = g.sem, g.sem.past, g.sem.count, g.sem.add
    x_landed, const_made, vecs_landed = "x_landed", "const_made", "vecs_landed"
    vecs_cleared, cols_turned, cols_made = "vecs_cleared", "cols_turned", "cols_made"
    banks = [0, 1, 2, 3, 4, 5]
    x_tiles = t["x"][0].rearrange("(j p) d -> p j d", p=P)
    with ExitStack() as stack:
        x_tok = g.sb(stack, "x_tok", [P, NT, D])
        vec_rows = g.sb(stack, "vec_rows", [P, P])
        pos_i = g.sb(stack, "pos_i", [P, NT], I32)
        pos = g.sb(stack, "pos", [P, NT])
        freq = g.sb(stack, "freq", [P, NFQ])
        angle = g.sb(stack, "angle", [P, NT, NFQ])
        turns = g.sb(stack, "turns", [P, NT, NFQ])
        wrap = g.sb(stack, "wrap", [P, NT, NFQ])
        both = g.sb(stack, "both", [P, 2, NT, NFQ])
        tab = g.sb(stack, "tab", [P, NT, 2 * P + 4 * HALF])
        idx_c, idx_s = tab[:, :, 0:P], tab[:, :, P:2 * P]
        head_c, head_s = tab[:, :, 2 * P:2 * P + 2 * HALF], tab[:, :, 2 * P + 2 * HALF:]
        with nc.Block("load", no_gpsimd_drain=True) as block:

            @block.sync
            def _(sp):
                sp.dma_start(pos_i[:], t["positions"][0].rearrange("(j p) -> p j", p=P), allow_slow_non_contiguous=True).then_inc(sem["pos_landed"], add("pos_landed", 16))
                for j in range(NT):
                    sp.dma_start(x_tok[:, j, :], x_tiles[:, j, :]).then_inc(sem[x_landed], add(x_landed, 16))
                g.load_chunks(sp)

            @block.scalar
            def _(act):
                act.wait_ge(sem[vecs_cleared], past[vecs_cleared] + 1)
                for name, view, row, rows, width in g.vec_rows:
                    act.dma_start(vec_rows[row:row + rows, 0:width], view).then_inc(sem[vecs_landed], add(vecs_landed, 16))
                act.wait_ge(sem["angles"], past["angles"] + 1)
                act.wait_ge(sem["rope_step"], count["rope_step"])
                nc.scalar.activation(both[:], both[:], ACT.Sin).then_inc(sem["sines"], add("sines", 1))
                split_feature_major_act(g, act, 0, g.xT, KD, banks)
                g.split_high(act, RING)

            @block.vector
            def _(dve):
                nc.vector.memset(vec_rows[:], 0.0).then_inc(sem[vecs_cleared], add(vecs_cleared, 1))
                step = "rope_step"

                def then(ins):
                    ins.then_inc(sem[step], add(step, 1))
                    dve.wait_ge(sem[step], count[step])

                for i, f in enumerate(inverse_frequencies()):
                    nc.vector.memset(freq[:, i:i + 1], f).then_inc(sem[step], add(step, 1))
                nc.vector.memset(tab[:, :, 0:P], 1.0).then_inc(sem[step], add(step, 1))
                nc.vector.memset(tab[:, :, P:2 * P], 0.0).then_inc(sem[step], add(step, 1))
                dve.wait_ge(sem["pos_landed"], past["pos_landed"] + 16)
                then(nc.vector.tensor_copy(pos[:], pos_i[:]))
                for j in range(NT):
                    then(nc.vector.tensor_scalar(angle[:, j, :], freq[:], pos[:, j:j + 1], None, ALU.mult))
                then(nc.vector.tensor_scalar(turns[:], angle[:], 1.0 / (2.0 * np.pi), None, ALU.mult))
                then(nc.vector.tensor_scalar(turns[:], turns[:], ROUND, None, ALU.add))
                then(nc.vector.tensor_scalar(turns[:], turns[:], ROUND, None, ALU.subtract))
                for part in TWO_PI_PARTS:
                    then(nc.vector.scalar_tensor_tensor(out=angle[:], in0=turns[:], scalar=-part, in1=angle[:], op0=ALU.mult, op1=ALU.add))
                then(nc.vector.tensor_scalar(both[:, 0], angle[:], np.pi / 2, None, ALU.add))
                then(nc.vector.tensor_scalar(wrap[:], both[:, 0], np.pi, -2.0 * np.pi, ALU.is_gt, ALU.mult))
                then(nc.vector.tensor_tensor(both[:, 0], both[:, 0], wrap[:], ALU.add))
                nc.vector.tensor_scalar(both[:, 0], both[:, 0], 3.1415925, -3.1415925, ALU.min, ALU.max).then_inc(sem[step], add(step, 1))
                nc.vector.tensor_scalar(both[:, 1], angle[:], 3.1415925, -3.1415925, ALU.min, ALU.max).then_inc(sem["angles"], add("angles", 1))
                blocks = "same64_made"
                nc.vector.memset(g.same64[:], 0.0).then_inc(sem[blocks], add(blocks, 1))
                nc.vector.memset(g.keep_state[:], 1.0).then_inc(sem[blocks], add(blocks, 1))
                dve.wait_ge(sem[blocks], past[blocks] + 2)
                for b in range(2):
                    nc.vector.memset(g.same64[64 * b:64 * b + 64, 64 * b:64 * b + 64], 1.0).then_inc(sem[blocks], add(blocks, 1))
                nc.vector.memset(g.keep_state[:].rearrange("p (c i) -> p c i", i=GLA_CHUNK)[:, :, 0:1], 0.0).then_inc(sem[blocks], add(blocks, 1))
                dve.wait_ge(sem[blocks], past[blocks] + 5)
                dve.wait_ge(sem[const_made], past[const_made] + 5)
                for out, m in ((g.not_before64, g.not_before), (g.after64, g.after)):
                    nc.vector.tensor_tensor(out[:], m[:], g.same64[:], ALU.mult).then_inc(sem["masks64"], add("masks64", 1))
                dve.wait_ge(sem["sines"], past["sines"] + 1)
                cos, sin = both[:, 0], both[:, 1]
                for out, src, f0, n, sign in ((head_c, cos, 0, HALF, 1.0), (head_s, sin, 0, HALF, -1.0)):
                    nc.vector.tensor_scalar(out[:, :, 0:n], src[:, :, f0:f0 + n], sign, None, ALU.mult).then_inc(sem["tables"], add("tables", 1))
                    nc.vector.tensor_copy(out[:, :, n:2 * n], src[:, :, f0:f0 + n]).then_inc(sem["tables"], add("tables", 1))
                for b in range(0, P, IDX_DIM):
                    for out, src, sign in ((idx_c, cos, 1.0), (idx_s, sin, -1.0)):
                        n = IDX_HALF
                        nc.vector.tensor_scalar(out[:, :, b:b + n], src[:, :, HALF:HALF + n], sign, None, ALU.mult).then_inc(sem["tables"], add("tables", 1))
                        nc.vector.tensor_copy(out[:, :, b + n:b + 2 * n], src[:, :, HALF:HALF + n]).then_inc(sem["tables"], add("tables", 1))
                split_feature_major_dve(g, dve, 0, g.xT, KD, banks)
                dve.wait_ge(sem[cols_turned], past[cols_turned] + 1)
                nc.vector.tensor_copy(g.cols[:], g.ps[:, 6, 0:P]).then_inc(sem[cols_made], add(cols_made, 1))
                dve.wait_ge(sem["tables_turned"], past["tables_turned"] + 1)
                for i, dst in enumerate((g.idx_cos, g.idx_sin)):
                    nc.vector.tensor_copy(dst[:], ps[:, i, :]).then_inc(sem["tables_copied"], add("tables_copied", 1))
                for i, dst in enumerate((g.head_cos, g.head_sin)):
                    nc.vector.tensor_copy(dst[:], ps[0:2 * HALF, 2 + i, :]).then_inc(sem["tables_copied"], add("tables_copied", 1))

            @block.tensor
            def _(pe):
                pe.wait_ge(sem[const_made], past[const_made] + 3)
                pe.wait_ge(sem[x_landed], past[x_landed] + 16 * NT)
                split_feature_major_pe(g, pe, 0, x_tok, KD, NT, banks)
                pe.wait_ge(sem[vecs_landed], past[vecs_landed] + 16 * len(g.vec_rows))
                nc.tensor.transpose(g.ps[:, 6, 0:P], vec_rows[:], g.ident[:]).then_inc(sem[cols_turned], add(cols_turned, 1))
                pe.wait_ge(sem["turned_low"], past["turned_low"] + KD)
                pe.wait_ge(sem["tables"], past["tables"] + 12)
                for i, src in enumerate((idx_c, idx_s, head_c, head_s)):
                    n = src.shape[2]
                    for j in range(NT):
                        ins = nc.tensor.transpose(ps[0:n, i, j * P:(j + 1) * P], src[:, j, :], g.ident[:])
                ins.then_inc(sem["tables_turned"], add("tables_turned", 1))

            @block.gpsimd
            def _(pool):
                nc.gpsimd.memset(g.ident[:], 0.0).then_inc(sem[const_made], add(const_made, 1))
                nc.gpsimd.memset(g.ones[:], 1.0).then_inc(sem[const_made], add(const_made, 1))
                pool.wait_ge(sem[const_made], past[const_made] + 2)
                nc.gpsimd.affine_select(out=g.ident[:], in_=g.ident[:], compare_op=ALU.not_equal, fill=1.0, base=0,
                                                      pattern=[[-1, P]], channel_multiplier=1).then_inc(sem[const_made], add(const_made, 1))
                for out, base, cm, step in ((g.not_before, 0, -1, 1), (g.after, -1, -1, 1)):
                    nc.gpsimd.affine_select(out=out[:], in_=g.ones[:], compare_op=ALU.is_ge, fill=0.0, base=base,
                                                          pattern=[[step, P]], channel_multiplier=cm).then_inc(sem[const_made], add(const_made, 1))

                for i, mask in enumerate(g.levelT + [g.level1]):
                    m = 2 ** i if i < len(g.levelT) else 1
                    n = P // (2 * m)
                    view = mask[:].rearrange("p (b x) -> p b x", x=2 * m)
                    up = 0 if i < len(g.levelT) else 1
                    for a, (base, cm, pattern) in enumerate(((-up * m, 1, [[-2 * m, n], [0, 2 * m]]), (up * m + m - 1, -1, [[2 * m, n], [0, 2 * m]]),
                                                            ((up - 1) * m, 0, [[0, n], [1 - 2 * up, 2 * m]]))):
                        src = g.ones[:].rearrange("p (b x) -> p b x", x=2 * m) if a == 0 else view
                        nc.gpsimd.affine_select(out=view, in_=src, compare_op=ALU.is_ge, fill=0.0, base=base, pattern=pattern, channel_multiplier=cm).then_inc(sem[const_made], add(const_made, 1))
                        pool.wait_ge(sem[const_made], count[const_made])
                g.split_low(pool)
    g.sem.end_phase()


def phase_gla(g, mix_a, mix_b, gT, first):
    nc, t = g.nc, g.t
    sem, past, count, add = g.sem, g.sem.past, g.sem.count, g.sem.add
    NF = GLA_HEADS * GLA_DK // P
    DT = GLA_DK // P
    with ExitStack() as stack:
        w_a = g.sb(stack, "w_a", [P, KD, GLA_RANK])
        w_a_parts = [g.sb(stack, f"w_a_{part}", [P, KD, GLA_RANK], F32R) for part in ("high", "low")]
        w_a2_room = g.sb(stack, "w_a2", [P, GLA_HEADS * GLA_DK])
        w_a2 = w_a2_room[0:GLA_RANK + 1, :]
        aT = g.sb(stack, "aT", [GLA_RANK + 1, T])
        decay_log = mix_b[:, 0:NF, :]
        ks_tok = mix_b[:, NF:, :].rearrange("p (j a) t -> p j (a t)", j=NT)
        v_tok = g.sb(stack, "v_tok", [P, NT, DI])
        chunk_decay = g.sb(stack, "chunk_decay", [P, NF, NCH])
        to_end = g.sb(stack, "to_end", [P, 2, T])
        attn = w_a2_room[:, 0:GLA_HEADS * P].rearrange("p (h s) -> p h s", h=GLA_HEADS)
        sq = w_a2_room[:, GLA_DV:2 * GLA_DV]
        sumsq = g.sb(stack, "sumsq", [P, NT * GLA_HEADS])
        root = g.sb(stack, "root", [P, NT * GLA_HEADS])
        rstd = g.sb(stack, "rstd", [P, NT * GLA_HEADS])
        z_silu = to_end
        qT, kT = mix_a[:, 0:NF, :], mix_a[:, NF:2 * NF, :]
        state = decay_log
        ps = g.ps
        HALVES = COLS // CHUNK
        c_v = first
        c_q = c_v + DI // CHUNK
        c_z = c_q + 2 * NF * P // CHUNK
        end = c_z + DI // CHUNK
        small_landed = "small_landed"
        w_in = t["gla_w_in"][0]
        a0 = 2 * GLA_HEADS * GLA_DK + 2 * DI

        with nc.Block("gla", no_gpsimd_drain=True) as block:

            @block.tensor
            def _(pe):
                def low_rank():
                    pe.wait_ge(sem[small_landed], past[small_landed] + 48)
                    pe.wait_ge(sem["w_a_split"], past["w_a_split"] + 2)
                    for k in range(KD):
                        ins = g.split_product(ps[0:GLA_RANK, 4, :], columns(w_a_parts, k), columns(g.xT, k), k == 0, k == KD - 1)
                    ins.then_inc(sem["aT_ready"], add("aT_ready", 1))

                def gates(b):
                    pe.wait_ge(sem["aT_copied"], past["aT_copied"] + 2)
                    for i in range(4):
                        if b:
                            pe.wait_ge(sem["log_gate"], past["log_gate"] + i + 1)
                        f = 4 * b + i
                        g.product(ps[:, 4 + i, :], w_a2[:, f * P:(f + 1) * P], aT[:]).then_inc(sem["u_ready"], add("u_ready", 1))

                for c in range(4):
                    for half in range(HALVES):
                        w = g.chunk(pe, c_v + HALVES * c + half)
                        done = "v_ready" if half == HALVES - 1 else "v_half"
                        for j in range(NT):
                            n = 4 * c + j
                            if half == 0 and n >= 4:
                                pe.wait_ge(sem["v_copied"], past["v_copied"] + n - 3)
                            for k in range(KD):
                                ins = g.split_product(ps[:, n % 4, half * CHUNK:(half + 1) * CHUNK], columns(g.xT, k, slice(j * P, (j + 1) * P)),
                                                      columns(w, k), k == 0, k == KD - 1)
                            ins.then_inc(sem[done], add(done, 1))
                        g.release(done)
                    if c == 0:
                        low_rank()
                    elif c < 3:
                        gates(c - 1)
                pe.wait_ge(sem["v_copied"], past["v_copied"] + 16)
                pe.wait_ge(sem["log_gate"], past["log_gate"] + 8)

                def turn_ks(f):
                    pe.wait_ge(sem["ks_made"], past["ks_made"] + f + 1)
                    if f >= 2:
                        pe.wait_ge(sem["ks_copied"], past["ks_copied"] + f - 1)
                    for j in range(NT):
                        ins = nc.tensor.transpose(ps[:, 6 + f % 2, j * P:(j + 1) * P], to_end[:, f % 2, j * P:(j + 1) * P], g.ident[:])
                    ins.then_inc(sem["ks_turned"], add("ks_turned", 1))

                for n in range(2 * NF):
                    if n % 2 == 0:
                        w = g.chunk(pe, c_q + n // 2)
                    if n >= 6:
                        pe.wait_ge(sem["qk_used"], past["qk_used"] + n - 5)
                    for k in range(KD):
                        ins = g.split_product(ps[:, n % 6, :], columns(w, k, slice((n % 2) * P, (n % 2 + 1) * P)), columns(g.xT, k), k == 0, k == KD - 1)
                    ins.then_inc(sem["qk_ready"], add("qk_ready", 1))
                    if n % 2 == 1:
                        g.release("qk_ready")
                    if n > NF:
                        turn_ks(n - NF - 1)
                turn_ks(NF - 1)

                pe.wait_ge(sem["qk_used"], past["qk_used"] + 2 * NF)
                pe.wait_ge(sem["ks_copied"], past["ks_copied"] + NF)
                update = 0
                for j in range(NT):
                    tile = slice(j * P, (j + 1) * P)
                    if j:
                        pe.wait_ge(sem["attn_masked"], past["attn_masked"] + j)
                    for h in range(GLA_HEADS):
                        for d in range(DT):
                            ins = g.product(ps[:, 7, h * P:(h + 1) * P], kT[:, DT * h + d, tile], qT[:, DT * h + d, tile],
                                            d == 0, d == DT - 1)
                    ins.then_inc(sem["attn_ready"], add("attn_ready", 1))
                    pe.wait_ge(sem["attn_masked"], past["attn_masked"] + j + 1)
                    for h in range(GLA_HEADS):
                        if j:
                            pe.wait_ge(sem["o_copied"], past["o_copied"] + 2 * (4 * (j - 1) + h) + 2)
                        ins = g.product(ps[:, h, :], attn[:, h, :], v_tok[:, j, h * GLA_DV:(h + 1) * GLA_DV], True, False, check=False)
                    ins.then_inc(sem["intra_done"], add("intra_done", 1))
                    for half in range(2):
                        c = 2 * j + half
                        rows = slice(half * GLA_CHUNK, (half + 1) * GLA_CHUNK)
                        toks = slice(c * GLA_CHUNK, (c + 1) * GLA_CHUNK)
                        for h in range(GLA_HEADS):
                            if c:
                                pe.wait_ge(sem["state_ready"], past["state_ready"] + DT * (4 * (c - 1) + h) + DT)
                                for d in range(DT):
                                    ins = g.product(ps[rows, h, :], qT[:, DT * h + d, toks], state[:, DT * h + d, :], False, d == DT - 1, check=False)
                                if half == 1:
                                    ins.then_inc(sem["o_ready"], add("o_ready", 1))
                            if c == NCH - 1:
                                continue
                            for d in range(DT):
                                f = DT * h + d
                                if update >= 3:
                                    pe.wait_ge(sem["state_ready"], past["state_ready"] + update - 2)
                                ins = g.product(ps[:, 4 + update % 3, :], ks_tok[rows, j, f * P:(f + 1) * P],
                                                v_tok[rows, j, h * GLA_DV:(h + 1) * GLA_DV])
                                ins.then_inc(sem["update_ready"], add("update_ready", 1))
                                update += 1

                for c in range(4):
                    for half in range(HALVES):
                        w = g.chunk(pe, c_z + HALVES * c + half)
                        done = "z_ready" if half == HALVES - 1 else "z_half"
                        for j in range(NT):
                            n = 4 * c + j
                            if half == 0 and n < 4:
                                pe.wait_ge(sem["o_copied"], past["o_copied"] + 2 * 16)
                            elif half == 0:
                                pe.wait_ge(sem["z_silu"], past["z_silu"] + n - 3)
                            for k in range(KD):
                                ins = g.split_product(ps[:, n % 4, half * CHUNK:(half + 1) * CHUNK], columns(g.xT, k, slice(j * P, (j + 1) * P)),
                                                      columns(w, k), k == 0, k == KD - 1)
                            ins.then_inc(sem[done], add(done, 1))
                        g.release(done)
                pe.wait_ge(sem["gated"], past["gated"] + 16)
                split_feature_major_pe(g, pe, 0, v_tok, KI, NT, [4, 5, 6, 7])

            @block.scalar
            def _(act):
                act.dma_start(w_a[:], w_in[:, a0:a0 + GLA_RANK].rearrange("(k p) n -> p k n", p=P)).then_inc(sem[small_landed], add(small_landed, 16))
                act.dma_start(w_a2[0:GLA_RANK, :], t["gla_w_a2"][0]).then_inc(sem[small_landed], add(small_landed, 16))
                act.dma_start(w_a2[GLA_RANK:GLA_RANK + 1, :], t["gla_b_a"]).then_inc(sem[small_landed], add(small_landed, 16))
                g.split_high(act, c_v + RING)
                act.wait_ge(sem[small_landed], past[small_landed] + 48)
                nc.scalar.activation(w_a_parts[0][:], w_a[:], ACT.Copy).then_inc(sem["w_a_split"], add("w_a_split", 1))
                def v_copy(c):
                    g.split_high(act, c_v + 2 * c + 3)
                    for j in range(NT):
                        n = 4 * c + j
                        act.wait_ge(sem["v_ready"], past["v_ready"] + n + 1)
                        nc.scalar.activation(v_tok[:, j, c * COLS:(c + 1) * COLS], ps[:, n % 4, :], ACT.Copy).then_inc(sem["v_copied"], add("v_copied", 1))
                    g.split_high(act, c_v + 2 * c + 4)

                v_copy(0)
                act.wait_ge(sem["aT_ready"], past["aT_ready"] + 1)
                act.wait_ge(sem["aT_copied"], past["aT_copied"] + 1)
                nc.scalar.activation(aT[0:GLA_RANK, :], ps[0:GLA_RANK, 4, :], ACT.Copy).then_inc(sem["aT_copied"], add("aT_copied", 1))
                v_copy(1)
                for b in range(2):
                    for i in range(4):
                        f = 4 * b + i
                        act.wait_ge(sem["u_ready"], past["u_ready"] + f + 1)
                        nc.scalar.activation(kT[:, f, :], ps[:, 4 + i, :], ACT.Abs).then_inc(sem["abs_u"], add("abs_u", 1))
                    for i in range(4):
                        f = 4 * b + i
                        act.wait_ge(sem["abs_u"], past["abs_u"] + f + 1)
                        nc.scalar.activation(kT[:, f, :], kT[:, f, :], ACT.Exp, scale=-1.0).then_inc(sem["exp_neg_abs"], add("exp_neg_abs", 1))
                    for i in range(4):
                        f = 4 * b + i
                        act.wait_ge(sem["exp_neg_abs"], past["exp_neg_abs"] + f + 1)
                        nc.scalar.activation(kT[:, f, :], kT[:, f, :], ACT.Ln, bias=1.0).then_inc(sem["log1p"], add("log1p", 1))
                    v_copy(2 + b)
                for f in range(NF):
                    if f >= 4 and f % 2 == 0:
                        g.split_high(act, c_q + f // 2 + 1)
                    act.wait_ge(sem["decay_log"], past["decay_log"] + f + 1)
                    nc.scalar.activation(qT[:, f, :], decay_log[:, f, :], ACT.Exp, scale=1.0 / GATE_NORM).then_inc(sem["decays"], add("decays", 1))
                    nc.scalar.activation(kT[:, f, :], decay_log[:, f, :], ACT.Exp, scale=-1.0 / GATE_NORM).then_inc(sem["decays"], add("decays", 1))
                    ends = decay_log[:, f, :].rearrange("p (c i) -> p c i", i=GLA_CHUNK)[:, :, GLA_CHUNK - 1]
                    nc.scalar.activation(chunk_decay[:, f, :], ends, ACT.Exp, scale=1.0 / GATE_NORM).then_inc(sem["decays"], add("decays", 1))

                def ks_copy(f):
                    act.wait_ge(sem["ks_turned"], past["ks_turned"] + f + 1)
                    nc.scalar.activation(ks_tok[:, :, f * P:(f + 1) * P],
                                                             ps[:, 6 + f % 2, :].rearrange("p (j i) -> p j i", i=P), ACT.Copy).then_inc(sem["ks_copied"], add("ks_copied", 1))

                g.split_high(act, c_q + 5)
                for f in range(NF):
                    if f % 2 == 0:
                        g.split_high(act, c_q + 6 + f // 2)
                    act.wait_ge(sem["rest_log"], past["rest_log"] + f + 1)
                    nc.scalar.activation(to_end[:, f % 2, :], to_end[:, f % 2, :], ACT.Exp, scale=1.0 / GATE_NORM).then_inc(sem["rest_decay"], add("rest_decay", 1))
                    if f:
                        ks_copy(f - 1)
                ks_copy(NF - 1)
                g.split_high(act, c_z + RING)
                for n in range(NT * GLA_HEADS):
                    j, h = n // GLA_HEADS, n % GLA_HEADS
                    act.wait_ge(sem["o_ready"], past["o_ready"] + n + 1)
                    if j < NT - 1:
                        act.wait_ge(sem["update_ready"], past["update_ready"] + DT * (4 * (2 * j + 1) + h + 1))
                    if n:
                        act.wait_ge(sem["o_copied"], past["o_copied"] + 2 * n)
                    nc.scalar.activation(sq[:], ps[:, h, :], ACT.Square, accum_out=sumsq[:, n:n + 1]).then_inc(sem["o_copied"], add("o_copied", 1))
                    nc.scalar.activation(v_tok[:, j, h * GLA_DV:(h + 1) * GLA_DV], ps[:, h, :], ACT.Copy).then_inc(sem["o_copied"], add("o_copied", 1))
                act.wait_ge(sem["mean_sq"], past["mean_sq"] + 1)
                nc.scalar.activation(root[:], root[:], ACT.Sqrt).then_inc(sem["root"], add("root", 1))
                for n in range(16):
                    if n % 4 == 0:
                        g.split_high(act, c_z + n // 2 + 3)
                    act.wait_ge(sem["z_ready"], past["z_ready"] + n + 1)
                    if n >= 2:
                        act.wait_ge(sem["gated"], past["gated"] + n - 1)
                    nc.scalar.activation(z_silu[:, n % 2, :], ps[:, n % 4, :], ACT.Silu).then_inc(sem["z_silu"], add("z_silu", 1))
                    if n % 4 == 3:
                        g.split_high(act, c_z + n // 2 + 3)
                split_feature_major_act(g, act, 0, gT, KI, [4, 5, 6, 7], scale=g.col("gla_gn_g"))

            @block.vector
            def _(dve):
                nc.vector.memset(aT[:], 1.0).then_inc(sem["aT_copied"], add("aT_copied", 1))
                dve.wait_ge(sem["w_a_split"], past["w_a_split"] + 1)
                nc.vector.tensor_tensor(w_a_parts[1][:], w_a[:], w_a_parts[0][:].bitcast(F32), ALU.subtract).then_inc(sem["w_a_split"], add("w_a_split", 1))
                for b in range(2):
                    for i in range(4):
                        f = 4 * b + i
                        dve.wait_ge(sem["log1p"], past["log1p"] + f + 1)
                        nc.vector.scalar_tensor_tensor(out=kT[:, f, :], in0=ps[:, 4 + i, :], scalar=0.0, in1=kT[:, f, :],
                                                                          op0=ALU.min, op1=ALU.subtract).then_inc(sem["log_gate"], add("log_gate", 1))
                        dve.wait_ge(sem["log_gate"], past["log_gate"] + f + 1)
                        nc.vector.tensor_tensor_scan(decay_log[:, f, :], g.keep_state[:], kT[:, f, :], 0.0, ALU.mult, ALU.add).then_inc(sem["decay_log"], add("decay_log", 1))
                for n in range(NF):
                    dve.wait_ge(sem["qk_ready"], past["qk_ready"] + n + 1)
                    dve.wait_ge(sem["decays"], past["decays"] + 3 * n + 3)
                    nc.vector.scalar_tensor_tensor(out=qT[:, n, :], in0=ps[:, n % 6, :], scalar=GLA_DK ** -0.5, in1=qT[:, n, :],
                                                                     op0=ALU.mult, op1=ALU.mult).then_inc(sem["qk_used"], add("qk_used", 1))
                for f in range(NF):
                    n = NF + f
                    if f >= 2:
                        dve.wait_ge(sem["ks_turned"], past["ks_turned"] + f - 1)
                    ends = decay_log[:, f, :].rearrange("p (c i) -> p c i", i=GLA_CHUNK)
                    nc.vector.tensor_tensor(to_end[:, f % 2, :].rearrange("p (c i) -> p c i", i=GLA_CHUNK),
                                                               ends[:, :, GLA_CHUNK - 1:GLA_CHUNK].to_broadcast([P, NCH, GLA_CHUNK]),
                                                               ends, ALU.subtract).then_inc(sem["rest_log"], add("rest_log", 1))
                    dve.wait_ge(sem["qk_ready"], past["qk_ready"] + n + 1)
                    dve.wait_ge(sem["rest_decay"], past["rest_decay"] + f + 1)
                    nc.vector.tensor_tensor(to_end[:, f % 2, :], ps[:, n % 6, :], to_end[:, f % 2, :], ALU.mult).then_inc(sem["ks_made"], add("ks_made", 1))
                    nc.vector.tensor_tensor(kT[:, f, :], ps[:, n % 6, :], kT[:, f, :], ALU.mult).then_inc(sem["qk_used"], add("qk_used", 1))
                update = 0
                for j in range(NT):
                    dve.wait_ge(sem["attn_ready"], past["attn_ready"] + j + 1)
                    if j:
                        dve.wait_ge(sem["intra_done"], past["intra_done"] + j)
                    nc.vector.tensor_tensor(attn[:], ps[:, 7, :].rearrange("p (h i) -> p h i", h=GLA_HEADS),
                                                                  g.not_before64[:].unsqueeze(1).to_broadcast([P, GLA_HEADS, P]), ALU.mult).then_inc(sem["attn_masked"], add("attn_masked", 1))
                    for half in range(2):
                        c = 2 * j + half
                        if c == NCH - 1:
                            continue
                        for f in range(NF):
                            dve.wait_ge(sem["update_ready"], past["update_ready"] + update + 1)
                            if c == 0:
                                ins = nc.vector.tensor_copy(state[:, f, :], ps[:, 4 + update % 3, :])
                            else:
                                ins = nc.vector.scalar_tensor_tensor(out=state[:, f, :], in0=state[:, f, :], scalar=chunk_decay[:, f, c:c + 1],
                                                                     in1=ps[:, 4 + update % 3, :], op0=ALU.mult, op1=ALU.add)
                            ins.then_inc(sem["state_ready"], add("state_ready", 1))
                            update += 1
                dve.wait_ge(sem["o_copied"], past["o_copied"] + 32)
                nc.vector.tensor_scalar(root[:], sumsq[:], 1.0 / GLA_DV, LN_EPS, ALU.mult, ALU.add).then_inc(sem["mean_sq"], add("mean_sq", 1))
                dve.wait_ge(sem["root"], past["root"] + 1)
                nc.vector.reciprocal(rstd[:], root[:]).then_inc(sem["rstd"], add("rstd", 1))
                dve.wait_ge(sem["rstd"], past["rstd"] + 1)
                for n in range(16):
                    h, j = n // 4, n % 4
                    dve.wait_ge(sem["z_silu"], past["z_silu"] + n + 1)
                    o = v_tok[:, j, h * GLA_DV:(h + 1) * GLA_DV]
                    i = j * GLA_HEADS + h
                    nc.vector.scalar_tensor_tensor(out=o, in0=o, scalar=rstd[:, i:i + 1], in1=z_silu[:, n % 2, :],
                                                                   op0=ALU.mult, op1=ALU.mult).then_inc(sem["gated"], add("gated", 1))
                split_feature_major_dve(g, dve, 0, gT, KI, [4, 5, 6, 7], scale=g.col("gla_gn_g"))

            @block.gpsimd
            def _(pool):
                g.split_low(pool)

            @block.sync
            def _(sp):
                g.load_chunks(sp)
    g.sem.end_phase()


def phase_post(g, layer, gT, first, then_norm, gT_at):
    nc, t = g.nc, g.t
    sem, past, count, add = g.sem, g.sem.past, g.sem.count, g.sem.add
    NH = D // COLS
    KP = 2
    HALVES = COLS // CHUNK
    ps = g.ps
    end = first + 2 * D // CHUNK + D // CHUNK
    x_from = t["x"][0].rearrange("(j p) d -> p j d", p=P) if layer == 0 else g.x_dram
    with ExitStack() as stack:
        x = r = g.sb(stack, f"x{layer}", [P, NT, D])
        w_ple = g.alias(f"w_ple{layer}", [P, KP, D], F32, gT_at)
        scaled = g.alias(f"x_scaled{layer}", [P, NT, D], F32, gT_at + 4 * KP * D)
        gain = g.sb(stack, f"gain{layer}", [P, D])
        shift = g.sb(stack, f"shift{layer}", [P, D])
        p_tok = g.sb(stack, f"p_tok{layer}", [P, NT, KP * P])
        pT = g.sb(stack, f"pT{layer}", [P, KP, T])
        gate = g.sb(stack, f"gate{layer}", [P, 2, COLS])
        stats = g.sb(stack, f"stats{layer}", [P, NT, NH, 6])
        moments = g.sb(stack, f"moments{layer}", [P, NT, 2])
        rstd = g.sb(stack, f"rstd_x{layer}", [P, NT])
        sumsq = g.sb(stack, f"sumsq_x{layer}", [P, NH, NT])
        with nc.Block(f"post{layer}", no_gpsimd_drain=True) as block:

            @block.tensor
            def _(pe):
                for n in range(NH * HALVES):
                    cols = slice((n % HALVES) * CHUNK, (n % HALVES + 1) * CHUNK)
                    for c in range(2):
                        w = g.chunk(pe, first + 2 * n + c)
                        for j in range(NT):
                            for k in range(KD):
                                ins = g.split_product(ps[:, n // HALVES * NT + j, cols], columns(gT, c * KD + k, slice(j * P, (j + 1) * P)), columns(w, k),
                                                      c == 0 and k == 0, c == 1 and k == KD - 1)
                            ins.then_inc(sem["y_part"], add("y_part", 1))
                        g.release("y_part")
                pe.wait_ge(sem["p_landed"], past["p_landed"] + 16)
                pe.wait_ge(sem["y_added"], past["y_added"] + NH * NT)
                to_feature_major_pe(g, pe, (0, 0), p_tok, KP, NT, [6, 7])
                to_x = [6, 7, 2, 3, 4, 5]
                pe.wait_ge(sem["turned_by_act"], past["turned_by_act"] + KP // 2)
                pe.wait_ge(sem["turned_by_dve"], past["turned_by_dve"] + KP // 2)
                pe.wait_ge(sem["normed"], past["normed"] + NT - 1)
                pe.wait_ge(sem["last_normed"], past["last_normed"] + 1)
                split_feature_major_pe(g, pe, 0, r, KD, NT, to_x)
                pe.wait_ge(sem["w_ple_landed"], past["w_ple_landed"] + 16)
                for n in range(NH):
                    for half in range(HALVES):
                        w = g.chunk(pe, first + 2 * NH * HALVES + HALVES * n + half)
                        done = "gate_ready" if half == HALVES - 1 else "gate_half"
                        for j in range(NT):
                            i = n * NT + j
                            tile = slice(j * P, (j + 1) * P)
                            if half == 0 and i >= 4:
                                pe.wait_ge(sem["ple_gated"], past["ple_gated"] + i - 3)
                            for k in range(KD):
                                if half == 0 and i == 0:
                                    pe.wait_ge(sem["turned_low"], past["turned_low"] + k + 1)
                                ins = g.split_product(ps[:, i % 4, half * CHUNK:(half + 1) * CHUNK], columns(g.xT, k, tile), columns(w, k), k == 0, k == KD - 1)
                            ins.then_inc(sem[done], add(done, 1))
                            if half == 0:
                                for k in range(KP):
                                    g.product(ps[:, 4 + i % 4, :], pT[:, k, tile], w_ple[:, k, n * COLS:(n + 1) * COLS], k == 0, k == KP - 1)
                        g.release(done)
                pe.wait_ge(sem["ple_gated"], past["ple_gated"] + NH * NT)
                if then_norm:
                    pe.wait_ge(sem["x_scaled"], past["x_scaled"] + NT // 2)
                    pe.wait_ge(sem["x_scaled_too"], past["x_scaled_too"] + NT // 2)
                else:
                    pe.wait_ge(sem["x_added"], past["x_added"] + NH * NT)
                split_feature_major_pe(g, pe, KD, scaled if then_norm else x, KD, NT, [0, 1, 2, 3, 4, 5])

            @block.scalar
            def _(act):
                act.dma_start(p_tok[:], t["p"][layer, 0].rearrange("(j p) d -> p j d", p=P)).then_inc(sem["p_landed"], add("p_landed", 16))
                act.dma_start(gain[:], t["ln_g"][layer:layer + 1, :].to_broadcast([P, D])).then_inc(sem["gain_landed"], add("gain_landed", 16))
                act.dma_start(shift[:], t["ln_b"][layer:layer + 1, :].to_broadcast([P, D])).then_inc(sem["gain_landed"], add("gain_landed", 16))
                for n in range(2 * NH * HALVES):
                    g.split_high(act, first + n + 1 + RING)
                act.wait_ge(sem["y_part"], past["y_part"] + 2 * NH * HALVES * NT)
                act.dma_start(w_ple[:], t["ple_w"][layer].rearrange("(k p) n -> p k n", p=P)).then_inc(sem["w_ple_landed"], add("w_ple_landed", 16))
                to_feature_major_act(g, act, 0, pT, KP, T, [6, 7])
                act.wait_ge(sem["variance"], past["variance"] + NT)
                nc.scalar.activation(rstd[:], rstd[:], ACT.Sqrt).then_inc(sem["deviation"], add("deviation", 1))
                split_feature_major_act(g, act, 0, g.xT, KD, [6, 7, 2, 3, 4, 5])
                gates = first + 2 * NH * HALVES

                def square(n, j):
                    cols = slice(n * COLS, (n + 1) * COLS)
                    act.wait_ge(sem["x_added"], past["x_added"] + n * NT + j + 1)
                    nc.scalar.activation(scaled[:, j, cols], x[:, j, cols], ACT.Square, accum_out=sumsq[:, n, j:j + 1]).then_inc(sem["x_squared"], add("x_squared", 1))

                for i in range(NH * NT):
                    if i % NT == 0:
                        g.split_high(act, gates + HALVES * (i // NT) + 1 + RING)
                    act.wait_ge(sem["gate_ready"], past["gate_ready"] + i + 1)
                    if i >= 2:
                        act.wait_ge(sem["ple_gated"], past["ple_gated"] + i - 1)
                        act.wait_ge(sem["x_added"], past["x_added"] + i - 1)
                    nc.scalar.activation(gate[:, i % 2, :], ps[:, i % 4, :], ACT.Sigmoid).then_inc(sem["gate_sigmoid"], add("gate_sigmoid", 1))
                    if then_norm and i >= NT:
                        square(0, i - NT)
                if then_norm:
                    for j in range(NT):
                        square(1, j)
                    act.wait_ge(sem["x_mean_sq"], past["x_mean_sq"] + 1)
                    nc.scalar.activation(sumsq[:, 0, :], sumsq[:, 0, :], ACT.Sqrt).then_inc(sem["x_root"], add("x_root", 1))
                    act.wait_ge(sem["x_rstd"], past["x_rstd"] + 1)
                    for j in range(NT // 2):
                        nc.scalar.activation(scaled[:, j, :], x[:, j, :], ACT.Copy, scale=sumsq[:, 0, j:j + 1]).then_inc(sem["x_scaled"], add("x_scaled", 1))
                g.split_high(act, end + RING)
                split_feature_major_act(g, act, KD, g.xT, KD, [0, 1, 2, 3, 4, 5], scale=g.col("norm_g_2") if then_norm else None)

            @block.vector
            def _(dve):
                dve.wait_ge(sem["x_back"], past["x_back"] + 16)
                for n in range(NH):
                    for j in range(NT):
                        cols = slice(n * COLS, (n + 1) * COLS)
                        dve.wait_ge(sem["y_part"], past["y_part"] + 2 * NT * (HALVES * n + HALVES - 1) + NT + j + 1)
                        i = n * NT + j
                        nc.vector.scalar_tensor_tensor(out=r[:, j, cols], in0=x[:, j, cols], scalar=ALPHA, in1=ps[:, i, :],
                                                                         op0=ALU.mult, op1=ALU.add).then_inc(sem["y_added"], add("y_added", 1))
                        dve.wait_ge(sem["y_added"], past["y_added"] + i + 1)
                        nc.vector.bn_stats(stats[:, j, n, :], r[:, j, cols]).then_inc(sem["bn_stats"], add("bn_stats", 1))
                to_feature_major_dve(g, dve, 0, pT, KP, T, [6, 7])
                dve.wait_ge(sem["bn_stats"], past["bn_stats"] + NH * NT)
                for j in range(NT):
                    nc.vector.bn_aggr(moments[:, j, :], stats[:, j, :, :].rearrange("p a b -> p (a b)")).then_inc(sem["moments"], add("moments", 1))
                dve.wait_ge(sem["moments"], past["moments"] + NT)
                for j in range(NT):
                    nc.vector.tensor_scalar(rstd[:, j:j + 1], moments[:, j, 1:2], LN_EPS, None, ALU.add).then_inc(sem["variance"], add("variance", 1))
                dve.wait_ge(sem["deviation"], past["deviation"] + 1)
                nc.vector.reciprocal(rstd[:], rstd[:]).then_inc(sem["rstd_x"], add("rstd_x", 1))
                dve.wait_ge(sem["rstd_x"], past["rstd_x"] + 1)
                dve.wait_ge(sem["gain_landed"], past["gain_landed"] + 32)
                last = NT - 1
                nc.vector.tensor_scalar(r[:, last, :], r[:, last, :], moments[:, last, 0:1], rstd[:, last:NT], ALU.subtract, ALU.mult).then_inc(sem["last_centred"], add("last_centred", 1))
                for j in range(NT - 1):
                    nc.vector.scalar_tensor_tensor(out=r[:, j, :], in0=r[:, j, :], scalar=moments[:, j, 0:1], in1=gain[:], op0=ALU.subtract, op1=ALU.mult).then_inc(sem["gained"], add("gained", 1))
                for j in range(NT - 1):
                    dve.wait_ge(sem["gained"], past["gained"] + j + 1)
                    nc.vector.scalar_tensor_tensor(out=r[:, j, :], in0=r[:, j, :], scalar=rstd[:, j:j + 1], in1=shift[:], op0=ALU.mult, op1=ALU.add).then_inc(sem["normed"], add("normed", 1))
                dve.wait_ge(sem["normed"], past["normed"] + NT - 1)
                dve.wait_ge(sem["last_normed"], past["last_normed"] + 1)
                split_feature_major_dve(g, dve, 0, g.xT, KD, [6, 7, 2, 3, 4, 5])
                for i in range(NH * NT):
                    n, j = i // NT, i % NT
                    cols = slice(n * COLS, (n + 1) * COLS)
                    dve.wait_ge(sem["gate_sigmoid"], past["gate_sigmoid"] + i + 1)
                    nc.vector.tensor_tensor(gate[:, i % 2, :], gate[:, i % 2, :], ps[:, 4 + i % 4, :], ALU.mult).then_inc(sem["ple_gated"], add("ple_gated", 1))
                    dve.wait_ge(sem["ple_gated"], past["ple_gated"] + i + 1)
                    nc.vector.tensor_tensor(x[:, j, cols], r[:, j, cols], gate[:, i % 2, :], ALU.add).then_inc(sem["x_added"], add("x_added", 1))
                if then_norm:
                    dve.wait_ge(sem["x_squared"], past["x_squared"] + NH * NT)
                    nc.vector.tensor_tensor(sumsq[:, 0, :], sumsq[:, 0, :], sumsq[:, 1, :], ALU.add).then_inc(sem["x_sumsq"], add("x_sumsq", 1))
                    dve.wait_ge(sem["x_sumsq"], past["x_sumsq"] + 1)
                    nc.vector.tensor_scalar(sumsq[:, 0, :], sumsq[:, 0, :], 1.0 / D, RMS_EPS, ALU.mult, ALU.add).then_inc(sem["x_mean_sq"], add("x_mean_sq", 1))
                    dve.wait_ge(sem["x_root"], past["x_root"] + 1)
                    nc.vector.reciprocal(sumsq[:, 0, :], sumsq[:, 0, :]).then_inc(sem["x_rstd"], add("x_rstd", 1))
                    dve.wait_ge(sem["x_rstd"], past["x_rstd"] + 1)
                    for j in range(NT // 2, NT):
                        nc.vector.tensor_scalar(scaled[:, j, :], x[:, j, :], sumsq[:, 0, j:j + 1], None, ALU.mult).then_inc(sem["x_scaled_too"], add("x_scaled_too", 1))
                split_feature_major_dve(g, dve, KD, g.xT, KD, [0, 1, 2, 3, 4, 5], scale=g.col("norm_g_2") if then_norm else None)

            @block.gpsimd
            def _(pool):
                g.split_low(pool, first + 2 * NH * HALVES + RING)
                j, step = NT - 1, "last_step"
                pool.wait_ge(sem["last_centred"], past["last_centred"] + 1)
                pool.wait_ge(sem["gain_landed"], past["gain_landed"] + 32)
                nc.gpsimd.tensor_tensor(r[:, j, :], r[:, j, :], gain[:], ALU.mult).then_inc(sem[step], add(step, 1))
                pool.wait_ge(sem[step], past[step] + 1)
                nc.gpsimd.tensor_tensor(r[:, j, :], r[:, j, :], shift[:], ALU.add).then_inc(sem["last_normed"], add("last_normed", 1))
                g.split_low(pool)

            @block.sync
            def _(sp):
                sp.dma_start(x[:], x_from).then_inc(sem["x_back"], add("x_back", 16))
                for n in range(NH):
                    g.load_chunks(sp, end + RING + n)
                    cols = slice(n * COLS, (n + 1) * COLS)
                    sp.wait_ge(sem["x_added"], past["x_added"] + (n + 1) * NT)
                    sp.dma_start(g.x_dram[:, :, cols], x[:, :, cols]).then_inc(sem["x_saved"], add("x_saved", 16))
                g.load_chunks(sp)
                sp.wait_ge(sem["x_saved"], past["x_saved"] + 16 * NH)
    g.sem.end_phase()

DSA_HEADS, DH, IDX_HEADS, IDX_DIM, TOPK = 16, 128, 8, 64, 128
HALF, IDX_HALF = DH // 8, IDX_DIM // 8
ROPE_THETA = 500000.0
ATTN_SCALE = DH ** -0.5
INDEX_SCALE = IDX_HEADS ** -0.5 * IDX_DIM ** -0.5
MASKED, TAKEN = -1e30, -3e38
SWAP_HEAD = [(i + HALF) % (2 * HALF) for i in range(32)]
SWAP_IDX = [(i + IDX_HALF) % (2 * IDX_HALF) if i < 2 * IDX_HALF else i for i in range(32)]
TWO_PI_PARTS = (6.28125, 0.0019350051879882812, 3.0199159819e-07)
ROUND = 1.5 * 2.0 ** 23


def inverse_frequencies():
    return [float(np.float32(ROPE_THETA ** (-2.0 * i / (2 * n)))) for n in (HALF, IDX_HALF) for i in range(n)]


def phase_dsa(g, qT, zT, gT, first):
    nc, t, ps = g.nc, g.t, g.ps
    sem, past, count, add = g.sem, g.sem.past, g.sem.count, g.sem.add
    IT = IDX_HEADS * IDX_DIM // P
    with ExitStack() as stack:
        kT = g.sb(stack, "dsa_kT", [P, T])
        v = g.sb(stack, "dsa_v", [P, NT, DH])
        rot = g.sb(stack, "rot", [P, 2, T])
        kiT = g.sb(stack, "kiT", [P, T])
        wi = g.sb(stack, "wi", [P, NT, IDX_HEADS])
        left = g.sb(stack, "left", [P, NT, T])
        top8 = g.sb(stack, "top8", [P, 8])
        prob = g.sb(stack, "prob", [P, 2, NT, T])
        score, qiT = prob[:, 0], prob[:, 1]
        probT = g.sb(stack, "probT", [P, NT, T])
        relu = probT[:, 0:2]
        peak = g.sb(stack, "peak", [P, 2 * NT])
        shift = g.sb(stack, "peak_shift", [P, 2 * NT])
        total = g.sb(stack, "total", [P, 2 * NT])
        inv = g.sb(stack, "inv_total", [P, 2 * NT])
        bias = left
        gated = g.sb(stack, "dsa_gated", [P, 2, T])
        turned = gated[:, 1, :]
        wiT = gated[0:IDX_HEADS, 0, :]
        c_kv, c_qi = first, first + 1
        c_ki = c_qi + IDX_HEADS * IDX_DIM // CHUNK
        c_heads = c_ki + 1
        PER = CHUNK // P
        n_tiles = 2 * DSA_HEADS
        n_scores = DSA_HEADS // 2
        n_silu = 4
        n_early = DSA_HEADS + n_silu
        score_tiles = range(1, NT)
        pairs = [(j, h) for j in score_tiles for h in range(IDX_HEADS)]
        with nc.Block("dsa", no_gpsimd_drain=True) as block:

            @block.tensor
            def _(pe):
                w = g.chunk(pe, c_kv)
                for k in range(KD):
                    ins = g.split_product(ps[:, 0, :], columns(w, k, slice(0, DH)), columns(g.xT, k), k == 0, k == KD - 1)
                ins.then_inc(sem["kT_ready"], add("kT_ready", 1))
                for j in range(NT):
                    for k in range(KD):
                        ins = g.split_product(ps[:, 1, j * DH:(j + 1) * DH], columns(g.xT, k, slice(j * P, (j + 1) * P)), columns(w, k, slice(DH, 2 * DH)), k == 0, k == KD - 1)
                ins.then_inc(sem["v_tok_ready"], add("v_tok_ready", 1))
                g.release("v_tok_ready")
                for i in range(IT):
                    if i % PER == 0:
                        w = g.chunk(pe, c_qi + i // PER)
                    for k in range(KD):
                        ins = g.split_product(ps[:, 2 + i, :], columns(w, k, slice(i % PER * P, (i % PER + 1) * P)), columns(g.xT, k), k == 0, k == KD - 1)
                    ins.then_inc(sem["qi_ready"], add("qi_ready", 1))
                    if i % PER == PER - 1:
                        g.release("qi_ready")
                w = g.chunk(pe, c_ki)
                for k in range(KD):
                    ins = g.split_product(ps[:, 6, :], columns(w, k, slice(0, 2 * IDX_DIM)), columns(g.xT, k), k == 0, k == KD - 1)
                ins.then_inc(sem["ki_ready"], add("ki_ready", 1))
                for k in range(KD):
                    ins = g.split_product(ps[0:IDX_HEADS, 7, :], columns(w, k, slice(2 * IDX_DIM, 2 * IDX_DIM + IDX_HEADS)), columns(g.xT, k), k == 0, k == KD - 1)
                ins.then_inc(sem["wiT_ready"], add("wiT_ready", 1))
                g.release("wiT_ready")

                chunk = [None]

                def project(n, ks=range(KD)):
                    if n % PER == 0 and 0 in ks:
                        chunk[0] = g.chunk(pe, c_heads + n // PER)
                    w = chunk[0]
                    if 0 not in ks:
                        pass
                    elif n < 2:
                        pe.wait_ge(sem["kiT_ready" if n == 0 else "wi_copied"], past["kiT_ready" if n == 0 else "wi_copied"] + 1)
                    else:
                        b = n - 2
                        done = "q_copied" if b < DSA_HEADS else "z_gated"
                        pe.wait_ge(sem[done], past[done] + b % DSA_HEADS + 1)
                    for k in ks:
                        ins = g.split_product(ps[:, 6 + n % 2, :], columns(w, k, slice(n % PER * P, (n % PER + 1) * P)), columns(g.xT, k), k == 0, k == KD - 1)
                    if KD - 1 not in ks:
                        return
                    ins.then_inc(sem["head_ready"], add("head_ready", 1))
                    if n % PER == PER - 1:
                        g.release("head_ready")

                project(0)
                pe.wait_ge(sem["wiT_copied"], past["wiT_copied"] + 1)
                for j in range(NT):
                    ins = nc.tensor.transpose(ps[:, 7, j * IDX_HEADS:(j + 1) * IDX_HEADS], wiT[:, j * P:(j + 1) * P], g.ident[0:IDX_HEADS, 0:IDX_HEADS])
                ins.then_inc(sem["wi_ready"], add("wi_ready", 1))
                for n in range(1, 4):
                    project(n)
                pe.wait_ge(sem["qiT_ready"], past["qiT_ready"] + IT)
                pe.wait_ge(sem["kiT_ready"], past["kiT_ready"] + 2)
                for m, (j, h) in enumerate(pairs):
                    if m >= 2:
                        pe.wait_ge(sem["relu"], past["relu"] + m - 1)
                    rows = slice((h % 2) * IDX_DIM, (h % 2 + 1) * IDX_DIM)
                    n = (j + 1) * P
                    g.product(ps[:, m % 2, 0:n], qiT[rows, h // 2, j * P:(j + 1) * P], kiT[rows, 0:n]).then_inc(sem["index_ready"], add("index_ready", 1))
                    if m % 6 == 5 and 4 + m // 6 < n_scores:
                        project(4 + m // 6)
                for n in range(n_scores, n_early):
                    project(n)

                def logits(h):
                    pe.wait_ge(sem["q_rotated"], past["q_rotated"] + h + 1)
                    if h == 0:
                        pe.wait_ge(sem["kT_rotated"], past["kT_rotated"] + 1)
                        pe.wait_ge(sem["relu"], past["relu"] + len(pairs))
                    for j in range(NT):
                        m = NT * h + j
                        if m >= 2:
                            pe.wait_ge(sem["masked"], past["masked"] + m - 1)
                        n = (j + 1) * P
                        g.product(ps[:, m % 2, 0:n], qT[:, h, j * P:(j + 1) * P], kT[:, 0:n]).then_inc(sem["logits_ready"], add("logits_ready", 1))

                logits(0)
                logits(1)
                for h in range(DSA_HEADS):
                    for j in range(NT):
                        m = NT * h + j
                        pe.wait_ge(sem["prob_ready"], past["prob_ready"] + m + 1)
                        if m >= 2:
                            b = m - 2
                            done = "probT_by_dve" if b % 2 else "probT_by_act"
                            pe.wait_ge(sem[done], past[done] + b // 2 + 1)
                        for i in range(j + 1):
                            ins = nc.tensor.transpose(ps[:, 2 + m % 2, i * P:(i + 1) * P], prob[:, h % 2, j, i * P:(i + 1) * P], g.ident[:])
                        ins.then_inc(sem["prob_turned"], add("prob_turned", 1))
                        if n_early + h < n_tiles and j % 2:
                            project(n_early + h, range(j // 2 * KD // 2, (j // 2 + 1) * KD // 2))
                    if h + 2 < DSA_HEADS:
                        logits(h + 2)
                    pe.wait_ge(sem["probT_by_act"], past["probT_by_act"] + 2 * h + 2)
                    pe.wait_ge(sem["probT_by_dve"], past["probT_by_dve"] + 2 * h + 2)
                    if h >= 2:
                        pe.wait_ge(sem["head_done"], past["head_done"] + h - 1)
                    for i in range(NT):
                        ins = g.product(ps[:, 4 + h % 2, i * P:T], v[:, i, :], probT[:, i, i * P:T], i == 0, i == NT - 1, check=False)
                    ins.then_inc(sem["o_head"], add("o_head", 1))

            @block.scalar
            def _(act):
                g.split_high(act, c_kv + RING)
                act.wait_ge(sem["kT_ready"], past["kT_ready"] + 1)
                nc.scalar.activation(kT[:], ps[:, 0, :], ACT.Copy).then_inc(sem["kT_copied"], add("kT_copied", 1))
                act.wait_ge(sem["v_tok_ready"], past["v_tok_ready"] + 1)
                nc.scalar.activation(v[:], ps[:, 1, :].rearrange("p (j d) -> p j d", j=NT), ACT.Copy).then_inc(sem["v_tok_copied"], add("v_tok_copied", 1))
                g.split_high(act, c_kv + 1 + RING)
                for i in range(IT):
                    act.wait_ge(sem["qi_ready"], past["qi_ready"] + i + 1)
                    nc.scalar.activation(qiT[:, i, :], ps[:, 2 + i, :], ACT.Copy).then_inc(sem["qi_copied"], add("qi_copied", 1))
                    if i % PER == PER - 1:
                        g.split_high(act, c_qi + i // PER + 1 + RING)
                act.wait_ge(sem["ki_ready"], past["ki_ready"] + 1)
                nc.scalar.activation(kiT[:], ps[:, 6, :], ACT.Copy).then_inc(sem["kiT_ready"], add("kiT_ready", 1))
                act.wait_ge(sem["wiT_ready"], past["wiT_ready"] + 1)
                nc.scalar.activation(wiT[:], ps[0:IDX_HEADS, 7, :], ACT.Copy).then_inc(sem["wiT_copied"], add("wiT_copied", 1))
                g.split_high(act, c_ki + 1 + RING)
                act.wait_ge(sem["wi_ready"], past["wi_ready"] + 1)
                nc.scalar.activation(wi[:], ps[:, 7, 0:NT * IDX_HEADS].rearrange("p (j h) -> p j h", j=NT), ACT.Copy,
                                                         scale=INDEX_SCALE).then_inc(sem["wi_copied"], add("wi_copied", 1))
                g.split_high(act, c_ki + 1 + RING)

                def project(n):
                    h = n % DSA_HEADS
                    act.wait_ge(sem["head_ready"], past["head_ready"] + n + 1)
                    src = ps[:, 6 + n % 2, :]
                    if n < DSA_HEADS:
                        nc.scalar.activation(qT[:, h, :], src, ACT.Copy).then_inc(sem["q_copied"], add("q_copied", 1))
                    elif h < n_silu:
                        nc.scalar.activation(zT[:, h, :], src, ACT.Silu).then_inc(sem["z_gated"], add("z_gated", 1))
                    else:
                        nc.scalar.activation(zT[:, h, :], src, ACT.Tanh, scale=0.5).then_inc(sem["z_tanh"], add("z_tanh", 1))
                    if n % PER == PER - 1:
                        g.split_high(act, c_heads + n // PER + 1 + RING)

                for n in range(4):
                    project(n)
                for m, (j, h) in enumerate(pairs):
                    n = (j + 1) * P
                    act.wait_ge(sem["index_ready"], past["index_ready"] + m + 1)
                    if m >= 2:
                        act.wait_ge(sem["summed"], past["summed"] + m - 1)
                    nc.scalar.activation(relu[:, m % 2, 0:n], ps[:, m % 2, 0:n], ACT.Relu).then_inc(sem["relu"], add("relu", 1))
                    if m % 6 == 5 and 4 + m // 6 < n_scores:
                        project(4 + m // 6)
                for n in range(n_scores, n_early):
                    project(n)

                def exps(h):
                    for j in range(NT):
                        m = NT * h + j
                        i = m % (2 * NT)
                        act.wait_ge(sem["peak_shift"], past["peak_shift"] + m + 1)
                        row = prob[:, h % 2, j, 0:(j + 1) * P]
                        nc.scalar.activation(row, row, ACT.Exp, bias=shift[:, i:i + 1], scale=ATTN_SCALE, accum_out=total[:, i:i + 1]).then_inc(sem["exps"], add("exps", 1))

                def high(h):
                    act.wait_ge(sem["head_done"], past["head_done"] + h + 1)
                    nc.scalar.activation(gT[0][:, h, :], gated[:, h % 2, :], ACT.Copy).then_inc(sem["head_high"], add("head_high", 1))

                exps(0)
                exps(1)
                for h in range(DSA_HEADS):
                    for j in range(0, NT, 2):
                        m = NT * h + j
                        act.wait_ge(sem["prob_turned"], past["prob_turned"] + m + 1)
                        if h:
                            act.wait_ge(sem["o_head"], past["o_head"] + h)
                        nc.scalar.activation(probT[:, 0:j + 1, j * P:(j + 1) * P],
                                                                    ps[:, 2 + m % 2, 0:(j + 1) * P].rearrange("p (i t) -> p i t", t=P), ACT.Copy).then_inc(sem["probT_by_act"], add("probT_by_act", 1))
                    if n_early + h < n_tiles:
                        project(n_early + h)
                    if h + 2 < DSA_HEADS:
                        exps(h + 2)
                    if h:
                        high(h - 1)
                high(DSA_HEADS - 1)

            @block.vector
            def _(dve):
                swaps = [0]

                def swap(x, rows, mask):
                    n = swaps[0]
                    swaps[0] += 1
                    if n >= 2:
                        dve.wait_ge(sem["q_rotated"], past["q_rotated"] + n - 1)
                    nc.vector.stream_shuffle(rot[0:rows, n % 2, :], x, mask).then_inc(sem["swapped"], add("swapped", 1))

                R = 2 * HALF
                nc.vector.tensor_scalar(bias[:, 0, 0:P], g.after[:], MASKED, None, ALU.mult).then_inc(sem["causal_bias"], add("causal_bias", 1))
                def turn(x, rows, mask, cos, sin, done):
                    nc.vector.stream_shuffle(turned[0:rows, :], x, mask).then_inc(sem["turn_step"], add("turn_step", 1))
                    dve.wait_ge(sem["turn_step"], count["turn_step"])
                    nc.vector.tensor_tensor(x, x, cos, ALU.mult).then_inc(sem["turn_step"], add("turn_step", 1))
                    nc.vector.tensor_tensor(turned[0:rows, :], turned[0:rows, :], sin, ALU.mult).then_inc(sem["turn_step"], add("turn_step", 1))
                    dve.wait_ge(sem["turn_step"], count["turn_step"])
                    nc.vector.tensor_tensor(x, x, turned[0:rows, :], ALU.add).then_inc(sem[done], add(done, 1))
                    dve.wait_ge(sem[done], count[done])

                dve.wait_ge(sem["kT_copied"], past["kT_copied"] + 1)
                turn(kT[0:R, :], R, SWAP_HEAD, g.head_cos[:], g.head_sin[:], "kT_rotated")
                for i in range(IT):
                    dve.wait_ge(sem["qi_copied"], past["qi_copied"] + i + 1)
                    turn(qiT[:, i, :], P, SWAP_IDX, g.idx_cos[:], g.idx_sin[:], "qiT_ready")
                dve.wait_ge(sem["kiT_ready"], past["kiT_ready"] + 1)
                turn(kiT[:], P, SWAP_IDX, g.idx_cos[:], g.idx_sin[:], "kiT_ready")

                def swap_query(h):
                    dve.wait_ge(sem["q_copied"], past["q_copied"] + h + 1)
                    swap(qT[0:R, h, :], R, SWAP_HEAD)

                def project(n):
                    h = n - DSA_HEADS
                    dve.wait_ge(sem["z_tanh"], past["z_tanh"] + h - n_silu + 1)
                    nc.vector.scalar_tensor_tensor(out=zT[:, h, :], in0=zT[:, h, :], scalar=1.0, in1=ps[:, 6 + n % 2, :],
                                                   op0=ALU.add, op1=ALU.mult).then_inc(sem["z_gated"], add("z_gated", 1))

                for n in range(4):
                    swap_query(n)
                dve.wait_ge(sem["wi_copied"], past["wi_copied"] + 1)
                for m, (j, h) in enumerate(pairs):
                    n = (j + 1) * P
                    dve.wait_ge(sem["relu"], past["relu"] + m + 1)
                    r, w, s = relu[:, m % 2, 0:n], wi[:, j, h:h + 1], score[:, j, 0:n]
                    if h == 0:
                        ins = nc.vector.tensor_scalar(s, r, w, None, ALU.mult)
                    else:
                        dve.wait_ge(sem["summed"], past["summed"] + m)
                        ins = nc.vector.scalar_tensor_tensor(out=s, in0=r, scalar=w, in1=s, op0=ALU.mult, op1=ALU.add)
                    ins.then_inc(sem["summed"], add("summed", 1))
                    if m % 6 == 5 and 4 + m // 6 < n_scores:
                        swap_query(4 + m // 6)
                dve.wait_ge(sem["summed"], past["summed"] + len(pairs))
                step = "top_step"

                def then(ins):
                    ins.then_inc(sem[step], add(step, 1))
                    dve.wait_ge(sem[step], count[step])

                for j in score_tiles:
                    then(nc.vector.tensor_tensor(score[:, j, j * P:(j + 1) * P], score[:, j, j * P:(j + 1) * P], bias[:, 0, 0:P], ALU.add))
                    n = (j + 1) * P
                    for r in range(TOPK // 8):
                        src = (left if r else score)[:, j, 0:n]
                        then(nc.vector.max(top8[:], src))
                        then(nc.vector.match_replace(left[:, j, 0:n], top8[:], src, TAKEN))
                    then(nc.vector.tensor_tensor(left[:, j, 0:n], left[:, j, 0:n], score[:, j, 0:n], ALU.is_equal))
                    then(nc.vector.tensor_scalar(bias[:, j, 0:n], left[:, j, 0:n], MASKED, None, ALU.mult))

                def mask(h):
                    for j in range(NT):
                        m = NT * h + j
                        i = m % (2 * NT)
                        n = (j + 1) * P
                        dve.wait_ge(sem["logits_ready"], past["logits_ready"] + m + 1)
                        if h >= 2:
                            dve.wait_ge(sem["prob_turned"], past["prob_turned"] + m - 2 * NT + 1)
                        nc.vector.tensor_tensor_reduce(out=prob[:, h % 2, j, 0:n], in0=ps[:, m % 2, 0:n], in1=bias[:, j, 0:n],
                                                                        scale=1.0, scalar=TAKEN, op0=ALU.add, op1=ALU.max, accum_out=peak[:, i:i + 1]).then_inc(sem["masked"], add("masked", 1))
                        dve.wait_ge(sem["masked"], past["masked"] + m + 1)
                        nc.vector.tensor_scalar(shift[:, i:i + 1], peak[:, i:i + 1], -ATTN_SCALE, None, ALU.mult).then_inc(sem["peak_shift"], add("peak_shift", 1))

                def normalise(h):
                    for j in range(NT):
                        m = NT * h + j
                        i = m % (2 * NT)
                        dve.wait_ge(sem["exps"], past["exps"] + m + 1)
                        nc.vector.reciprocal(inv[:, i:i + 1], total[:, i:i + 1]).then_inc(sem["inv_total"], add("inv_total", 1))
                    for j in range(NT):
                        m = NT * h + j
                        i = m % (2 * NT)
                        dve.wait_ge(sem["inv_total"], past["inv_total"] + m + 1)
                        row = prob[:, h % 2, j, 0:(j + 1) * P]
                        nc.vector.tensor_scalar(row, row, inv[:, i:i + 1], None, ALU.mult).then_inc(sem["prob_ready"], add("prob_ready", 1))

                for h in range(2):
                    mask(h)
                    normalise(h)
                for h in range(DSA_HEADS):
                    for j in range(1, NT, 2):
                        m = NT * h + j
                        dve.wait_ge(sem["prob_turned"], past["prob_turned"] + m + 1)
                        if h:
                            dve.wait_ge(sem["o_head"], past["o_head"] + h)
                        nc.vector.tensor_copy(probT[:, 0:j + 1, j * P:(j + 1) * P],
                                                                     ps[:, 2 + m % 2, 0:(j + 1) * P].rearrange("p (i t) -> p i t", t=P)).then_inc(sem["probT_by_dve"], add("probT_by_dve", 1))
                    if h + 2 < DSA_HEADS:
                        mask(h + 2)
                    if n_scores + h < DSA_HEADS:
                        swap_query(n_scores + h)
                    if n_early + h < n_tiles:
                        project(n_early + h)
                    if h + 2 < DSA_HEADS:
                        normalise(h + 2)
                    dve.wait_ge(sem["o_head"], past["o_head"] + h + 1)
                    if h >= 2:
                        dve.wait_ge(sem["head_low"], past["head_low"] + h - 1)
                    nc.vector.scalar_tensor_tensor(out=gated[:, h % 2, :], in0=ps[:, 4 + h % 2, :], scalar=1.0 if h < n_silu else 0.5, in1=zT[:, h, :],
                                                                       op0=ALU.mult, op1=ALU.mult).then_inc(sem["head_done"], add("head_done", 1))
                dve.wait_ge(sem["head_low"], past["head_low"] + DSA_HEADS)

            @block.gpsimd
            def _(pool):
                def rotate(x, slot, cos, sin, done):
                    nc.gpsimd.tensor_tensor(x, x, cos, ALU.mult).then_inc(sem["rope_parts"], add("rope_parts", 1))
                    nc.gpsimd.tensor_tensor(slot, slot, sin, ALU.mult).then_inc(sem["rope_parts"], add("rope_parts", 1))
                    pool.wait_ge(sem["rope_parts"], count["rope_parts"])
                    nc.gpsimd.tensor_tensor(x, x, slot, ALU.add).then_inc(sem[done], add(done, 1))
                    pool.wait_ge(sem[done], count[done])

                def low(h):
                    pool.wait_ge(sem["head_high"], past["head_high"] + h + 1)
                    nc.gpsimd.tensor_tensor(gT[1][:, h, :], gated[:, h % 2, :], gT[0][:, h, :].bitcast(F32), ALU.subtract).then_inc(sem["head_low"], add("head_low", 1))

                R = 2 * HALF
                turns = [0]

                def turn(x, rows, done):
                    n = turns[0]
                    turns[0] += 1
                    pool.wait_ge(sem["swapped"], past["swapped"] + n + 1)
                    rotate(x, rot[0:rows, n % 2, :], g.head_cos[:], g.head_sin[:], done)

                def project(n):
                    if n % PER == PER - 1:
                        g.split_low(pool, c_heads + n // PER + 1 + RING)

                def turn_query(h):
                    turn(qT[0:R, h, :], R, "q_rotated")

                g.split_low(pool, c_heads + RING)
                for n in range(n_early):
                    project(n)
                    if n < n_scores:
                        turn_query(n)
                for h in range(DSA_HEADS):
                    if n_early + h < n_tiles:
                        project(n_early + h)
                    if n_scores + h < DSA_HEADS:
                        turn_query(n_scores + h)
                    low(h)
                g.split_low(pool)

            @block.sync
            def _(sp):
                g.load_chunks(sp)
    g.sem.end_phase()

GH, HD = 4, 64
GW = GH * HD
N_MEM = 256
MT = N_MEM // P
CONV_K = 4
RANK2 = 16
HEAD_SCALE = HD ** -0.5
DECAY_SCALE = float(np.exp(np.float32(-0.5)))
A0, B0 = 0, 3 * GW
C0 = B0 + 4 * GW + GH
D0 = C0 + 5 * GW + 2 * GH
M0 = D0 + 4 * GW + 2 * RANK2
IN2 = M0 + 2 * GW
GATES = 3 * GH
MIX_TILES = 5 * GW // P
SECOND_CHUNKS = {"uA": [(A0, A0 + GW)], "vA": [(A0 + GW, A0 + 2 * GW)], 
                 "qB": [(B0, B0 + GW)], "kB": [(B0 + GW, B0 + 2 * GW)], "qM": [(M0, M0 + GW)], "vB": [(B0 + 2 * GW, B0 + 3 * GW)],
                 "small": [(B0 + 3 * GW, B0 + 3 * GW + GH), (C0 + 3 * GW + GH, C0 + 3 * GW + 2 * GH), (C0 + 3 * GW, C0 + 3 * GW + GH),
                           (D0 + GW, D0 + GW + RANK2), (D0 + 3 * GW + RANK2, D0 + 3 * GW + 2 * RANK2)],
                 "zA": [(A0 + 2 * GW, B0)], "zB": [(B0 + 3 * GW + GH, C0)],
                 "qC": [(C0, C0 + GW)], "kC": [(C0 + GW, C0 + 2 * GW)], "vC": [(C0 + 2 * GW, C0 + 3 * GW)],
                 "oC": [(C0 + 3 * GW + 2 * GH, C0 + 4 * GW + 2 * GH)], "zC": [(C0 + 4 * GW + 2 * GH, D0)],
                 "rD": [(D0, D0 + GW)], "kD": [(D0 + GW + RANK2, D0 + 2 * GW + RANK2)], "vD": [(D0 + 2 * GW + RANK2, D0 + 3 * GW + RANK2)],
                 "zD": [(D0 + 3 * GW + 2 * RANK2, M0)], "zM": [(M0 + GW, IN2)]}


def phase_project(g, s, first):
    nc, t, ps = g.nc, g.t, g.ps
    sem, past, count, add = g.sem, g.sem.past, g.sem.count, g.sem.add
    w2 = {name: i for i, name in enumerate(SECOND_CHUNKS)}
    c_in = first
    end = first + len(w2)
    tiles = []

    def tok(c, col, width, engine, what):
        tiles.extend((w2[c], col, width, j, engine, what) for j in range(NT))

    def fm(c, col, n, engine, what, width=P):
        tiles.extend((w2[c], col + i * width, width, None, engine, (what, i)) for i in range(n))

    tok("uA", 0, GW, "act", "u")
    tok("vA", 0, GW, "act", "v")
    for name in ("qB", "kB", "qM", "vB"):
        tok(name, 0, GW, "dve", name)
    fm("small", 0, 1, "dve", "gates", GATES)
    fm("small", GATES, 1, "dve", "wlo", RANK2)
    fm("small", GATES + RANK2, 1, "dve", "alo", RANK2)
    tiles.append((w2["small"], 0, 0, None, "dve", ("gates_turned", 0)))
    fm("zA", 0, 2, "act", "zA")
    fm("zB", 0, 2, "act", "zB")
    fm("qC", 0, 2, "dve", "qC")
    fm("kC", 0, 2, "dve", "kC")
    tok("vC", 0, GW, "dve", "vC")
    tok("oC", 0, GW, "act", "oC")
    fm("zC", 0, 2, "act", "zC")
    for name in ("rD", "kD", "vD", "zD"):
        fm(name, 0, 2, "dve", name)
    fm("zM", 0, 2, "act", "zM")
    nth = []
    for i, tile in enumerate(tiles):
        nth.append(sum(x[4] == tile[4] for x in tiles[:i + 1]))
    NB = 6
    with ExitStack() as stack:
        per = D // T
        mem = s.mixT[:, 0:MT * per, :].rearrange("p (j k) n -> p j (k n)", j=MT)
        memT = s.mixT[:, 2 * MT:4 * MT, :].rearrange("p a (b n) -> p (a b) n", n=N_MEM)
        msq = s.mixT[:, 4 * MT:4 * MT + per, :].rearrange("p a n -> p (a n)")
        gatesT = s.conv_in[0:GATES, 3, CONV_K - 1:]
        NG = 4 * GH
        heads_from = 5 * NT
        x = s.heads[:, :, 1:5, :]
        sq = [s.mixT[:, 4 * MT + half, :].rearrange("p (a d) -> p a d", d=GW) for half in range(2)]
        ss = s.head_ss
        mss = g.sb(stack, "mss", [P, MT])
        with nc.Block("project", no_gpsimd_drain=True) as block:

            @block.tensor
            def _(pe):
                for i, (c, col, width, j, engine, what) in enumerate(tiles):
                    if i == 0 or c != tiles[i - 1][0]:
                        w = g.chunk(pe, c_in + c)
                    if i >= NB:
                        pe.wait_ge(sem["projected_by_" + tiles[i - NB][4]], past["projected_by_" + tiles[i - NB][4]] + nth[i - NB])
                    if what[0] == "gates_turned":
                        pe.wait_ge(sem["projected_by_dve"], past["projected_by_dve"] + nth[i - 3])
                        for j in range(NT):
                            ins = nc.tensor.transpose(ps[:, i % NB, j * GATES:(j + 1) * GATES], gatesT[:, j * P:(j + 1) * P], g.ident[0:GATES, 0:GATES])
                    for k in range(KD if width else 0):
                        if j is None:
                            ins = g.split_product(ps[0:width, i % NB, :], columns(w, k, slice(col, col + width)), columns(g.xT, k), k == 0, k == KD - 1)
                        else:
                            ins = g.split_product(ps[:, i % NB, 0:width], columns(g.xT, k, slice(j * P, (j + 1) * P)), columns(w, k, slice(col, col + width)), k == 0, k == KD - 1)
                    ins.then_inc(sem["projected"], add("projected", 1))
                    if i + 1 == len(tiles) or tiles[i + 1][0] != c:
                        g.release("projected")
                pe.wait_ge(sem["mem_scaled"], past["mem_scaled"] + MT)
                to_feature_major_pe(g, pe, (0, 0), mem, KD, MT, [6, 7])
                pe.wait_ge(sem["turned_by_act"], past["turned_by_act"] + KD // 2)
                pe.wait_ge(sem["turned_by_dve"], past["turned_by_dve"] + KD // 2)
                for half in range(2):
                    w = g.chunk(pe, end + half)
                    done = "mem_kv" if half else "mem_k"
                    for j in range(MT):
                        for k in range(KD):
                            ins = g.product(ps[:, 6 + j, half * GW:(half + 1) * GW], memT[:, k, j * P:(j + 1) * P], w[:, k, :], k == 0, k == KD - 1)
                        ins.then_inc(sem[done], add(done, 1))
                    g.release(done)

            @block.scalar
            def _(act):
                act.dma_start(mem[:], t["mem_2"][0].rearrange("(j p) d -> p j d", p=P)).then_inc(sem["mem_landed"], add("mem_landed", 16))
                act.dma_start(s.w_sgu[:], t["sgu_w_2"][0].rearrange("g t s -> t g s")).then_inc(sem["w_sgu_landed"], add("w_sgu_landed", 16))
                rows = ((s.gains[:, 0, :].rearrange("p (h d) -> p h d", h=1), t["sgu_norm_g_2"]),
                        (s.gains[:, 1, :].rearrange("p (h d) -> p h d", h=GH), t["fox_q_g_2"]),
                        (s.gains[:, 2, :].rearrange("p (h d) -> p h d", h=GH), t["fox_k_g_2"]),
                        (s.gains[:, 3, :].rearrange("p (h d) -> p h d", h=GH), t["mem_q_g_2"]),
                        (s.gains[:, 4, :].rearrange("p (h d) -> p h d", h=GH), t["mem_k_g_2"]),
                        (s.gains[:, 5, :].rearrange("p (h d) -> p h d", h=1), t["mlstm_out_g_2"]),
                        (s.gains[:, 6, :].rearrange("p (h d) -> p h d", h=1), t["rwkv_ln_g_2"]))
                for dst, v in rows:
                    for h in range(dst.shape[1]):
                        act.dma_start(dst[:, h, :], v.to_broadcast([P, dst.shape[2]])).then_inc(sem["gains_landed"], add("gains_landed", 16))
                for i, name in enumerate(("fox_f_b_2", "mlstm_f_b_2", "mlstm_i_b_2")):
                    act.dma_start(s.gate_bias[:, i * GH:(i + 1) * GH], t[name].to_broadcast([P, GH])).then_inc(sem["gate_bias_landed"], add("gate_bias_landed", 16))
                act.dma_start(s.w2_decay[:], t["rwkv_w2_2"][0]).then_inc(sem["low_rank_landed"], add("low_rank_landed", 16))
                act.dma_start(s.w2_a[:], t["rwkv_a2_2"][0]).then_inc(sem["low_rank_landed"], add("low_rank_landed", 16))
                act.wait_ge(sem["mem_landed"], past["mem_landed"] + 16)
                for j in range(MT):
                    if j:
                        act.wait_ge(sem["mem_squared"], past["mem_squared"] + j)
                    nc.scalar.activation(msq[:], mem[:, j, :], ACT.Square, accum_out=mss[:, j:j + 1]).then_inc(sem["mem_squared"], add("mem_squared", 1))
                act.wait_ge(sem["mem_mean_sq"], past["mem_mean_sq"] + 1)
                nc.scalar.activation(mss[:], mss[:], ACT.Sqrt).then_inc(sem["mem_root"], add("mem_root", 1))
                act.wait_ge(sem["mem_rstd"], past["mem_rstd"] + 1)
                for j in range(MT):
                    nc.scalar.activation(mem[:, j, :], mem[:, j, :], ACT.Copy, scale=mss[:, j:j + 1]).then_inc(sem["mem_scaled"], add("mem_scaled", 1))
                g.split_high(act, c_in + RING)
                last = 0
                for i, (c, col, width, j, engine, what) in enumerate(tiles):
                    if c != last:
                        g.split_high(act, c_in + c + RING)
                        last = c
                    unit = i - heads_from
                    if unit == 0:
                        act.wait_ge(sem["projected_by_act"], past["projected_by_act"] + 2 * NT)
                        act.wait_ge(sem["projected_by_dve"], past["projected_by_dve"] + 3 * NT)
                    if 0 <= unit < 2 * NT:
                        half = unit % 2
                        if unit >= 2:
                            act.wait_ge(sem["head_sums"], past["head_sums"] + unit - 1)
                        nc.scalar.activation(sq[half], x[:, unit // 2, 2 * half:2 * half + 2], ACT.Square).then_inc(sem["head_squared"], add("head_squared", 1))
                    if unit == 2 * NT + 2:
                        act.wait_ge(sem["head_mean_sq"], past["head_mean_sq"] + 1)
                        nc.scalar.activation(ss[:], ss[:], ACT.Sqrt).then_inc(sem["head_root"], add("head_root", 1))
                    if engine != "act":
                        continue
                    src = ps[:, i % NB, :]
                    act.wait_ge(sem["projected"], past["projected"] + i + 1)
                    if what in ("u", "v"):
                        ins = nc.scalar.activation(s.heads[:, j, int(what == "v"), :], src[:, 0:GW], ACT.Gelu_apprx_tanh)
                    elif what == "oC":
                        ins = nc.scalar.activation(s.o_sig[:, j, :], src[:, 0:GW], ACT.Sigmoid)
                    else:
                        tile = {"zA": 0, "zB": 2, "zC": 4, "zM": 6}[what[0]] + what[1]
                        ins = nc.scalar.activation(s.zT[:, tile, :], src, ACT.Silu)
                    ins.then_inc(sem["projected_by_act"], add("projected_by_act", 1))
                to_feature_major_act(g, act, 0, memT, KD, N_MEM, [6, 7], scale=g.col("mem_norm_g_2"))
                for j in range(MT):
                    act.wait_ge(sem["mem_kv"], past["mem_kv"] + j + 1)
                    nc.scalar.activation(s.mem_kv[:, j, :], ps[:, 6 + j, :], ACT.Copy).then_inc(sem["mem_kv_copied"], add("mem_kv_copied", 1))

            @block.vector
            def _(dve):
                nc.vector.memset(s.conv_in[:, :, 0:CONV_K - 1], 0.0).then_inc(sem["pads"], add("pads", 1))
                nc.vector.memset(s.raw[:, :, 0:1], 0.0).then_inc(sem["pads"], add("pads", 1))
                nc.vector.memset(s.low[:, :, 0:1], 0.0).then_inc(sem["pads"], add("pads", 1))
                nc.vector.memset(s.vC[:, :, :, HD:HD + 1], 1.0).then_inc(sem["pads"], add("pads", 1))
                dve.wait_ge(sem["mem_squared"], past["mem_squared"] + MT)
                nc.vector.tensor_scalar(mss[:], mss[:], 1.0 / D, RMS_EPS, ALU.mult, ALU.add).then_inc(sem["mem_mean_sq"], add("mem_mean_sq", 1))
                dve.wait_ge(sem["mem_root"], past["mem_root"] + 1)
                nc.vector.reciprocal(mss[:], mss[:]).then_inc(sem["mem_rstd"], add("mem_rstd", 1))
                dve.wait_ge(sem["gate_bias_landed"], past["gate_bias_landed"] + 48)
                def norm_heads(unit):
                    if 0 <= unit < 2 * NT:
                        j, half = unit // 2, unit % 2
                        dve.wait_ge(sem["head_squared"], past["head_squared"] + unit + 1)
                        nc.vector.tensor_reduce(ss[:, j * NG + half * NG // 2:j * NG + (half + 1) * NG // 2], sq[half].rearrange("p a (h d) -> p (a h) d", d=HD),
                                                AX, ALU.add).then_inc(sem["head_sums"], add("head_sums", 1))
                    elif unit == 2 * NT:
                        dve.wait_ge(sem["head_sums"], past["head_sums"] + 2 * NT)
                        nc.vector.tensor_scalar(ss[:], ss[:], 1.0 / HD, RMS_EPS, ALU.mult, ALU.add).then_inc(sem["head_mean_sq"], add("head_mean_sq", 1))
                    elif unit == 2 * NT + 3:
                        dve.wait_ge(sem["head_root"], past["head_root"] + 1)
                        nc.vector.reciprocal(ss[:], ss[:]).then_inc(sem["head_rstd"], add("head_rstd", 1))
                        dve.wait_ge(sem["gains_landed"], count["gains_landed"])
                    j = unit - 2 * NT - 4
                    if 0 <= j < NT:
                        dve.wait_ge(sem["head_rstd"], past["head_rstd"] + 1)
                        y = x[:, j].rearrange("p a (h d) -> p (a h) d", d=HD)
                        nc.vector.tensor_tensor(y, y, ss[:, j * NG:(j + 1) * NG].unsqueeze(2).to_broadcast([P, NG, HD]), ALU.mult).then_inc(sem["head_scaled"], add("head_scaled", 1))
                    if 0 < j <= NT:
                        dve.wait_ge(sem["head_scaled"], past["head_scaled"] + j)
                        nc.vector.tensor_tensor(x[:, j - 1], x[:, j - 1], s.gains[:, 0:4, :], ALU.mult).then_inc(sem["head_gained"], add("head_gained", 1))

                for i, (c, col, width, j, engine, what) in enumerate(tiles):
                    norm_heads(i - heads_from)
                    if engine != "dve":
                        continue
                    src = ps[:, i % NB, :]
                    dve.wait_ge(sem["projected"], past["projected"] + i + 1)
                    done = "projected_by_dve"
                    part = "projected_part"
                    if what == "qB":
                        nc.vector.tensor_copy(s.heads[:, j, 2, :], src[:, 0:GW]).then_inc(sem[done], add(done, 1))
                    elif what == "kB":
                        nc.vector.tensor_copy(s.heads[:, j, 3, :], src[:, 0:GW]).then_inc(sem[done], add(done, 1))
                    elif what == "vB":
                        nc.vector.tensor_copy(s.vB[:, j, :], src[:, 0:GW]).then_inc(sem[done], add(done, 1))
                    elif what[0] == "gates":
                        nc.vector.tensor_copy(gatesT, src[0:GATES, :]).then_inc(sem[done], add(done, 1))
                    elif what[0] == "gates_turned":
                        nc.vector.tensor_tensor(s.gates[:], src[:, 0:NT * GATES].rearrange("p (j a) -> p j a", j=NT),
                                                s.gate_bias[:].unsqueeze(1).to_broadcast([P, NT, GATES]), ALU.add).then_inc(sem[done], add(done, 1))
                    elif what == "vC":
                        nc.vector.tensor_copy(s.vC[:, j, :, 0:HD], src[:, 0:GW].rearrange("p (h d) -> p h d", h=GH)).then_inc(sem[done], add(done, 1))
                    elif what == "qM":
                        nc.vector.tensor_copy(s.heads[:, j, 4, :], src[:, 0:GW]).then_inc(sem[done], add(done, 1))
                    elif what[0] in ("qC", "kC"):
                        nc.vector.tensor_copy(s.conv_in[:, 2 * int(what[0] == "kC") + what[1], CONV_K - 1:], src).then_inc(sem[done], add(done, 1))
                    elif what[0] in ("wlo", "alo"):
                        nc.vector.tensor_copy(s.low[:, int(what[0] == "alo"), 1:], src[0:RANK2, :]).then_inc(sem[done], add(done, 1))
                    else:
                        tile = {"rD": 0, "kD": 2, "vD": 4, "zD": 6}[what[0]] + what[1]
                        nc.vector.tensor_copy(s.raw[:, tile, 1:], src).then_inc(sem[done], add(done, 1))
                to_feature_major_dve(g, dve, 0, memT, KD, N_MEM, [6, 7], scale=g.col("mem_norm_g_2"))
                dve.wait_ge(sem["gains_landed"], count["gains_landed"])
                dve.wait_ge(sem["low_rank_landed"], past["low_rank_landed"] + 32)
                dve.wait_ge(sem["w_sgu_landed"], past["w_sgu_landed"] + 16)

            @block.gpsimd
            def _(pool):
                g.split_low(pool)

            @block.sync
            def _(sp):
                g.load_chunks(sp)
    g.sem.end_phase()


def phase_heads(g, s):
    nc, t, ps = g.nc, g.t, g.ps
    sem, past, count, add = g.sem, g.sem.past, g.sem.count, g.sem.add
    with ExitStack() as stack:
        ksq = s.mixT[:, 0, :].rearrange("p (j d) -> p j d", j=MT)
        ss = g.sb(stack, "mem_ss", [P, MT * GH])
        la = g.sb(stack, "log_abs", [P, NT, 2 * GH])
        lg = g.sb(stack, "log_gates", [P, NT, 2 * GH])
        k_mem = s.mem_kv[:, :, 0:GW]
        with nc.Block("heads", no_gpsimd_drain=True) as block:

            @block.scalar
            def _(act):
                nc.scalar.activation(la[:], s.gates[:, :, 0:2 * GH], ACT.Abs).then_inc(sem["gate_abs"], add("gate_abs", 1))
                act.wait_ge(sem["gate_abs"], past["gate_abs"] + 1)
                nc.scalar.activation(la[:], la[:], ACT.Exp, scale=-1.0).then_inc(sem["gate_exp"], add("gate_exp", 1))
                act.wait_ge(sem["gate_exp"], past["gate_exp"] + 1)
                nc.scalar.activation(la[:], la[:], ACT.Ln, bias=1.0).then_inc(sem["gate_ln"], add("gate_ln", 1))
                nc.scalar.activation(ksq[:], k_mem, ACT.Square).then_inc(sem["head_squared"], add("head_squared", 1))
                act.wait_ge(sem["head_mean_sq"], past["head_mean_sq"] + 1)
                nc.scalar.activation(ss[:], ss[:], ACT.Sqrt).then_inc(sem["head_root"], add("head_root", 1))

            @block.tensor
            def _(pe):
                for h in range(GH):
                    ins = nc.tensor.transpose(ps[:, 1, h * P:(h + 1) * P], s.w_sgu[:, h, :], g.ident[:])
                ins.then_inc(sem["w_sgu_turned"], add("w_sgu_turned", 1))

                def gating(pair):
                    for j in range(2 * pair, 2 * pair + 2):
                        for h in range(GH):
                            ins = g.product(ps[:, 4 + pair, (j % 2) * GW + h * HD:(j % 2) * GW + (h + 1) * HD], s.w_sguT[:, h, :], s.heads[:, j, 1, h * HD:(h + 1) * HD])
                    ins.then_inc(sem["sgu_mixed"], add("sgu_mixed", 1))

                pe.wait_ge(sem["w_sgu_masked"], past["w_sgu_masked"] + 1)
                gating(0)
                pe.wait_ge(sem["log_gates"], past["log_gates"] + 1)
                for j in range(NT):
                    for i in range(j + 1):
                        ins = g.product(ps[:, 0, j * 2 * GH:(j + 1) * 2 * GH], (g.ones if i < j else g.not_before)[:], lg[:, i, :], i == 0, i == j, check=False)
                ins.then_inc(sem["cum_ready"], add("cum_ready", 1))
                gating(1)
                pe.wait_ge(sem["sgu_y"], past["sgu_y"] + GH)
                to_gated(g, pe, s.heads[:, :, 0, :], [2, 3])

            @block.vector
            def _(dve):
                dve.wait_ge(sem["w_sgu_turned"], past["w_sgu_turned"] + 1)
                nc.vector.tensor_tensor(s.w_sguT[:], ps[:, 1, :].rearrange("p (h t) -> p h t", h=GH),
                                                               g.not_before[:].unsqueeze(1).to_broadcast([P, GH, P]), ALU.mult).then_inc(sem["w_sgu_masked"], add("w_sgu_masked", 1))
                dve.wait_ge(sem["gate_ln"], past["gate_ln"] + 1)
                nc.vector.scalar_tensor_tensor(out=lg[:], in0=s.gates[:, :, 0:2 * GH], scalar=0.0, in1=la[:],
                                                                   op0=ALU.min, op1=ALU.subtract).then_inc(sem["log_gates"], add("log_gates", 1))
                dve.wait_ge(sem["head_squared"], past["head_squared"] + 1)
                nc.vector.tensor_reduce(ss[:], ksq[:].rearrange("p j (h d) -> p (j h) d", d=HD), AX, ALU.add).then_inc(sem["head_sums"], add("head_sums", 1))
                dve.wait_ge(sem["head_sums"], past["head_sums"] + 1)
                nc.vector.tensor_scalar(ss[:], ss[:], 1.0 / HD, RMS_EPS, ALU.mult, ALU.add).then_inc(sem["head_mean_sq"], add("head_mean_sq", 1))
                dve.wait_ge(sem["head_root"], past["head_root"] + 1)
                nc.vector.reciprocal(ss[:], ss[:]).then_inc(sem["head_rstd"], add("head_rstd", 1))
                dve.wait_ge(sem["head_rstd"], past["head_rstd"] + 1)
                y = k_mem.rearrange("p j (h d) -> p j h d", d=HD)
                for j in range(MT):
                    nc.vector.tensor_tensor(y[:, j], y[:, j], ss[:, j * GH:(j + 1) * GH].unsqueeze(2).to_broadcast([P, GH, HD]), ALU.mult).then_inc(sem["head_scaled"], add("head_scaled", 1))
                for j in range(MT):
                    dve.wait_ge(sem["head_scaled"], past["head_scaled"] + j + 1)
                    nc.vector.tensor_tensor(k_mem[:, j, :], k_mem[:, j, :], s.gains[:, 4, :], ALU.mult).then_inc(sem["head_gained"], add("head_gained", 1))
                dve.wait_ge(sem["cum_ready"], past["cum_ready"] + 1)
                nc.vector.tensor_copy(s.cum[:], ps[:, 0, 0:NT * 2 * GH].rearrange("p (j h) -> p j h", j=NT)).then_inc(sem["cum_copied"], add("cum_copied", 1))
                q, k = s.fox_qk[:, :, 0], s.fox_qk[:, :, 1]
                dve.wait_ge(sem["cum_copied"], past["cum_copied"] + 1)
                for j in range(NT):
                    f = s.cum[:, j, 0:GH].unsqueeze(2)
                    nc.vector.tensor_scalar(q[:, j, :, 0:HD], s.heads[:, j, 2, :].rearrange("p (h d) -> p h d", h=GH), HEAD_SCALE, None, ALU.mult).then_inc(sem["fox_parts"], add("fox_parts", 1))
                    nc.vector.tensor_copy(k[:, j, :, 0:HD], s.heads[:, j, 3, :].rearrange("p (h d) -> p h d", h=GH)).then_inc(sem["fox_parts"], add("fox_parts", 1))
                    nc.vector.tensor_copy(q[:, j, :, HD:HD + 1], f).then_inc(sem["fox_parts"], add("fox_parts", 1))
                    nc.vector.tensor_scalar(k[:, j, :, HD + 1:HD + 2], f, -1.0, None, ALU.mult).then_inc(sem["fox_parts"], add("fox_parts", 1))
                    nc.vector.memset(q[:, j, :, HD + 1:HD + 2], 1.0).then_inc(sem["fox_parts"], add("fox_parts", 1))
                    nc.vector.memset(k[:, j, :, HD:HD + 1], 1.0).then_inc(sem["fox_parts"], add("fox_parts", 1))
                nc.vector.tensor_tensor(s.a_tok[:], s.gates[:, :, 2 * GH:3 * GH], s.cum[:, :, GH:2 * GH], ALU.subtract).then_inc(sem["a_made"], add("a_made", 1))
                dve.wait_ge(sem["sgu_mixed"], past["sgu_mixed"] + 2)
                for h in range(GH):
                    u = s.heads[:, :, 0, h * HD:(h + 1) * HD]
                    mixed = ps[:, 4:6, :].rearrange("p b (j d) -> p (b j) d", j=2)[:, :, h * HD:(h + 1) * HD]
                    nc.vector.scalar_tensor_tensor(out=u, in0=mixed, scalar=g.col("sgu_b")[:, h:h + 1], in1=u, op0=ALU.add, op1=ALU.mult).then_inc(sem["sgu_y"], add("sgu_y", 1))
                gate_turned(g, dve, s, 0, 0, [2, 3])

            @block.sync
            def _(sp):
                g.load_chunks(sp)
    g.sem.end_phase()


def to_gated(g, pe, y, banks):
    sem, add = g.sem, g.sem.add
    for i in range(2):
        for j in range(NT):
            ins = g.nc.tensor.transpose(g.ps[:, banks[i], j * P:(j + 1) * P], y[:, j, i * P:(i + 1) * P], g.ident[:])
        ins.then_inc(sem["y_turned"], add("y_turned", 1))


def gate_turned(g, dve, s, mix_tile, z_tile, banks):
    sem, past, add = g.sem, g.sem.past, g.sem.add
    for i in range(2):
        dve.wait_ge(sem["y_turned"], past["y_turned"] + i + 1)
        g.nc.vector.tensor_tensor(s.mixT[:, mix_tile + i, :], g.ps[:, banks[i], :], s.zT[:, z_tile + i, :], ALU.mult).then_inc(sem["y_gated"], add("y_gated", 1))


def phase_fox(g, s):
    nc, t, ps = g.nc, g.t, g.ps
    sem, past, count, add = g.sem, g.sem.past, g.sem.count, g.sem.add
    K = HD + 2
    with ExitStack() as stack:
        prob = g.room[:, 0].rearrange("p (b j) n -> p b j n", b=2)
        probT = g.room[:, 1, 0:NT]
        qT, kT = g.room[0:K, 1, NT:NT + GH], g.room[0:K, 2, 0:GH]
        bias = g.room[:, 2, GH, :]
        peak = g.sb(stack, "fox_peak", [P, GH * NT])
        shift = g.sb(stack, "fox_shift", [P, GH * NT])
        total = g.sb(stack, "fox_total", [P, GH * NT])
        inv = g.sb(stack, "fox_inv", [P, GH * NT])
        with nc.Block("fox", no_gpsimd_drain=True) as block:

            @block.tensor
            def _(pe):
                for h in range(GH):
                    for a in range(2):
                        n = 2 * h + a
                        if n >= 2:
                            pe.wait_ge(sem["fox_T_copied"], past["fox_T_copied"] + n - 1)
                        for j in range(NT):
                            ins = nc.tensor.transpose(ps[0:K, 6 + n % 2, j * P:(j + 1) * P], s.fox_qk[:, j, a, h, :], g.ident[:])
                        ins.then_inc(sem["fox_turned"], add("fox_turned", 1))

                def logits(h):
                    pe.wait_ge(sem["fox_T_copied"], past["fox_T_copied"] + 2 * h + 2)
                    for j in range(NT):
                        m = NT * h + j
                        if m >= 2:
                            pe.wait_ge(sem["fox_masked"], past["fox_masked"] + m - 1)
                        n = (j + 1) * P
                        g.product(ps[:, m % 2, 0:n], qT[:, h, j * P:(j + 1) * P], kT[:, h, 0:n]).then_inc(sem["fox_logits"], add("fox_logits", 1))

                logits(0)
                for h in range(GH):
                    if h + 1 < GH:
                        logits(h + 1)
                    for j in range(NT):
                        m = NT * h + j
                        pe.wait_ge(sem["fox_prob"], past["fox_prob"] + m + 1)
                        if m >= 2:
                            pe.wait_ge(sem["fox_probT"], past["fox_probT"] + m - 1)
                        for i in range(j + 1):
                            ins = nc.tensor.transpose(ps[:, 2 + m % 2, i * P:(i + 1) * P], prob[:, h % 2, j, i * P:(i + 1) * P], g.ident[:])
                        ins.then_inc(sem["fox_prob_turned"], add("fox_prob_turned", 1))
                    pe.wait_ge(sem["fox_probT"], past["fox_probT"] + NT * h + NT)
                    if h >= 2:
                        pe.wait_ge(sem["fox_done"], past["fox_done"] + h - 1)
                    rows = slice((h % 2) * HD, (h % 2 + 1) * HD)
                    for i in range(NT):
                        ins = g.product(ps[rows, 4 + h % 2, i * P:T], s.vB[:, i, h * HD:(h + 1) * HD], probT[:, i, i * P:T], i == 0, i == NT - 1, check=False)
                    ins.then_inc(sem["fox_o"], add("fox_o", 1))

            @block.scalar
            def _(act):
                for h in range(GH):
                    for j in range(NT):
                        m = NT * h + j
                        row = prob[:, h % 2, j, 0:(j + 1) * P]
                        act.wait_ge(sem["fox_shift"], past["fox_shift"] + m + 1)
                        nc.scalar.activation(row, row, ACT.Exp, bias=shift[:, m:m + 1], accum_out=total[:, m:m + 1]).then_inc(sem["fox_exp"], add("fox_exp", 1))
                    for j in range(NT):
                        m = NT * h + j
                        act.wait_ge(sem["fox_prob_turned"], past["fox_prob_turned"] + m + 1)
                        if h:
                            act.wait_ge(sem["fox_o"], past["fox_o"] + h)
                        nc.scalar.activation(probT[:, 0:j + 1, j * P:(j + 1) * P],
                                                                 ps[:, 2 + m % 2, 0:(j + 1) * P].rearrange("p (i t) -> p i t", t=P), ACT.Copy).then_inc(sem["fox_probT"], add("fox_probT", 1))

            @block.vector
            def _(dve):
                nc.vector.memset(bias[:, 0:T - P], 0.0).then_inc(sem["fox_bias"], add("fox_bias", 1))
                nc.vector.tensor_scalar(bias[:, T - P:T], g.after[:], MASKED, None, ALU.mult).then_inc(sem["fox_bias"], add("fox_bias", 1))
                for n in range(2 * GH):
                    dve.wait_ge(sem["fox_turned"], past["fox_turned"] + n + 1)
                    nc.vector.tensor_copy((kT if n % 2 else qT)[:, n // 2, :], ps[0:K, 6 + n % 2, :]).then_inc(sem["fox_T_copied"], add("fox_T_copied", 1))
                dve.wait_ge(sem["fox_bias"], past["fox_bias"] + 2)

                def mask(h):
                    for j in range(NT):
                        m = NT * h + j
                        n = (j + 1) * P
                        dve.wait_ge(sem["fox_logits"], past["fox_logits"] + m + 1)
                        if h >= 2:
                            dve.wait_ge(sem["fox_prob_turned"], past["fox_prob_turned"] + m - 2 * NT + 1)
                        nc.vector.tensor_tensor_reduce(out=prob[:, h % 2, j, 0:n], in0=ps[:, m % 2, 0:n], in1=bias[:, T - n:T],
                                                                            scale=1.0, scalar=TAKEN, op0=ALU.add, op1=ALU.max, accum_out=peak[:, m:m + 1]).then_inc(sem["fox_masked"], add("fox_masked", 1))
                        dve.wait_ge(sem["fox_masked"], past["fox_masked"] + m + 1)
                        nc.vector.tensor_scalar(shift[:, m:m + 1], peak[:, m:m + 1], -1.0, None, ALU.mult).then_inc(sem["fox_shift"], add("fox_shift", 1))

                def normalise(h):
                    for j in range(NT):
                        m = NT * h + j
                        dve.wait_ge(sem["fox_exp"], past["fox_exp"] + m + 1)
                        nc.vector.reciprocal(inv[:, m:m + 1], total[:, m:m + 1]).then_inc(sem["fox_inv"], add("fox_inv", 1))
                        dve.wait_ge(sem["fox_inv"], past["fox_inv"] + m + 1)
                        row = prob[:, h % 2, j, 0:(j + 1) * P]
                        nc.vector.tensor_scalar(row, row, inv[:, m:m + 1], None, ALU.mult).then_inc(sem["fox_prob"], add("fox_prob", 1))

                mask(0)
                normalise(0)
                for h in range(GH):
                    if h + 1 < GH:
                        mask(h + 1)
                        normalise(h + 1)
                    rows = slice((h % 2) * HD, (h % 2 + 1) * HD)
                    dve.wait_ge(sem["fox_o"], past["fox_o"] + h + 1)
                    nc.vector.tensor_tensor(s.mixT[rows, 2 + h // 2, :], ps[rows, 4 + h % 2, :], s.zT[rows, 2 + h // 2, :], ALU.mult).then_inc(sem["fox_done"], add("fox_done", 1))

            @block.gpsimd
            def _(pool):
                for i in range(8):
                    x, previous = s.raw[:, i, 1:], s.raw[:, i, 0:T]
                    out = s.shifted[:, i, :]
                    nc.gpsimd.tensor_tensor(out, previous, x, ALU.subtract).then_inc(sem["shift_step"], add("shift_step", 1))
                    pool.wait_ge(sem["shift_step"], count["shift_step"])
                    nc.gpsimd.tensor_scalar(out, out, g.col("mu")[:, i:i + 1], None, ALU.mult).then_inc(sem["shift_step"], add("shift_step", 1))
                    pool.wait_ge(sem["shift_step"], count["shift_step"])
                    nc.gpsimd.tensor_tensor(out, out, x, ALU.add).then_inc(sem["shifted"], add("shifted", 1))

            @block.sync
            def _(sp):
                g.load_chunks(sp)
                sp.wait_ge(sem["shifted"], past["shifted"] + 8)
    g.sem.end_phase()


def phase_mem(g, s):
    nc, t, ps = g.nc, g.t, g.ps
    sem, past, count, add = g.sem, g.sem.past, g.sem.count, g.sem.add
    PAIRS = GH // 2
    with ExitStack() as stack:
        qT = g.room[:, 1, 2:2 + PAIRS, :]
        kT = g.room[:, 1, 4, :].rearrange("p (a m) -> p a m", a=PAIRS)
        prob = g.room[:, 0, 0:NT].rearrange("p (b j) (i m) -> p b (j i) m", b=2, m=N_MEM)
        probT = g.room[:, 1, 0:MT]
        conv = g.room[:, 2, 0:4, :]
        taps = g.col("conv_w")
        peak = g.sb(stack, "mem_peak", [P, GH, NT])
        total = g.sb(stack, "mem_total", [P, GH * NT])
        inv = g.sb(stack, "mem_inv", [P, GH, NT])
        with nc.Block("memory", no_gpsimd_drain=True) as block:

            @block.tensor
            def _(pe):
                for i in range(PAIRS):
                    for j in range(NT):
                        ins = nc.tensor.transpose(ps[:, 6, j * P:(j + 1) * P], s.heads[:, j, 4, i * P:(i + 1) * P], g.ident[:])
                    for j in range(MT):
                        ins = nc.tensor.transpose(ps[:, 7, j * P:(j + 1) * P], s.mem_kv[:, j, i * P:(i + 1) * P], g.ident[:])
                    ins.then_inc(sem["mem_turned"], add("mem_turned", 1))
                    pe.wait_ge(sem["mem_T_copied"], past["mem_T_copied"] + 2 * i + 2)

                def logits(h):
                    rows = slice((h % 2) * HD, (h % 2 + 1) * HD)
                    for j in range(NT):
                        b = 2 * h + j // 2
                        if b >= 4 and j % 2 == 0:
                            pe.wait_ge(sem["mem_exp"], past["mem_exp"] + 2 * (b - 4) + 2)
                        ins = g.product(ps[:, b % 4, (j % 2) * N_MEM:(j % 2 + 1) * N_MEM], qT[rows, h // 2, j * P:(j + 1) * P], kT[rows, h // 2, :])
                        if j % 2:
                            ins.then_inc(sem["mem_logits"], add("mem_logits", 1))

                logits(0)
                for h in range(GH):
                    if h + 1 < GH:
                        logits(h + 1)
                    for i in range(MT):
                        n = MT * h + i
                        if n >= 2:
                            pe.wait_ge(sem["mem_probT"], past["mem_probT"] + n - 1)
                        pe.wait_ge(sem["mem_prob"], past["mem_prob"] + h + 1)
                        for j in range(NT):
                            ins = nc.tensor.transpose(ps[:, 4 + n % 2, j * P:(j + 1) * P], prob[:, h % 2, j, i * P:(i + 1) * P], g.ident[:])
                        ins.then_inc(sem["mem_prob_turned"], add("mem_prob_turned", 1))
                    pe.wait_ge(sem["mem_probT"], past["mem_probT"] + MT * h + MT)
                    if h >= 2:
                        pe.wait_ge(sem["mem_done"], past["mem_done"] + h - 1)
                    rows = slice((h % 2) * HD, (h % 2 + 1) * HD)
                    for i in range(MT):
                        ins = g.product(ps[rows, 6 + h % 2, :], s.mem_kv[:, i, GW + h * HD:GW + (h + 1) * HD], probT[:, i, :], i == 0, i == MT - 1)
                    ins.then_inc(sem["mem_o"], add("mem_o", 1))

            @block.scalar
            def _(act):
                def exps(h):
                    act.wait_ge(sem["mem_peak"], past["mem_peak"] + 2 * h + 2)
                    for j in range(NT):
                        if h >= 2:
                            act.wait_ge(sem["mem_prob_turned"], past["mem_prob_turned"] + MT * (h - 2) + MT)
                        b = 2 * h + j // 2
                        nc.scalar.activation(prob[:, h % 2, j, :], ps[:, b % 4, (j % 2) * N_MEM:(j % 2 + 1) * N_MEM], ACT.Exp,
                                                               bias=peak[:, h, j:j + 1], scale=HEAD_SCALE, accum_out=total[:, h * NT + j:h * NT + j + 1]).then_inc(sem["mem_exp"], add("mem_exp", 1))

                exps(0)
                for h in range(GH):
                    if h + 1 < GH:
                        exps(h + 1)
                    for i in range(MT):
                        act.wait_ge(sem["mem_prob_turned"], past["mem_prob_turned"] + MT * h + i + 1)
                        if h:
                            act.wait_ge(sem["mem_o"], past["mem_o"] + h)
                        nc.scalar.activation(probT[:, i, :], ps[:, 4 + (MT * h + i) % 2, :], ACT.Copy).then_inc(sem["mem_probT"], add("mem_probT", 1))
                    if h == 1:
                        act.wait_ge(sem["low_shifted"], past["low_shifted"] + 2)
                        nc.scalar.activation(s.low_shifted[:, 0, :], s.low_shifted[:, 0, :], ACT.Tanh).then_inc(sem["low_tanh"], add("low_tanh", 1))
                    elif h == 2:
                        act.wait_ge(sem["kk"], past["kk"] + PAIRS)
                        nc.scalar.activation(s.kk_norm[:], s.kk[:], ACT.Square).then_inc(sem["kk_sq"], add("kk_sq", 1))
                for i in range(4):
                    act.wait_ge(sem["convolved"], past["convolved"] + CONV_K * (i + 1))
                    nc.scalar.activation(s.qkT[:, i, :], conv[:, i, :], ACT.Silu, bias=g.col("conv_b")[:, i:i + 1]).then_inc(sem["conv_silu"], add("conv_silu", 1))

            @block.gpsimd
            def _(pool):
                for i in range(2):
                    mu = g.col("mu_wlo" if i == 0 else "mu_alo")[0:RANK2, 0:1]
                    out, x = s.low_shifted[:, i, :], s.low[:, i, 1:]
                    nc.gpsimd.tensor_tensor(out, s.low[:, i, 0:T], x, ALU.subtract).then_inc(sem["low_step"], add("low_step", 1))
                    pool.wait_ge(sem["low_step"], count["low_step"])
                    nc.gpsimd.tensor_scalar(out, out, mu, None, ALU.mult).then_inc(sem["low_step"], add("low_step", 1))
                    pool.wait_ge(sem["low_step"], count["low_step"])
                    nc.gpsimd.tensor_tensor(out, out, x, ALU.add).then_inc(sem["low_shifted"], add("low_shifted", 1))
                for i in range(PAIRS):
                    nc.gpsimd.tensor_scalar(s.kk[:, i, :], s.shifted[:, PAIRS + i, :], g.col("k_k")[:, i:i + 1], None, ALU.mult).then_inc(sem["kk"], add("kk", 1))

            @block.vector
            def _(dve):
                for i in range(PAIRS):
                    dve.wait_ge(sem["mem_turned"], past["mem_turned"] + i + 1)
                    nc.vector.tensor_copy(qT[:, i, :], ps[:, 6, :]).then_inc(sem["mem_T_copied"], add("mem_T_copied", 1))
                    nc.vector.tensor_copy(kT[:, i, :], ps[:, 7, 0:N_MEM]).then_inc(sem["mem_T_copied"], add("mem_T_copied", 1))

                def peaks(h):
                    for b in range(2):
                        dve.wait_ge(sem["mem_logits"], past["mem_logits"] + 2 * h + b + 1)
                        nc.vector.tensor_reduce(peak[:, h, 2 * b:2 * b + 2], ps[:, (2 * h + b) % 4, :].rearrange("p (j m) -> p j m", j=2), AX, ALU.max).then_inc(sem["mem_max"], add("mem_max", 1))
                    for b in range(2):
                        dve.wait_ge(sem["mem_max"], past["mem_max"] + 2 * h + b + 1)
                        nc.vector.tensor_scalar(peak[:, h, 2 * b:2 * b + 2], peak[:, h, 2 * b:2 * b + 2], -HEAD_SCALE, None, ALU.mult).then_inc(sem["mem_peak"], add("mem_peak", 1))

                def normalise(h):
                    dve.wait_ge(sem["mem_exp"], past["mem_exp"] + NT * h + NT)
                    nc.vector.reciprocal(inv[:, h, :], total[:, h * NT:(h + 1) * NT]).then_inc(sem["mem_inv"], add("mem_inv", 1))
                    dve.wait_ge(sem["mem_inv"], past["mem_inv"] + h + 1)
                    nc.vector.tensor_tensor(prob[:, h % 2], prob[:, h % 2], inv[:, h, :].unsqueeze(2).to_broadcast([P, NT, N_MEM]), ALU.mult).then_inc(sem["mem_prob"], add("mem_prob", 1))

                def convolve(i):
                    for a in range(CONV_K):
                        src = s.conv_in[:, i, a:a + T]
                        w = taps[:, a * 4 + i:a * 4 + i + 1]
                        if a == 0:
                            ins = nc.vector.tensor_scalar(conv[:, i, :], src, w, None, ALU.mult)
                        else:
                            dve.wait_ge(sem["convolved"], past["convolved"] + CONV_K * i + a)
                            ins = nc.vector.scalar_tensor_tensor(out=conv[:, i, :], in0=src, scalar=w, in1=conv[:, i, :], op0=ALU.mult, op1=ALU.add)
                        ins.then_inc(sem["convolved"], add("convolved", 1))

                peaks(0)
                normalise(0)
                for h in range(GH):
                    if h + 1 < GH:
                        peaks(h + 1)
                        normalise(h + 1)
                    convolve(h)
                    rows = slice((h % 2) * HD, (h % 2 + 1) * HD)
                    dve.wait_ge(sem["mem_o"], past["mem_o"] + h + 1)
                    nc.vector.tensor_tensor(s.mixT[rows, 8 + h // 2, :], ps[rows, 6 + h % 2, :], s.zT[rows, 6 + h // 2, :], ALU.mult).then_inc(sem["mem_done"], add("mem_done", 1))

            @block.sync
            def _(sp):
                g.load_chunks(sp)
    g.sem.end_phase()


def phase_mlstm(g, s):
    nc, t, ps = g.nc, g.t, g.ps
    sem, past, count, add = g.sem, g.sem.past, g.sem.count, g.sem.add
    PAIRS = GH // 2
    with ExitStack() as stack:
        a_row, mu_row = g.room[0:GH, 2, 4, :], g.room[0:GH, 2, 5, :]
        pick = g.room[0:GH, 2, 6, :].rearrange("p (h t) -> p h t", h=GH)
        mu = g.sb(stack, "mu", [P, NT, GH])
        floor = g.sb(stack, "floor", [P, NT, GH])
        weight, score = (g.room[:, i].rearrange("p (b j) n -> p b j n", b=2) for i in range(2))
        den = g.sb(stack, "den", [P, NT, GH])
        y, sq = (g.room[:, 2, 2 * i:2 * i + 2, :].rearrange("p a (b d) -> p (a b) d", d=GW) for i in range(2))
        ss = g.sb(stack, "mlstm_ss", [P, NT * GH])
        W = HD + 1
        with nc.Block("mlstm", no_gpsimd_drain=True) as block:

            @block.tensor
            def _(pe):
                for j in range(NT):
                    ins = nc.tensor.transpose(ps[0:GH, 0, j * P:(j + 1) * P], s.a_tok[:, j, :], g.ident[:])
                ins.then_inc(sem["a_turned"], add("a_turned", 1))
                for i in range(PAIRS):
                    g.product(ps[:, 2 + i, :], g.same64[:], s.kk_norm[:, i, :]).then_inc(sem["kk_sums"], add("kk_sums", 1))
                for i in range(PAIRS):
                    g.product(ps[:, 4 + i, :], s.w2_decay[:, i * P:(i + 1) * P], s.low_shifted[:, 0, :]).then_inc(sem["decay_in"], add("decay_in", 1))
                pe.wait_ge(sem["mu_row"], past["mu_row"] + 1)
                for j in range(NT):
                    ins = nc.tensor.transpose(ps[:, 1, j * GH:(j + 1) * GH], mu_row[:, j * P:(j + 1) * P], g.ident[0:GH, 0:GH])
                ins.then_inc(sem["mu_turned"], add("mu_turned", 1))
                for i in range(PAIRS):
                    g.product(ps[:, 6 + i, :], s.w2_a[:, i * P:(i + 1) * P], s.low_shifted[:, 1, :]).then_inc(sem["a_in"], add("a_in", 1))
                pe.wait_ge(sem["mu_copied"], past["mu_copied"] + 1)
                pe.wait_ge(sem["pick"], past["pick"] + GH)

                def spread(h):
                    if h:
                        pe.wait_ge(sem["weight_log"], past["weight_log"] + NT * h)
                    g.product(ps[:, 0, :], pick[:, h, :], mu_row[:]).then_inc(sem["mu_spread"], add("mu_spread", 1))

                def products(h):
                    rows = slice((h % 2) * HD, (h % 2 + 1) * HD)
                    for i in range(NT):
                        m = NT * h + i
                        if m >= 3:
                            pe.wait_ge(sem["weighted"], past["weighted"] + m - 2)
                        g.product(ps[:, 1 + m % 3, i * P:T], s.qkT[rows, 2 + h // 2, i * P:(i + 1) * P], s.qkT[rows, h // 2, i * P:T]).then_inc(sem["mlstm_scores"], add("mlstm_scores", 1))

                spread(0)
                spread(1)
                pe.wait_ge(sem["kk_root"], past["kk_root"] + PAIRS)
                products(0)
                pe.wait_ge(sem["decay_sigmoid"], past["decay_sigmoid"] + PAIRS)
                pe.wait_ge(sem["a_sigmoid"], past["a_sigmoid"] + PAIRS)
                for h in range(GH):
                    if h + 2 < GH:
                        spread(h + 2)
                    if h + 1 < GH:
                        products(h + 1)
                    pe.wait_ge(sem["weighted"], past["weighted"] + NT * h + NT)
                    for j in range(NT):
                        for i in range(j + 1):
                            ins = g.product(ps[:, 4 + j, h * W:(h + 1) * W], score[:, h % 2, i, j * P:(j + 1) * P], s.vC[:, i, h, :], i == 0, i == j, check=False)
                    ins.then_inc(sem["mlstm_num"], add("mlstm_num", 1))
                pe.wait_ge(sem["mlstm_gained"], past["mlstm_gained"] + 1)
                to_gated(g, pe, y, [0, 1])

            @block.scalar
            def _(act):
                for i in range(PAIRS):
                    act.wait_ge(sem["kk_sums"], past["kk_sums"] + PAIRS)
                    nc.scalar.activation(s.kk_norm[:, i, :], ps[:, 2 + i, :], ACT.Sqrt).then_inc(sem["kk_root"], add("kk_root", 1))
                for i in range(PAIRS):
                    act.wait_ge(sem["decay_in"], past["decay_in"] + i + 1)
                    nc.scalar.activation(s.decay[:, i, :], ps[:, 4 + i, :], ACT.Sigmoid, bias=g.col("w0")[:, i:i + 1]).then_inc(sem["decay_sigmoid"], add("decay_sigmoid", 1))
                for i in range(PAIRS):
                    act.wait_ge(sem["a_in"], past["a_in"] + i + 1)
                    nc.scalar.activation(s.a_gate[:, i, :], ps[:, 6 + i, :], ACT.Sigmoid, bias=g.col("a0")[:, i:i + 1]).then_inc(sem["a_sigmoid"], add("a_sigmoid", 1))
                act.wait_ge(sem["m_made"], past["m_made"] + 1)
                nc.scalar.activation(floor[:], floor[:], ACT.Exp, scale=-1.0).then_inc(sem["floor"], add("floor", 1))
                for h in range(GH):
                    for i in range(NT):
                        m = NT * h + i
                        act.wait_ge(sem["weight_log"], past["weight_log"] + m + 1)
                        w = weight[:, h % 2, i, i * P:T]
                        nc.scalar.activation(w, w, ACT.Exp).then_inc(sem["weight"], add("weight", 1))
                act.wait_ge(sem["before"], past["before"] + 1)
                nc.scalar.activation(s.decay[:], s.decay[:], ACT.Exp, scale=-DECAY_SCALE).then_inc(sem["decays"], add("decays", 1))
                nc.scalar.activation(s.decay_at[:], s.log_decay[:], ACT.Exp, scale=-DECAY_SCALE).then_inc(sem["decays"], add("decays", 1))
                ends = s.log_decay[:].rearrange("p a (c i) -> p a c i", c=NCH)
                nc.scalar.activation(s.end_decay[:], ends[:, :, :, T // NCH - 1], ACT.Exp, scale=-DECAY_SCALE).then_inc(sem["decays"], add("decays", 1))
                nc.scalar.activation(s.grow[:], s.log_decay[:], ACT.Exp, scale=DECAY_SCALE).then_inc(sem["decays"], add("decays", 1))
                nc.scalar.activation(s.zD[:], s.shifted[:, 6:8, :], ACT.Silu).then_inc(sem["z_silu2"], add("z_silu2", 1))
                act.wait_ge(sem["mlstm_num"], past["mlstm_num"] + GH)
                for j in range(NT):
                    nc.scalar.activation(den[:, j, :], ps[:, 4 + j, 0:GH * W].rearrange("p (h d) -> p h d", h=GH)[:, :, HD], ACT.Abs).then_inc(sem["den_abs"], add("den_abs", 1))
                act.wait_ge(sem["mlstm_y"], past["mlstm_y"] + NT + 1)
                nc.scalar.activation(sq[:], y[:], ACT.Square).then_inc(sem["mlstm_sq"], add("mlstm_sq", 1))
                act.wait_ge(sem["mlstm_mean_sq"], past["mlstm_mean_sq"] + 1)
                nc.scalar.activation(ss[:], ss[:], ACT.Sqrt).then_inc(sem["mlstm_root"], add("mlstm_root", 1))

            @block.gpsimd
            def _(pool):
                for h in range(GH):
                    for i in range(NT):
                        m = NT * h + i
                        pool.wait_ge(sem["weight"], past["weight"] + m + 1)
                        w = weight[:, h % 2, i, i * P:(i + 1) * P]
                        nc.gpsimd.tensor_tensor(w, w, g.not_before[:], ALU.mult).then_inc(sem["weight_masked"], add("weight_masked", 1))
                r_, k_, step = s.shifted[:, 0:PAIRS, :], s.shifted[:, PAIRS:2 * PAIRS, :], "key_step"
                pool.wait_ge(sem["a_sigmoid"], past["a_sigmoid"] + PAIRS)
                for i in range(PAIRS):
                    nc.gpsimd.tensor_scalar(s.rk[:, i, :], s.a_gate[:, i, :], 1.0, g.col("k_a")[:, i:i + 1], ALU.subtract, ALU.mult).then_inc(sem[step], add(step, 1))
                pool.wait_ge(sem[step], count[step])
                nc.gpsimd.tensor_scalar(s.rk[:], s.rk[:], 1.0, None, ALU.add).then_inc(sem[step], add(step, 1))
                pool.wait_ge(sem[step], count[step])
                nc.gpsimd.tensor_tensor(k_, k_, s.rk[:], ALU.mult).then_inc(sem[step], add(step, 1))
                pool.wait_ge(sem[step], count[step])
                for i in range(PAIRS):
                    nc.gpsimd.tensor_scalar(s.rk[:, i, :], r_[:, i, :], g.col("r_k")[:, i:i + 1], None, ALU.mult).then_inc(sem[step], add(step, 1))
                pool.wait_ge(sem[step], count[step])
                nc.gpsimd.tensor_tensor(s.rk[:], s.rk[:], k_, ALU.mult).then_inc(sem["rk"], add("rk", 1))

            @block.vector
            def _(dve):
                for h in range(GH):
                    nc.vector.tensor_scalar(pick[:, h, :], g.ident[0:GH, h:h + 1].to_broadcast([GH, P]), -1.0, None, ALU.mult).then_inc(sem["pick"], add("pick", 1))
                dve.wait_ge(sem["a_turned"], past["a_turned"] + 1)
                nc.vector.tensor_copy(a_row[:], ps[0:GH, 0, :]).then_inc(sem["a_row"], add("a_row", 1))
                dve.wait_ge(sem["a_row"], past["a_row"] + 1)
                nc.vector.tensor_tensor_scan(mu_row[:], a_row[:], a_row[:], 0.0, ALU.max, ALU.max).then_inc(sem["mu_row"], add("mu_row", 1))
                dve.wait_ge(sem["mu_turned"], past["mu_turned"] + 1)
                nc.vector.tensor_copy(mu[:], ps[:, 1, 0:NT * GH].rearrange("p (j h) -> p j h", j=NT)).then_inc(sem["mu_copied"], add("mu_copied", 1))
                dve.wait_ge(sem["mu_copied"], past["mu_copied"] + 1)
                nc.vector.tensor_tensor(floor[:], mu[:], s.cum[:, :, GH:2 * GH], ALU.add).then_inc(sem["m_made"], add("m_made", 1))

                def logs(h):
                    dve.wait_ge(sem["mu_spread"], past["mu_spread"] + h + 1)
                    for i in range(NT):
                        if h >= 2:
                            dve.wait_ge(sem["weighted"], past["weighted"] + NT * (h - 2) + i + 1)
                        nc.vector.tensor_scalar(weight[:, h % 2, i, i * P:T], ps[:, 0, i * P:T], s.a_tok[:, i, h:h + 1], 0.0, ALU.add, ALU.min).then_inc(sem["weight_log"], add("weight_log", 1))

                def running_decay():
                    for i in range(PAIRS):
                        dve.wait_ge(sem["decay_sigmoid"], past["decay_sigmoid"] + i + 1)
                        nc.vector.tensor_tensor_scan(s.log_decay[:, i, :], g.keep_state[:], s.decay[:, i, :], 0.0, ALU.mult, ALU.add).then_inc(sem["log_decay"], add("log_decay", 1))

                def decay_before():
                    dve.wait_ge(sem["log_decay"], past["log_decay"] + PAIRS)
                    nc.vector.tensor_tensor(s.decay[:], s.log_decay[:], s.decay[:], ALU.subtract).then_inc(sem["before"], add("before", 1))
                    dve.wait_ge(sem["kk_root"], past["kk_root"] + PAIRS)
                    nc.vector.tensor_scalar(s.kk_norm[:], s.kk_norm[:], 1e-12, None, ALU.max).then_inc(sem["kk_floor"], add("kk_floor", 1))

                logs(0)
                for h in range(GH):
                    if h + 1 < GH:
                        logs(h + 1)
                    if h == 0:
                        running_decay()
                    elif h == 1:
                        decay_before()
                    for i in range(NT):
                        m = NT * h + i
                        dve.wait_ge(sem["mlstm_scores"], past["mlstm_scores"] + m + 1)
                        dve.wait_ge(sem["weight_masked"], past["weight_masked"] + m + 1)
                        if h >= 2:
                            dve.wait_ge(sem["mlstm_num"], past["mlstm_num"] + h - 1)
                        nc.vector.scalar_tensor_tensor(out=score[:, h % 2, i, i * P:T], in0=ps[:, 1 + m % 3, i * P:T], scalar=HEAD_SCALE,
                                                       in1=weight[:, h % 2, i, i * P:T], op0=ALU.mult, op1=ALU.mult).then_inc(sem["weighted"], add("weighted", 1))
                dve.wait_ge(sem["kk_floor"], past["kk_floor"] + 1)
                nc.vector.reciprocal(s.kk_norm[:], s.kk_norm[:]).then_inc(sem["kk_inverse"], add("kk_inverse", 1))
                dve.wait_ge(sem["kk_inverse"], past["kk_inverse"] + 1)
                nc.vector.tensor_tensor(s.kk[:], s.kk[:], s.kk_norm[:], ALU.mult).then_inc(sem["kk_unit"], add("kk_unit", 1))
                dve.wait_ge(sem["den_abs"], past["den_abs"] + NT)
                dve.wait_ge(sem["floor"], past["floor"] + 1)
                nc.vector.tensor_tensor(den[:], den[:], floor[:], ALU.max).then_inc(sem["den"], add("den", 1))
                dve.wait_ge(sem["den"], past["den"] + 1)
                nc.vector.reciprocal(den[:], den[:]).then_inc(sem["den"], add("den", 1))
                dve.wait_ge(sem["den"], past["den"] + 2)
                for j in range(NT):
                    num = ps[:, 4 + j, 0:GH * W].rearrange("p (h d) -> p h d", h=GH)[:, :, 0:HD]
                    nc.vector.tensor_tensor(y[:, j, :].rearrange("p (h d) -> p h d", h=GH), num, den[:, j, :].unsqueeze(2).to_broadcast([P, GH, HD]), ALU.mult).then_inc(sem["mlstm_y"], add("mlstm_y", 1))
                dve.wait_ge(sem["mlstm_y"], past["mlstm_y"] + NT)
                nc.vector.tensor_tensor(y[:], y[:], s.o_sig[:], ALU.mult).then_inc(sem["mlstm_y"], add("mlstm_y", 1))
                dve.wait_ge(sem["mlstm_sq"], past["mlstm_sq"] + 1)
                nc.vector.tensor_reduce(ss[:], sq[:].rearrange("p j (h d) -> p (j h) d", d=HD), AX, ALU.add).then_inc(sem["mlstm_sums"], add("mlstm_sums", 1))
                dve.wait_ge(sem["mlstm_sums"], past["mlstm_sums"] + 1)
                nc.vector.tensor_scalar(ss[:], ss[:], 1.0 / HD, RMS_EPS, ALU.mult, ALU.add).then_inc(sem["mlstm_mean_sq"], add("mlstm_mean_sq", 1))
                dve.wait_ge(sem["mlstm_root"], past["mlstm_root"] + 1)
                nc.vector.reciprocal(ss[:], ss[:]).then_inc(sem["mlstm_rstd"], add("mlstm_rstd", 1))
                dve.wait_ge(sem["mlstm_rstd"], past["mlstm_rstd"] + 1)
                v = y[:].rearrange("p j (h d) -> p (j h) d", d=HD)
                nc.vector.tensor_tensor(v, v, ss[:].unsqueeze(2).to_broadcast([P, NT * GH, HD]), ALU.mult).then_inc(sem["mlstm_scaled"], add("mlstm_scaled", 1))
                dve.wait_ge(sem["mlstm_scaled"], past["mlstm_scaled"] + 1)
                nc.vector.tensor_tensor(y[:], y[:], s.gains[:, 5, :].unsqueeze(1).to_broadcast([P, NT, GW]), ALU.mult).then_inc(sem["mlstm_gained"], add("mlstm_gained", 1))
                gate_turned(g, dve, s, 4, 4, [0, 1])

            @block.sync
            def _(sp):
                g.load_chunks(sp)
                sp.wait_ge(sem["rk"], past["rk"] + 1)
    g.sem.end_phase()


def phase_rwkv(g, s, w_out):
    nc, t, ps = g.nc, g.t, g.ps
    sem, past, count, add = g.sem, g.sem.past, g.sem.count, g.sem.add
    C = 64
    PAIRS = GH // 2
    LEVELS = 6
    with ExitStack() as stack:
        new = lambda name, shape: g.sb(stack, name, shape)
        shifted = s.shifted
        LT = new("LT", [P, NT, GH, P])
        RBT = new("RBT", [P, NT, GH, P])
        ar = new("ar", [P, PAIRS, NT, 2, P])
        bt = new("bt", [P, PAIRS, T])
        kt = new("kt", [P, PAIRS, T])
        end_decay = s.end_decay
        tok = new("rwkv_tok", [P, 4, NT, GW])
        bonus = new("bonus", [P, NT, GH])
        WT = new("WT", [P, PAIRS, T])
        U = new("U", [P, NT, GW])
        sa = new("sa", [P, NT, GW])
        state = new("rwkv_state", [P, NCH + 1, PAIRS, C])
        MTt = new("MTt", [P, NT, GH, P])
        rooms = [g.room[:, i, h * NT:(h + 1) * NT].rearrange("p j (h t) -> p j h t", t=P) for i in range(2) for h in range(2)]
        first_slot = g.chunks[w_out][3] % RING
        Ti, RKT = rooms[first_slot], rooms[1 - first_slot]
        Cm, TiT = rooms[2 + first_slot][:, 0:2], rooms[3 - first_slot]
        ss = new("rwkv_ss", [P, NT * GH])
        flat = lambda x, i: x[:].rearrange("p j h t -> p (j h t)")[:, i * PAIRS * T:(i + 1) * PAIRS * T].rearrange("p (a t) -> p a t", a=PAIRS)
        hats = flat(MTt, 0), flat(MTt, 1)
        X = shifted[:, 0:4, :].rearrange("p a (h t) -> p a h t", h=GH)
        y = U
        x_back = shifted[:].rearrange("p (j a) t -> p j (a t)", j=NT)
        HALF_TILES = MIX_TILES // 2
        OWN = (6, 7)
        early = (slice(0, 3), slice(3, 6), slice(8, 10))
        r_, k_, v_, z_ = (shifted[:, PAIRS * i:PAIRS * (i + 1), :] for i in range(4))
        ch = lambda x: x.rearrange("p a (c i) -> p a c i", i=C)
        order = (2, 3, 0, 1)
        with nc.Block("rwkv_prep", no_gpsimd_drain=True) as block:

            @block.vector
            def _(dve):
                tiles = lambda x: x.rearrange("p a (j t) -> p a j t", j=NT)
                for i in range(PAIRS):
                    nc.vector.tensor_tensor(ar[:, i, :, 0, :], tiles(s.kk[:])[:, i], tiles(s.decay[:])[:, i], ALU.mult).then_inc(sem["at"], add("at", 1))
                for i in range(PAIRS):
                    nc.vector.tensor_tensor(ar[:, i, :, 1, :], tiles(r_)[:, i], tiles(s.decay_at[:])[:, i], ALU.mult).then_inc(sem["rt"], add("rt", 1))
                dve.wait_ge(sem["at"], past["at"] + PAIRS)
                nc.vector.tensor_tensor(s.kk[:], s.kk[:], s.a_gate[:], ALU.mult).then_inc(sem["b_made"], add("b_made", 1))
                dve.wait_ge(sem["b_made"], past["b_made"] + 1)
                nc.vector.tensor_tensor(bt[:], s.kk[:], s.grow[:], ALU.mult).then_inc(sem["bt"], add("bt", 1))
                nc.vector.tensor_tensor(kt[:], k_, s.grow[:], ALU.mult).then_inc(sem["kt"], add("kt", 1))
                dve.wait_ge(sem["bt"], past["bt"] + 1)
                dve.wait_ge(sem["kt"], past["kt"] + 1)
                for x, h in ((bt, hats[0]), (kt, hats[1])):
                    for i in range(PAIRS):
                        nc.vector.tensor_tensor(ch(h)[:, i], ch(x[:])[:, i], end_decay[:, i, :].unsqueeze(2).to_broadcast([P, NCH, C]), ALU.mult).then_inc(sem["hats"], add("hats", 1))
                nc.vector.memset(state[:, 0], 0.0).then_inc(sem["state_zero"], add("state_zero", 1))
                dve.wait_ge(sem["bonus_ready"], past["bonus_ready"] + 1)
                nc.vector.tensor_copy(bonus[:], ps[:, 3, 0:NT * GH].rearrange("p (j h) -> p j h", j=NT)).then_inc(sem["bonus_copied"], add("bonus_copied", 1))

            @block.scalar
            def _(act):
                for n, which in enumerate(which for which in order for _ in range(NT // 2)):
                    act.wait_ge(sem["tok_turned"], past["tok_turned"] + n + 1)
                    j2 = n % 2
                    nc.scalar.activation(tok[:, which, 2 * j2:2 * j2 + 2, :], ps[:, 4 + n % 4, :].rearrange("p (j d) -> p j d", j=2), ACT.Copy).then_inc(sem["tok_copied"], add("tok_copied", 1))

            @block.tensor
            def _(pe):
                for j in range(NT):
                    for i in range(PAIRS):
                        ins = g.product(ps[:, 3, j * GH + 2 * i:j * GH + 2 * i + 2], s.rk[:, i, j * P:(j + 1) * P], g.same64[:, 0:P:HD])
                ins.then_inc(sem["bonus_ready"], add("bonus_ready", 1))
                for n, which in enumerate(which for which in order for _ in range(NT // 2)):
                    j2 = n % 2
                    if n >= 4:
                        pe.wait_ge(sem["tok_copied"], past["tok_copied"] + n - 3)
                    if which < 2:
                        pe.wait_ge(sem["hats"], past["hats"] + PAIRS * (which + 1))
                    elif which == 3:
                        pe.wait_ge(sem["at"], past["at"] + PAIRS)
                    for j in (2 * j2, 2 * j2 + 1):
                        for i in range(PAIRS):
                            src = (hats[0][:, i, j * P:(j + 1) * P], hats[1][:, i, j * P:(j + 1) * P], v_[:, i, j * P:(j + 1) * P], ar[:, i, j, 0, :])[which]
                            at = (j - 2 * j2) * GW + i * P
                            ins = nc.tensor.transpose(ps[:, 4 + n % 4, at:at + P], src, g.ident[:])
                    ins.then_inc(sem["tok_turned"], add("tok_turned", 1))

            @block.sync
            def _(sp):
                g.load_chunks(sp)
        g.sem.end_phase()

        y_in = lambda j: ps[:, 4 + 2 * (j // 2):6 + 2 * (j // 2), (j % 2) * P:(j % 2 + 1) * P].rearrange("p b (i d) -> p b i d", d=HD)
        by_parity = lambda x: x.rearrange("p (i b d) -> p b i d", b=2, d=HD)
        g.load_limit = len(g.chunks)
        doubled = NT * (LEVELS - 1)
        with nc.Block("rwkv", no_gpsimd_drain=True) as block:

            @block.tensor
            def _(pe):
                for j in range(NT):
                    tile = slice(j * P, (j + 1) * P)
                    for a, x in enumerate((bt, kt)):
                        for i in range(PAIRS):
                            n = 2 * PAIRS * j + PAIRS * a + i
                            if n >= 2:
                                pe.wait_ge(sem["pair_masked"], past["pair_masked"] + 2 * (n - 2) + 2)
                            for b in range(2):
                                rows = slice(b * HD, (b + 1) * HD)
                                ins = g.product(ps[:, 2 * (n % 2) + b, 0:2 * P], x[rows, i, tile], ar[rows, i, j].rearrange("p a t -> p (a t)"))
                            ins.then_inc(sem["pair_ready"], add("pair_ready", 1))
                    if j >= 2:
                        pe.wait_ge(sem["Ti_init"], past["Ti_init"] + j - 1)
                    for h in range(GH):
                        rows = slice((h % 2) * HD, (h % 2 + 1) * HD)
                        ins = g.product(ps[:, 4 + 2 * (j % 2) + h % 2, (h // 2) * P:(h // 2 + 1) * P], ar[rows, h // 2, j, 0, :], bt[rows, h // 2, tile])
                    ins.then_inc(sem["L_ready"], add("L_ready", 1))
                units = [(m, j) for m in range(1, LEVELS) for j in range(NT)]

                def first_product(n):
                    m, j = units[n]
                    pe.wait_ge(sem["Cm_made"], past["Cm_made"] + n + 1)
                    if m > 1:
                        pe.wait_ge(sem["TiT_new"], past["TiT_new"] + n - NT + 1)
                    else:
                        pe.wait_ge(sem["TiT_init"], past["TiT_init"] + j + 1)
                        pe.wait_ge(sem["Ti_init"], past["Ti_init"] + NT)
                        pe.wait_ge(sem["pair_masked"], past["pair_masked"] + 2 * 2 * PAIRS * NT)
                    if n >= 2:
                        pe.wait_ge(sem["X_copied"], past["X_copied"] + n - 1)
                    for h in range(GH):
                        ins = g.product(ps[:, n % 2, h * P:(h + 1) * P], Cm[:, n % 2, h, :], Ti[:, j, h, :])
                    ins.then_inc(sem["X_ready"], add("X_ready", 1))

                first_product(0)
                for n, (m, j) in enumerate(units):
                    if n + 1 < len(units):
                        first_product(n + 1)
                    pe.wait_ge(sem["X_copied"], past["X_copied"] + n + 1)
                    if n >= 2:
                        pe.wait_ge(sem["TiT_new"], past["TiT_new"] + n - 1)
                    if m < LEVELS - 1:
                        if n >= 2:
                            pe.wait_ge(sem["Ti_new"], past["Ti_new"] + n - 1)
                        for h in range(GH):
                            ins = g.product(ps[:, 2 + n % 2, h * P:(h + 1) * P], TiT[:, j, h, :], X[:, j, h, :])
                        ins.then_inc(sem["Y_ready"], add("Y_ready", 1))
                    for h in range(GH):
                        ins = g.product(ps[:, 4 + n % 2, h * P:(h + 1) * P], X[:, j, h, :], TiT[:, j, h, :])
                    ins.then_inc(sem["YT_ready"], add("YT_ready", 1))
                for j in range(NT):
                    pe.wait_ge(sem["TiT_new"], past["TiT_new"] + NT * (LEVELS - 2) + j + 1)
                    if j == 0:
                        pe.wait_ge(sem["X_copied"], past["X_copied"] + NT * (LEVELS - 1))
                        pe.wait_ge(sem["TiT_new"], past["TiT_new"] + NT * (LEVELS - 1))
                    for h in range(GH):
                        rows = slice((h % 2) * HD, (h % 2 + 1) * HD)
                        at = (h // 2) * T + j * P
                        ins = g.product(ps[rows, h // 2, j * P:(j + 1) * P], tok[:, 3, j, h * HD:(h + 1) * HD], TiT[:, j, h, :])
                    ins.then_inc(sem["WT_ready"], add("WT_ready", 1))
                    for h in range(GH):
                        ins = g.product(ps[:, 2 + j // 2, (j % 2) * GW + h * HD:(j % 2) * GW + (h + 1) * HD], MTt[:, j, h, :], tok[:, 2, j, h * HD:(h + 1) * HD])
                    ins.then_inc(sem["Mv_ready"], add("Mv_ready", 1))
                for j in range(NT):
                    pe.wait_ge(sem["Mv_copied"], past["Mv_copied"] + j + 1)
                    for h in range(GH):
                        ins = g.product(ps[:, 4 + j // 2, (j % 2) * GW + h * HD:(j % 2) * GW + (h + 1) * HD], TiT[:, j, h, :], sa[:, j, h * HD:(h + 1) * HD])
                    ins.then_inc(sem["U_ready"], add("U_ready", 1))
                pe.wait_ge(sem["WT_copied"], past["WT_copied"] + PAIRS)
                pe.wait_ge(sem["U_copied"], past["U_copied"] + NT)
                outputs = [(j, h) for j in range(NT) for h in range(GH)]

                def output(j, h):
                    cols = slice(h * HD, (h + 1) * HD)
                    rows = slice((h % 2) * HD, (h % 2 + 1) * HD)
                    bank = 4 + 2 * (j // 2) + h % 2
                    at = slice(((j % 2) * PAIRS + h // 2) * HD, ((j % 2) * PAIRS + h // 2 + 1) * HD)
                    g.product(ps[:, bank, at], RKT[:, j, h, :], tok[:, 2, j, cols], True, False, check=False)
                    g.product(ps[:, bank, at], RBT[:, j, h, :], sa[:, j, cols], False, False, check=False)
                    for half in range(2):
                        out = slice(half * C, (half + 1) * C)
                        ins = g.product(ps[out, bank, at], ar[rows, h // 2, j, 1, out], state[rows, 2 * j + half, h // 2, :], False, half == 1, check=False)
                    if h == GH - 1:
                        ins.then_inc(sem["y_ready"], add("y_ready", 1))

                for c in range(NCH):
                    j, b = c // 2, c % 2
                    toks = slice(b * C, (b + 1) * C)
                    if c:
                        pe.wait_ge(sem["state_new"], past["state_new"] + PAIRS * c)
                    for h in range(GH):
                        rows = slice((h % 2) * HD, (h % 2 + 1) * HD)
                        ins = g.product(ps[toks, h % 2, (h // 2) * HD:(h // 2 + 1) * HD], WT[rows, h // 2, c * C:(c + 1) * C], state[rows, c, h // 2, :])
                    ins.then_inc(sem["WS_ready"], add("WS_ready", 1))
                    place = [(slice(h * HD, (h + 1) * HD), ps[(h % 2) * HD:(h % 2 + 1) * HD, 2 + h // 2, 0:C]) for h in range(GH)]
                    for cols, out in place:
                        g.product(out, tok[toks, 1, j, cols], tok[toks, 2, j, cols], True, False, check=False)
                    for n in range(2 * (c - 2), 2 * (c - 1)):
                        if n >= 0:
                            output(*outputs[n])
                    pe.wait_ge(sem["sa_ready"], past["sa_ready"] + 2 * c + 2)
                    for cols, out in place:
                        ins = g.product(out, tok[toks, 0, j, cols], sa[toks, j, cols], False, True, check=False)
                    ins.then_inc(sem["S_ready"], add("S_ready", 1))
                for n in range(2 * (NCH - 2), len(outputs)):
                    output(*outputs[n])
                def project(n, c, tiles, done):
                    w = g.chunk(pe, w_out + 2 * n + c)
                    for j in range(NT):
                        for k in tiles:
                            ins = g.split_product(ps[:, n * CHUNK // COLS * NT + j, n % 2 * CHUNK:(n % 2 + 1) * CHUNK],
                                                  columns(s.mix_parts, k, slice(j * P, (j + 1) * P)), columns(w, k - c * HALF_TILES), k == 0, done and k == tiles[-1] and c == 1)
                        if done:
                            ins.then_inc(sem["out_part"], add("out_part", 1))
                    if done:
                        g.release("out_part")

                halves = [[k for k in range(MIX_TILES) if k // HALF_TILES == c] for c in range(2)]
                pe.wait_ge(sem["state_new"], past["state_new"] + PAIRS * NCH)
                pe.wait_ge(sem["mix_low"], past["mix_low"] + 2)
                project(0, 0, halves[0], True)
                pe.wait_ge(sem["mix_low"], past["mix_low"] + len(early))
                project(0, 1, [k for k in halves[1] if k not in OWN], False)
                pe.wait_ge(sem["y_final"], past["y_final"] + NT)
                to_gated(g, pe, y, [4, 5])
                pe.wait_ge(sem["own_low"], past["own_low"] + len(OWN))
                project(0, 1, OWN, True)
                for n in range(1, D // CHUNK):
                    for c in range(2):
                        project(n, c, halves[c], True)

            @block.scalar
            def _(act):
                for m in range(1, LEVELS):
                    for j in range(NT):
                        n = NT * (m - 1) + j
                        act.wait_ge(sem["X_ready"], past["X_ready"] + n + 1)
                        if m > 1:
                            act.wait_ge(sem["YT_ready"], past["YT_ready"] + n - NT + 1)
                        nc.scalar.activation(X[:, j], ps[:, n % 2, :].rearrange("p (h t) -> p h t", h=GH), ACT.Copy).then_inc(sem["X_copied"], add("X_copied", 1))
                act.wait_ge(sem["WT_ready"], past["WT_ready"] + NT)
                for i in range(PAIRS):
                    nc.scalar.activation(WT[:, i, :], ps[:, i, :], ACT.Copy).then_inc(sem["WT_copied"], add("WT_copied", 1))
                for j in range(NT):
                    act.wait_ge(sem["Mv_ready"], past["Mv_ready"] + j - j % 2 + 2)
                    nc.scalar.activation(sa[:, j, :], ps[:, 2 + j // 2, (j % 2) * GW:(j % 2 + 1) * GW], ACT.Copy).then_inc(sem["Mv_copied"], add("Mv_copied", 1))
                for j in range(NT):
                    act.wait_ge(sem["U_ready"], past["U_ready"] + j - j % 2 + 2)
                    nc.scalar.activation(U[:, j, :], ps[:, 4 + j // 2, (j % 2) * GW:(j % 2 + 1) * GW], ACT.Copy).then_inc(sem["U_copied"], add("U_copied", 1))
                g.split_high(act, w_out + 1)
                for tiles in early:
                    nc.scalar.activation(s.mix_parts[0][:, tiles, :], s.mixT[:, tiles, :], ACT.Copy).then_inc(sem["mix_high"], add("mix_high", 1))
                for j in range(NT):
                    act.wait_ge(sem["y_ready"], past["y_ready"] + j - j % 2 + 2)
                    sq = RBT[:, j, 0:2, :].rearrange("p h t -> p (h t)").rearrange("p (i b d) -> p b i d", b=2, d=HD)
                    nc.scalar.activation(sq, y_in(j), ACT.Square).then_inc(sem["y_sq"], add("y_sq", 1))
                act.wait_ge(sem["y_mean_sq"], past["y_mean_sq"] + 1)
                nc.scalar.activation(ss[:], ss[:], ACT.Sqrt).then_inc(sem["y_root"], add("y_root", 1))
                g.split_high(act, w_out + 2)
                for i, k in enumerate(OWN):
                    act.wait_ge(sem["y_gated"], past["y_gated"] + i + 1)
                    nc.scalar.activation(s.mix_parts[0][:, k, :], s.mixT[:, k, :], ACT.Copy).then_inc(sem["own_high"], add("own_high", 1))
                g.split_high(act, len(g.chunks))

            @block.gpsimd
            def _(pool):
                pool.wait_ge(sem["X_ready"], past["X_ready"] + doubled)
                g.split_low(pool, w_out + 1)
                for i, tiles in enumerate(early):
                    pool.wait_ge(sem["mix_high"], past["mix_high"] + i + 1)
                    nc.gpsimd.tensor_tensor(s.mix_parts[1][:, tiles, :], s.mixT[:, tiles, :], s.mix_parts[0][:, tiles, :].bitcast(F32), ALU.subtract).then_inc(sem["mix_low"], add("mix_low", 1))
                pool.wait_ge(sem["U_ready"], past["U_ready"] + NT)
                g.split_low(pool)

            @block.vector
            def _(dve):
                for j in range(NT):
                    for a, dsts in enumerate(((LT, RBT), (MTt, RKT))):
                        for i in range(PAIRS):
                            n = 2 * PAIRS * j + PAIRS * a + i
                            dve.wait_ge(sem["pair_ready"], past["pair_ready"] + n + 1)
                            both = ps[:, 2 * (n % 2):2 * (n % 2) + 2, 0:2 * P].rearrange("p b (w t) -> p b w t", w=2)
                            for w, (dst, mask) in enumerate(zip(dsts, (g.after64, g.not_before64))):
                                nc.vector.tensor_tensor(dst[:, j, 2 * i:2 * i + 2, :], both[:, :, w, :],
                                                                              mask[:].unsqueeze(1).to_broadcast([P, 2, P]), ALU.mult).then_inc(sem["pair_masked"], add("pair_masked", 1))
                    dve.wait_ge(sem["L_ready"], past["L_ready"] + j + 1)
                    wide = lambda x: x[:].unsqueeze(1).to_broadcast([P, GH, P])
                    step = "Ti_step"
                    for b in range(2):
                        nc.vector.tensor_tensor(Ti[:, j, b:GH:2, :], ps[:, 4 + 2 * (j % 2) + b, 0:PAIRS * P].rearrange("p (h t) -> p h t", h=PAIRS),
                                                        g.level1[:].unsqueeze(1).to_broadcast([P, PAIRS, P]), ALU.mult).then_inc(sem[step], add(step, 1))
                    dve.wait_ge(sem["pair_masked"], past["pair_masked"] + 2 * (2 * PAIRS * (j + 1)))
                    nc.vector.tensor_tensor(TiT[:, j], LT[:, j], wide(g.levelT[0]), ALU.mult).then_inc(sem[step], add(step, 1))
                    dve.wait_ge(sem[step], past[step] + 3 * j + 3)
                    nc.vector.tensor_tensor(Ti[:, j], wide(g.ident), Ti[:, j], ALU.subtract).then_inc(sem["Ti_init"], add("Ti_init", 1))
                    nc.vector.tensor_tensor(TiT[:, j], wide(g.ident), TiT[:, j], ALU.subtract).then_inc(sem["TiT_init"], add("TiT_init", 1))

                def mask(n):
                    m, j = n // NT + 1, n % NT
                    if n >= 2:
                        dve.wait_ge(sem["X_ready"], past["X_ready"] + n - 1)
                    nc.vector.tensor_tensor(Cm[:, n % 2], LT[:, j], g.levelT[m][:].unsqueeze(1).to_broadcast([P, GH, P]), ALU.mult).then_inc(sem["Cm_made"], add("Cm_made", 1))

                total = NT * (LEVELS - 1)
                mask(0)
                mask(1)
                for n in range(total):
                    m, j = n // NT + 1, n % NT
                    if n + 2 < total:
                        mask(n + 2)
                    if m < LEVELS - 1:
                        dve.wait_ge(sem["Y_ready"], past["Y_ready"] + n + 1)
                        if n >= NT:
                            dve.wait_ge(sem["Ti_new"], past["Ti_new"] + n - NT + 1)
                        else:
                            dve.wait_ge(sem["Ti_init"], past["Ti_init"] + NT)
                        nc.vector.tensor_tensor(Ti[:, j], Ti[:, j], ps[:, 2 + n % 2, :].rearrange("p (h t) -> p h t", h=GH), ALU.subtract).then_inc(sem["Ti_new"], add("Ti_new", 1))
                    dve.wait_ge(sem["YT_ready"], past["YT_ready"] + n + 1)
                    if n >= NT:
                        dve.wait_ge(sem["TiT_new"], past["TiT_new"] + n - NT + 1)
                    else:
                        dve.wait_ge(sem["TiT_init"], past["TiT_init"] + NT)
                    nc.vector.tensor_tensor(TiT[:, j], TiT[:, j], ps[:, 4 + n % 2, :].rearrange("p (h t) -> p h t", h=GH), ALU.subtract).then_inc(sem["TiT_new"], add("TiT_new", 1))
                for c in range(NCH):
                    j, b = c // 2, c % 2
                    toks = slice(b * C, (b + 1) * C)
                    dve.wait_ge(sem["WS_ready"], past["WS_ready"] + c + 1)
                    dve.wait_ge(sem["U_copied"], past["U_copied"] + NT)
                    for odd in range(2):
                        nc.vector.scalar_tensor_tensor(out=by_parity(sa[toks, j, :])[:, odd], scalar=-1.0, in1=by_parity(U[toks, j, :])[:, odd],
                                                                          in0=ps[toks, odd, 0:PAIRS * HD].rearrange("p (i d) -> p i d", d=HD),
                                                                          op0=ALU.mult, op1=ALU.subtract).then_inc(sem["sa_ready"], add("sa_ready", 1))
                    dve.wait_ge(sem["S_ready"], past["S_ready"] + c + 1)
                    if c:
                        dve.wait_ge(sem["state_new"], past["state_new"] + PAIRS * c)
                    for i in range(PAIRS):
                        nc.vector.scalar_tensor_tensor(out=state[:, c + 1, i, :], in0=state[:, c, i, :], scalar=end_decay[:, i, c:c + 1],
                                                                           in1=ps[:, 2 + i, 0:C], op0=ALU.mult, op1=ALU.add).then_inc(sem["state_new"], add("state_new", 1))
                for j in range(NT):
                    dve.wait_ge(sem["y_sq"], past["y_sq"] + j + 1)
                    sq = RBT[:, j, 0:2, :].rearrange("p h t -> p (h t)")
                    nc.vector.tensor_reduce(ss[:, j * GH:(j + 1) * GH], sq.rearrange("p (h d) -> p h d", d=HD), AX, ALU.add).then_inc(sem["y_sums"], add("y_sums", 1))
                dve.wait_ge(sem["y_sums"], past["y_sums"] + NT)
                nc.vector.tensor_scalar(ss[:], ss[:], 1.0 / HD, RMS_EPS, ALU.mult, ALU.add).then_inc(sem["y_mean_sq"], add("y_mean_sq", 1))
                dve.wait_ge(sem["y_root"], past["y_root"] + 1)
                nc.vector.reciprocal(ss[:], ss[:]).then_inc(sem["y_rstd"], add("y_rstd", 1))
                dve.wait_ge(sem["y_rstd"], past["y_rstd"] + 1)
                heads = lambda x: x.rearrange("p (h d) -> p h d", d=HD)
                for j in range(NT):
                    nc.vector.tensor_tensor(by_parity(y[:, j, :]), y_in(j),
                                                              ss[:, j * GH:(j + 1) * GH].rearrange("p (i b) -> p b i", b=2).unsqueeze(3).to_broadcast([P, 2, PAIRS, HD]), ALU.mult).then_inc(sem["y_steps"], add("y_steps", 1))
                    nc.vector.tensor_tensor(heads(sa[:, j, :]), heads(tok[:, 2, j, :]), bonus[:, j, :].unsqueeze(2).to_broadcast([P, GH, HD]), ALU.mult).then_inc(sem["y_steps"], add("y_steps", 1))
                for j in range(NT):
                    dve.wait_ge(sem["y_steps"], past["y_steps"] + 2 * j + 2)
                    nc.vector.tensor_tensor(y[:, j, :], y[:, j, :], s.gains[:, 6, :], ALU.mult).then_inc(sem["y_gain"], add("y_gain", 1))
                for j in range(NT):
                    dve.wait_ge(sem["y_gain"], past["y_gain"] + j + 1)
                    nc.vector.tensor_tensor(y[:, j, :], y[:, j, :], sa[:, j, :], ALU.add).then_inc(sem["y_final"], add("y_final", 1))
                for i, k in enumerate(OWN):
                    dve.wait_ge(sem["y_turned"], past["y_turned"] + i + 1)
                    nc.vector.tensor_tensor(s.mixT[:, k, :], ps[:, 4 + i, :], s.zD[:, i, :], ALU.mult).then_inc(sem["y_gated"], add("y_gated", 1))
                for i, k in enumerate(OWN):
                    dve.wait_ge(sem["own_high"], past["own_high"] + i + 1)
                    nc.vector.tensor_tensor(s.mix_parts[1][:, k, :], s.mixT[:, k, :], s.mix_parts[0][:, k, :].bitcast(F32), ALU.subtract).then_inc(sem["own_low"], add("own_low", 1))
                dve.wait_ge(sem["x_back"], past["x_back"] + 16)
                for n in range(D // COLS):
                    for j in range(NT):
                        cols = slice(n * COLS, (n + 1) * COLS)
                        dve.wait_ge(sem["out_part"], past["out_part"] + 2 * NT * (COLS // CHUNK * (n + 1) - 1) + NT + j + 1)
                        nc.vector.tensor_tensor(x_back[:, j, cols], x_back[:, j, cols], ps[:, n * NT + j, :], ALU.add).then_inc(sem["out_added"], add("out_added", 1))

            @block.sync
            def _(sp):
                sp.wait_ge(sem["YT_ready"], past["YT_ready"] + doubled)
                sp.dma_start(x_back, g.x_dram).then_inc(sem["x_back"], add("x_back", 16))
                g.load_chunks(sp)
                out_tiles = g.out[0].rearrange("(j p) d -> p j d", p=P)
                for n in range(D // COLS):
                    for j in range(NT):
                        sp.wait_ge(sem["out_added"], past["out_added"] + n * NT + j + 1)
                        sp.dma_start(out_tiles[:, j, n * COLS:(n + 1) * COLS], x_back[:, j, n * COLS:(n + 1) * COLS]).then_inc(sem["out_landed"], add("out_landed", 16))
                sp.wait_ge(sem["out_landed"], past["out_landed"] + 16 * NT * (D // COLS))
        g.sem.end_phase()


def second_block(g, first):
    class Store:
        pass

    s = Store()
    with ExitStack() as kept:
        new = lambda name, shape: g.sb(kept, name, shape)
        mix_at = g.address()
        s.mixT = new("mixT", [P, MIX_TILES, T])
        s.zD = new("zD", [P, 2, T])
        s.gains = new("gains", [P, 7, GW])
        s.end_decay = new("end_decay", [P, GH // 2, NCH])
        s.w2_decay, s.w2_a = new("w2_decay", [RANK2, GW]), new("w2_a", [RANK2, GW])
        with ExitStack() as raw:
            raw_at = g.address()
            s.raw = g.sb(raw, "raw", [P, 8, T + 1])
            s.low = g.sb(raw, "low", [RANK2, 2, T + 1])
            with ExitStack() as mid:
                new = lambda name, shape: g.sb(mid, name, shape)
                heads_at = g.address()
                s.heads = new("heads", [P, NT, 5, GW])
                s.zT = new("zT", [P, 8, T])
                vB_at = g.address()
                s.vB = new("vB", [P, NT, GW])
                s.gates, s.gate_bias = new("gates", [P, NT, GATES]), new("gate_bias", [P, GATES])
                s.conv_in = new("conv_in", [P, 4, CONV_K - 1 + T])
                s.vC = new("vC", [P, NT, GH, HD + 1])
                s.o_sig = new("o_sig", [P, NT, GW])
                s.mem_kv = new("mem_kv", [P, MT, 2 * GW])
                s.w_sgu = new("w_sgu", [P, GH, P])
                s.head_ss = new("head_ss", [P, NT * 4 * GH])
                phase_project(g, s, first)
                g.x_stack.close()
                s.shifted = g.sb(kept, "shifted", [P, 8, T], side="right")
                s.w_sguT = g.room[:, 0, 2, :].rearrange("p (h t) -> p h t", h=GH)
                s.cum = new("cum", [P, NT, 2 * GH])
                s.a_tok = new("a_tok", [P, NT, GH])
                s.qkT = new("qkT", [P, 4, T])
                s.fox_qk = new("fox_qk", [P, NT, 2, GH, HD + 2])
                phase_heads(g, s)
                phase_fox(g, s)
                size = 4 * GH // 2 * T
                s.low_shifted = g.alias("low_shifted", [RANK2, 2, T], F32, vB_at)
                s.kk, s.kk_norm, s.decay, s.a_gate = (g.alias(n, [P, GH // 2, T], F32, raw_at + size * i) for i, n in enumerate(("kk", "kk_norm", "decay", "a_gate")))
                s.decay_at, s.grow, s.log_decay, s.rk = (g.alias(n, [P, GH // 2, T], F32, heads_at + size * i) for i, n in enumerate(("decay_at", "grow", "log_decay", "rk")))
                phase_mem(g, s)
                phase_mlstm(g, s)
            s.mix_parts = [g.alias(f"mix_{part}", [P, MIX_TILES, T], F32R, at) for part, at in (("high", raw_at), ("low", mix_at))]
            g.load_limit += RING
            phase_rwkv(g, s, first + len(SECOND_CHUNKS) + 2 * GW // CHUNK)


def build(nc, t, out, upto=99, dump=None):
    g = Program(nc, t, out)
    with g.ctx:
        sb = lambda name, shape: g.sb(g.ctx, name, shape)
        sb_typed = lambda name, shape, dtype: g.sb(g.ctx, name, shape, dtype)
        g.make_ring(sb_typed)
        g.room = g.alias("branch_room", [P, 3, KD, COLS], F32, g.ring_at)
        names = ("ident", "ones", "not_before", "after", "same64", "not_before64", "after64")
        g.ident, g.ones, g.not_before, g.after, g.same64, g.not_before64, g.after64 = (sb(name, [P, P]) for name in names)
        g.keep_state = sb("keep_state", [P, T])
        g.cols = sb("cols", [P, P])
        g.level1 = sb("level1", [P, P])
        g.levelT = [sb(f"levelT{i}", [P, P]) for i in range(6)]
        g.x_stack = g.ctx.enter_context(ExitStack())
        g.xT = [g.sb(g.x_stack, f"xT_{part}", [P, KD, T], F32R, side="right") for part in ("high", "low")]
        rope_stack = g.ctx.enter_context(ExitStack())
        g.idx_cos, g.idx_sin = (g.sb(rope_stack, n, [P, T]) for n in ("idx_cos", "idx_sin"))
        g.head_cos, g.head_sin = (g.sb(rope_stack, n, [2 * HALF, T]) for n in ("head_cos", "head_sin"))
        g.x_dram = nc.dram_tensor("x_scratch", [P, NT, D], F32, kind="Internal").ap()
        g.ps = g.ctx.enter_context(nc.psum_tensor("ps", [P, 8, COLS], F32))
        g.vec_rows, at = [], {}
        row = 0

        def vec(name, view, width=P):
            nonlocal row
            rows = view.shape[0]
            g.vec_rows.append((name, view, row, rows, width))
            at[name] = (row, rows)
            row += rows

        def rows_of(v):
            return v.rearrange("a (f p) -> (a f) p", p=P)

        vec("gla_gn_g", rows_of(t["gla_gn_g"]))
        vec("norm_g_2", rows_of(t["norm_g_2"]))
        vec("mem_norm_g_2", rows_of(t["mem_norm_g_2"]))
        vec("conv_w", t["mlstm_conv_w_2"][0].rearrange("a (f p) -> (a f) p", p=P))
        vec("conv_b", rows_of(t["mlstm_conv_b_2"]))
        mu = t["rwkv_mu_2"]
        for name, a, n in (("mu", 0, 1), ("mu_k", GW + RANK2, 2), ("mu_z", 3 * GW + 2 * RANK2, 1)):
            vec(name, rows_of(mu[:, a:a + n * GW]))
        at["mu"] = (at["mu"][0], 4 * GW // P)
        vec("mu_wlo", mu[:, GW:GW + RANK2], RANK2)
        vec("mu_alo", mu[:, 3 * GW + RANK2:3 * GW + 2 * RANK2], RANK2)
        for name in ("w0", "a0", "k_k", "k_a"):
            vec(name, rows_of(t[f"rwkv_{name}_2"]))
        vec("r_k", t["rwkv_r_k_2"].rearrange("a (i h) d -> (a i) (h d)", h=2))
        vec("sgu_b", t["sgu_b_2"][0])
        g.col = lambda name: g.cols[:, at[name][0]:at[name][0] + at[name][1]]

        w = t["gla_w_in"][0]
        qk = GLA_HEADS * GLA_DK
        gla_first = g.add_chunks(w, 2 * qk, 2 * qk + DI)
        g.add_chunks(w, 0, 2 * qk)
        g.add_chunks(w, 2 * qk + DI, 2 * qk + 2 * DI)
        post_first = [g.add_chunks(t["gla_w_out"][0], 0, D)]
        g.add_chunks(t["ple_gate_w"][0], 0, D)
        w = t["dsa_w_in"][0]
        dq, dkv = DSA_HEADS * DH, 2 * DH
        qi = 2 * dq + dkv
        ki = qi + IDX_HEADS * IDX_DIM
        dsa_first = g.add_chunks(w, dq, dq + dkv)
        g.add_chunks(w, qi, ki)
        g.add_chunk(w, [(ki, ki + IDX_DIM), (ki, ki + IDX_DIM), (ki + IDX_DIM, w.shape[1])])
        g.add_chunks(w, 0, dq)
        g.add_chunks(w, dq + dkv, 2 * dq + dkv)
        post_first.append(g.add_chunks(t["dsa_w_out"][0], 0, D))
        g.add_chunks(t["ple_gate_w"][1], 0, D)
        second_first = len(g.chunks)
        for name in SECOND_CHUNKS:
            g.add_chunk(t["w_in_2"][0], SECOND_CHUNKS[name])
        g.add_chunks(t["mem_w_kv_2"][0], 0, 2 * GW, split=False)
        g.load_limit = len(g.chunks)
        g.add_chunks(t["w_out_2"][0], 0, D, most=MIX_TILES // 2 * P)
        phase_load(g)
        with ExitStack() as stack:
            mix_at = g.address()
            mix_a, mix_b = (g.sb(stack, f"mix_{n}", [P, KI, T]) for n in "ab")
            gT = [g.alias(f"gT_{part}", [P, KI, T], F32R, mix_at + 4 * KI * T * i) for i, part in enumerate(("high", "low"))]
            if upto >= 1:
                phase_gla(g, mix_a, mix_b, gT, gla_first)
            if upto >= 2:
                phase_post(g, 0, gT, post_first[0], False, mix_at)
            if upto >= 3:
                phase_dsa(g, mix_a, mix_b, gT, dsa_first)
            if upto >= 4:
                phase_post(g, 1, gT, post_first[1], True, mix_at)
        rope_stack.close()
        if upto >= 5:
            second_block(g, second_first)
        if dump:
            dump(g)


_INS = ["x", "p", "positions", "gla_w_in", "gla_w_a2", "gla_b_a", "gla_gn_g", "gla_w_out", "dsa_w_in", "dsa_w_out", "ln_g", "ln_b", "ple_w",
        "ple_gate_w", "mem_2", "norm_g_2", "w_in_2", "w_out_2", "sgu_norm_g_2", "sgu_w_2", "sgu_b_2", "fox_q_g_2", "fox_k_g_2", "fox_f_b_2",
        "mlstm_conv_w_2", "mlstm_conv_b_2", "mlstm_i_b_2", "mlstm_f_b_2", "mlstm_out_g_2", "rwkv_mu_2", "rwkv_w0_2", "rwkv_w2_2", "rwkv_a0_2",
        "rwkv_a2_2", "rwkv_k_k_2", "rwkv_k_a_2", "rwkv_r_k_2", "rwkv_ln_g_2", "mem_norm_g_2", "mem_w_kv_2", "mem_q_g_2", "mem_k_g_2"]


def kernel(**inputs):
    import numpy as _np
    import concourse.bacc as _bacc
    from concourse import mybir as _mybir
    from concourse.bass_utils import run_bass_kernel_spmd as _run

    nc = _bacc.Bacc("TRN2", target_bir_lowering=False, num_devices=1)
    arrays, tensors = {}, {}
    for name in _INS:
        a = _np.ascontiguousarray(inputs[name])
        arrays[f"in_{name}_dram"] = a
        tensors[name] = nc.dram_tensor(f"in_{name}_dram", a.shape, _mybir.dt.from_np(a.dtype), kind="ExternalInput").ap()
    out = nc.dram_tensor("out_0_dram", (1, T, D), _mybir.dt.float32, kind="ExternalOutput").ap()
    build(nc, tensors, out)
    r = _run(nc, [arrays], core_ids=[0])
    return r.results[0]["out_0_dram"]
```
